# Optimizing a Trainium2 kernel written in Bass

```python
import jax, jax.numpy as jnp
from jax import lax
import numpy as np

D_MODEL = 1024
BATCH = 1
SEQ = 4096
DEPTH = 1

GRID_W = 64
CTX_LEN = 256
D_MIX = D_MODEL
D_A = D_MIX // 2
D_B = D_MIX - D_A
CHUNK = 128
SGU_GROUPS = 4
SGU_CH = D_A // SGU_GROUPS
NA_HEAD_DIM = 64
NA_HEADS = D_B // NA_HEAD_DIM
WIN_R = 8
WIN_C = 16
D_IN = 3 * D_A + 4 * D_B
BRANCH_WIDTHS = (D_A, D_A, D_A, D_B, D_B, D_B, D_B)
SPLIT_POINTS = tuple(int(s) for s in np.cumsum(BRANCH_WIDTHS)[:-1])
KV_START = 3 * D_A + D_B
KV_END = 3 * D_A + 3 * D_B
EPS = 1e-6
NEG_INF = -1e30

kernel_name = "hybrid_sgu_natten_prefix_block"

def rms_norm(x, g):
    xf = x.astype(jnp.float32)
    y = xf * lax.rsqrt(jnp.mean(xf * xf, axis=-1, keepdims=True) + EPS)
    return (y * g.astype(jnp.float32)).astype(x.dtype)

def ada_params(cond, w_ada, b_ada):
    mod = jax.nn.silu(cond) @ w_ada + b_ada
    shift, scale, gate = jnp.split(mod, 3, axis=-1)
    return shift[..., None, :], scale[..., None, :], gate[..., None, :]

def chunk_sgu(u, v, g, sgu_g, w_s, b_s):
    B, L, _ = u.shape
    u = jax.nn.gelu(u, approximate=False)
    v = jax.nn.gelu(v, approximate=False).reshape(B, L // CHUNK, CHUNK, SGU_GROUPS, SGU_CH)
    v = rms_norm(v, sgu_g.reshape(SGU_GROUPS, SGU_CH))
    mixed = jnp.einsum('gpq,bnqgc->bnpgc', w_s, v) + b_s.T[:, :, None]
    return u * mixed.reshape(B, L, D_A) * jax.nn.silu(g)

def neighborhood_attention(q, k, v, k_ctx, v_ctx, rpb):
    B, L, H, Dh = q.shape
    rows = L // GRID_W
    wr = min(WIN_R, rows)
    scale = Dh ** -0.5
    qg = q.reshape(B, rows, GRID_W, H, Dh)
    kg = k.reshape(B, rows, GRID_W, H, Dh)
    vg = v.reshape(B, rows, GRID_W, H, Dh)
    r = jnp.arange(rows)
    r0 = jnp.clip(r - WIN_R // 2, 0, rows - wr)
    key_rows = r0[:, None] + jnp.arange(wr)[None, :]
    kw = jnp.take(kg, key_rows, axis=1)
    vw = jnp.take(vg, key_rows, axis=1)
    dr = key_rows - r[:, None] + (WIN_R - 1)
    cols = jnp.arange(GRID_W)
    c0 = jnp.clip(cols - WIN_C // 2, 0, GRID_W - WIN_C)
    in_win = (cols[None, :] >= c0[:, None]) & (cols[None, :] < c0[:, None] + WIN_C)
    dc = jnp.clip(cols[None, :] - cols[:, None] + (WIN_C - 1), 0, 2 * WIN_C - 2)
    bias = rpb.astype(jnp.float32)[:, dr[:, None, :, None], dc[None, :, None, :]]
    bias = bias.transpose(1, 0, 2, 3, 4)
    s_lat = jnp.einsum('brqhd,brjkhd->brhqjk', qg, kw).astype(jnp.float32) * scale + bias[None]
    s_lat = jnp.where(in_win[:, None, :], s_lat, NEG_INF)
    s_ctx = jnp.einsum('brqhd,bchd->brhqc', qg, k_ctx).astype(jnp.float32) * scale
    m = jnp.maximum(jnp.max(s_lat, axis=(-2, -1)), jnp.max(s_ctx, axis=-1))
    p_lat = jnp.exp(s_lat - m[..., None, None])
    p_ctx = jnp.exp(s_ctx - m[..., None])
    denom = jnp.sum(p_lat, axis=(-2, -1)) + jnp.sum(p_ctx, axis=-1)
    out = (jnp.einsum('brhqjk,brjkhd->brqhd', p_lat.astype(v.dtype), vw)
           + jnp.einsum('brhqc,bchd->brqhd', p_ctx.astype(v.dtype), v_ctx))
    out = out / denom.transpose(0, 1, 3, 2)[..., None].astype(out.dtype)
    return out.reshape(B, L, H, Dh)

def context_attention(q, k, v):
    s = jnp.einsum('bqhd,bkhd->bhqk', q, k).astype(jnp.float32) * (q.shape[-1] ** -0.5)
    p = jax.nn.softmax(s, axis=-1).astype(v.dtype)
    return jnp.einsum('bhqk,bkhd->bqhd', p, v)

def setup_inputs(seed: int = 0) -> dict:
    key = jax.random.key(seed)
    ks = jax.random.split(key, 16)
    f32 = jnp.float32
    nrm = lambda k, shape: jax.random.normal(k, shape, dtype=f32)
    return {
        "x": nrm(ks[0], (BATCH, SEQ, D_MODEL)),
        "c": nrm(ks[1], (BATCH, D_MODEL)),
        "ctx": nrm(ks[2], (BATCH, CTX_LEN, D_MODEL)),
        "c_ctx": nrm(ks[3], (D_MODEL,)),
        "w_ada": nrm(ks[4], (DEPTH, D_MODEL, 3 * D_MODEL)) * (0.5 * D_MODEL ** -0.5),
        "b_ada": nrm(ks[5], (DEPTH, 3 * D_MODEL)) * 0.02,
        "norm_g": 1.0 + 0.02 * nrm(ks[6], (DEPTH, D_MODEL)),
        "w_in": nrm(ks[7], (DEPTH, D_MODEL, D_IN)) * D_MODEL ** -0.5,
        "sgu_norm_g": 1.0 + 0.02 * nrm(ks[8], (DEPTH, D_A)),
        "w_spatial": nrm(ks[9], (DEPTH, SGU_GROUPS, CHUNK, CHUNK)) * CHUNK ** -0.5,
        "b_spatial": nrm(ks[10], (DEPTH, SGU_GROUPS, CHUNK)) * 0.02,
        "q_norm_g": 1.0 + 0.02 * nrm(ks[11], (DEPTH, NA_HEAD_DIM)),
        "k_norm_g": 1.0 + 0.02 * nrm(ks[12], (DEPTH, NA_HEAD_DIM)),
        "rpb": nrm(ks[13], (DEPTH, NA_HEADS, 2 * WIN_R - 1, 2 * WIN_C - 1)) * 0.02,
        "w_out": nrm(ks[14], (DEPTH, D_MIX, D_MODEL)) * D_MIX ** -0.5,
    }

def reference(x, c, ctx, c_ctx, w_ada, b_ada, norm_g, w_in, sgu_norm_g, w_spatial,
              b_spatial, q_norm_g, k_norm_g, rpb, w_out):
    B, L, _ = x.shape
    Bc, C, _ = ctx.shape
    for layer in range(DEPTH):
        last = layer == DEPTH - 1
        shift, scale, gate = ada_params(c, w_ada[layer], b_ada[layer])
        cshift, cscale, cgate = ada_params(c_ctx, w_ada[layer], b_ada[layer])
        h = rms_norm(x, norm_g[layer]) * (1.0 + scale) + shift
        hc = rms_norm(ctx, norm_g[layer]) * (1.0 + cscale) + cshift

        z = h @ w_in[layer]
        a_u, a_v, a_g, b_q, b_k, b_v, b_g = jnp.split(z, SPLIT_POINTS, axis=-1)
        q = rms_norm(b_q.reshape(B, L, NA_HEADS, NA_HEAD_DIM), q_norm_g[layer])
        k = rms_norm(b_k.reshape(B, L, NA_HEADS, NA_HEAD_DIM), k_norm_g[layer])
        v = b_v.reshape(B, L, NA_HEADS, NA_HEAD_DIM)

        if last:
            ck, cv = jnp.split(hc @ w_in[layer][:, KV_START:KV_END], 2, axis=-1)
        else:
            zc = hc @ w_in[layer]
            cu, cvv, cga, cq, ck, cv, cgb = jnp.split(zc, SPLIT_POINTS, axis=-1)
        ck = rms_norm(ck.reshape(Bc, C, NA_HEADS, NA_HEAD_DIM), k_norm_g[layer])
        cv = cv.reshape(Bc, C, NA_HEADS, NA_HEAD_DIM)

        out_a = chunk_sgu(a_u, a_v, a_g, sgu_norm_g[layer], w_spatial[layer], b_spatial[layer])
        out_b = neighborhood_attention(q, k, v, ck, cv, rpb[layer]).reshape(B, L, D_B) * jax.nn.silu(b_g)
        mix = jnp.concatenate([out_a, out_b], axis=-1) @ w_out[layer]
        new_x = x + gate * mix

        if not last:
            cq = rms_norm(cq.reshape(Bc, C, NA_HEADS, NA_HEAD_DIM), q_norm_g[layer])
            cout_a = chunk_sgu(cu, cvv, cga, sgu_norm_g[layer], w_spatial[layer], b_spatial[layer])
            cout_b = context_attention(cq, ck, cv).reshape(Bc, C, D_B) * jax.nn.silu(cgb)
            cmix = jnp.concatenate([cout_a, cout_b], axis=-1) @ w_out[layer]
            ctx = ctx + cgate * cmix
        x = new_x
    return x


_drawn_inputs = setup_inputs


def setup_inputs(seed=0):
    import zlib

    import numpy as np

    out = dict(_drawn_inputs(seed))
    spreads = {}
    factors = {'ctx': 5.773,
     'b_ada': 6.379,
     'norm_g': 8.0,
     'sgu_norm_g': 8.0,
     'b_spatial': 8.0,
     'q_norm_g': 8.0,
     'k_norm_g': 8.0,
     'rpb': 8.0}
    for name, (base, spread) in spreads.items():
        noise = np.random.default_rng([zlib.crc32(name.encode()), seed]).standard_normal(out[name].shape)
        drawn = base * np.exp(spread * noise) if base else spread * noise
        out[name] = __import__('jax').numpy.asarray(drawn.astype(out[name].dtype))
    for name, factor in factors.items():
        out[name] = (out[name] * factor).astype(out[name].dtype)
    return out
```

```python
import concourse.bass as bass
from concourse import mybir
from contextlib import ExitStack

F32 = mybir.dt.float32
F32R = mybir.dt.float32r
ACT = mybir.ActivationFunctionType
ALU = mybir.AluOpType
AX = mybir.AxisListType

P = 128
D = 1024
KT = D // P
L = 4096
CTX = 256
DA = 512
GROUPS = 4
H = 8
DH = 64
PAIRS = H // 2
GW = 64
GR = 4
HC = 32
GN = L // (GR * GW)
TILES = L // P
WR, WC = 8, 16
RPR, RPC = 2 * WR - 1, 2 * WC - 1
SC = 8
MAIN = 3 * P
SIDE = 3 * GR * SC
LAT = MAIN + SIDE
KEYS = LAT + CTX
SIDECTX = SIDE + CTX
KCH = 6
RING = 4
MIRROR = RING + 2
EPS = 1e-6
MASKED = -1e30
LOWEST = -3.0e38
PAD, PAD_END = 64, 192
MODS = 3 * D


def wait(e, sem, count):
    if not (isinstance(count, int) and count <= 0):
        e.wait_ge(sem, count)


def build(nc, x, c, ctx_in, c_ctx, w_ada, b_ada, norm_g, w_in, sgu_norm_g, w_spatial, b_spatial,
          q_norm_g, k_norm_g, rpb, w_out, out):
    x2, ctx2, out2 = x[0], ctx_in[0], out[0]
    with ExitStack() as top:
        def dram(name, shape):
            return nc.dram_tensor(name, shape, F32, kind="Internal").ap()

        outa_d = dram("outa_d", [L, DA])
        outb_d = dram("outb_d", [TILES, P, DA])
        kT_d = dram("kT_d", [TILES + 2, P, PAIRS, P])
        v_d = dram("v_d", [TILES + 2, P, DA])
        kside_d = dram("kside_d", [P, PAIRS, TILES + 2, GR * SC])
        qT_d = dram("qT_d", [TILES, P, PAIRS, P])
        sg_d = dram("sg_d", [TILES, P, DA])
        kctx_d = dram("kctx_d", [P, PAIRS, CTX])
        vctx_d = dram("vctx_d", [CTX, DA])
        rpbpad_d = dram("rpbpad_d", [1, PAD + H * RPR * RPC + PAD_END])
        bias_d = dram("bias_d", [2, P, H, RPR, HC + SC])
        mask_d = dram("mask_d", [P, 2, 3, LAT])

        def sbt(name, shape, dt=F32):
            return top.enter_context(nc.sbuf_tensor(name, shape, dt))

        ident = sbt("ident", [P, P])
        a_col = sbt("a_col", [P, 2, KT])
        b_col = sbt("b_col", [P, 2, KT])
        gate_bc = sbt("gate_bc", [P, D])

        modulate(nc, ident, a_col, b_col, gate_bc, c, c_ctx, w_ada, b_ada, norm_g, rpb,
                 rpbpad_d, mask_d, kT_d, v_d, kside_d)
        gating(nc, ident, a_col, b_col, x2, w_in, sgu_norm_g, w_spatial, b_spatial, outa_d,
               rpbpad_d, bias_d)
        project(nc, ident, a_col, b_col, x2, ctx2, w_in, q_norm_g, k_norm_g,
                qT_d, kT_d, v_d, kside_d, sg_d, kctx_d, vctx_d)
        attend(nc, ident, qT_d, kT_d, v_d, kside_d, sg_d, kctx_d, vctx_d, bias_d, mask_d, outb_d)
        combine(nc, ident, gate_bc, x2, w_out, outa_d, outb_d, out2)


def modulate(nc, ident, a_col, b_col, gate_bc, c, c_ctx, w_ada, b_ada, norm_g, rpb,
             rpbpad_d, mask_d, kT_d, v_d, kside_d):
    NB = MODS // 512
    ROWS = 5 * KT
    with nc.cleanup_on_exit(), ExitStack() as cx:
        sb = lambda n, s, d=F32: cx.enter_context(nc.sbuf_tensor("mod_" + n, s, d))
        ps = lambda n, s: cx.enter_context(nc.psum_tensor("mod_" + n, s, F32))
        sem = lambda n: nc.alloc_semaphore("mod_" + n)
        rows = sb("rows", [ROWS, P])
        cols = sb("cols", [P, ROWS])
        cth = sb("cth", [P, 2 * KT])
        csum = sb("csum", [P, 2 * KT])
        cond = sb("cond", [P, 2 * KT])
        wada = [sb(f"wada{k}", [P, MODS]) for k in range(4)]
        mod = sb("mod", [2, MODS])
        ones = sb("ones", [1, P])
        bgate = sb("bgate", [1, D])
        gate_row = sb("gate_row", [1, D])
        scale1 = sb("scale1", [P, 2, KT])
        scale2 = sb("scale2", [P, 2, KT])
        rpb_row = sb("rpb_row", [1, PAD + H * RPR * RPC + PAD_END])
        masks = sb("masks", [P, 2, 3, LAT])
        zeros = sb("zeros", [P, DA])
        p_mod = [ps(f"p_mod{n}", [2, 512]) for n in range(NB)]
        p_cols = ps("p_cols", [P, 512])
        p_gate = ps("p_gate", [P, 512])

        rows_in = sem("rows_in")
        wada_in = [sem(f"wada_in{k}") for k in range(4)]
        wada_used = sem("wada_used")
        bgate_in = sem("bgate_in")
        ident_ready = sem("ident_ready")
        consts_ready = sem("consts_ready")
        cols_t = sem("cols_t")
        cols_ready = sem("cols_ready")
        cth_ready = sem("cth_ready")
        csum_ready = sem("csum_ready")
        cond_ready = sem("cond_ready")
        mods_ready = sem("mods_ready")
        mod_copied = sem("mod_copied")
        modcols_t = sem("modcols_t")
        scale_step = sem("scale_step")
        gate_added = sem("gate_added")
        gate_p = sem("gate_p")
        gate_copied = sem("gate_copied")
        rpb_zeroed = sem("rpb_zeroed")
        rpb_in = sem("rpb_in")
        rpb_out = sem("rpb_out")
        mask_step = sem("mask_step")
        masks_ready = sem("masks_ready")
        zeros_ready = sem("zeros_ready")
        side_out = sem("side_out")
        block = cx.enter_context(nc.Block())

        @block.sync
        def _(sp):
            sp.dma_start(rows[0:KT, :], c.rearrange("b (k p) -> (b k) p", p=P)).then_inc(rows_in, 16)
            sp.dma_start(rows[KT:2 * KT, :], c_ctx.rearrange("(k p) -> k p", p=P)).then_inc(rows_in, 16)
            sp.dma_start(rows[2 * KT:3 * KT, :], norm_g.rearrange("b (k p) -> (b k) p", p=P)).then_inc(rows_in, 16)
            sp.dma_start(rows[3 * KT:5 * KT, :],
                         b_ada[:, 0:2 * D].rearrange("b (k p) -> (b k) p", p=P)).then_inc(rows_in, 16)
            for k in range(KT):
                if k >= 4:
                    sp.wait_ge(wada_used, k - 3)
                sp.dma_start(wada[k % 4][:], w_ada[0, k * P:(k + 1) * P, :]).then_inc(wada_in[k % 4], 16)
            sp.dma_start(bgate[:], b_ada[:, 2 * D:3 * D]).then_inc(bgate_in, 16)

        @block.scalar
        def _(act):
            act.wait_ge(zeros_ready, 1)
            for n in (0, TILES + 1):
                act.dma_start(kT_d[n], zeros[:].rearrange("p (a b) -> p a b", a=PAIRS)).then_inc(side_out, 16)
                act.dma_start(v_d[n], zeros[:]).then_inc(side_out, 16)
                act.dma_start(kside_d[:, :, n, :],
                              zeros[:, 0:P].rearrange("p (a b) -> p a b", a=PAIRS)).then_inc(side_out, 16)
            act.wait_ge(rpb_zeroed, 1)
            act.dma_start(rpb_row[:, PAD:PAD + H * RPR * RPC],
                          rpb.rearrange("b h r c -> b (h r c)")).then_inc(rpb_in, 16)
            act.wait_ge(cols_ready, 1)
            nc.scalar.activation(cth[:], cols[:, 0:2 * KT], ACT.Tanh, scale=0.5).then_inc(cth_ready, 1)
            act.wait_ge(rpb_in, 16)
            act.dma_start(rpbpad_d, rpb_row[:]).then_inc(rpb_out, 16)
            act.wait_ge(masks_ready, 1)
            act.dma_start(mask_d, masks[:]).then_inc(side_out, 16)
            act.wait_ge(rpb_out, 16)
            act.wait_ge(side_out, 7 * 16)

        @block.gpsimd
        def _(pool):
            nc.gpsimd.memset(ident[:], 0.0).then_inc(ident_ready, 1)
            nc.gpsimd.memset(ones[:], 1.0).then_inc(consts_ready, 1)
            pool.wait_ge(ident_ready, 1)
            nc.gpsimd.affine_select(out=ident[:], in_=ident[:], compare_op=ALU.not_equal, fill=1.0, base=0,
                                    pattern=[[-1, P]], channel_multiplier=1).then_inc(ident_ready, 1)
            nc.gpsimd.memset(zeros[:], 0.0).then_inc(zeros_ready, 1)
            nc.gpsimd.memset(rpb_row[:], 0.0).then_inc(rpb_zeroed, 1)
            step = 1
            nc.gpsimd.memset(masks[:], 0.0).then_inc(mask_step, 1)
            for half in range(2):
                for qr in range(GR):
                    q = slice(qr * HC, (qr + 1) * HC)
                    at_main, at_side = (0, HC), (MAIN, SC)

                    def keep(part, lo, hi, compare, base, mult, patt):
                        first, width = part
                        for edge in range(3):
                            view = masks[q, half, edge, first:first + 3 * GR * width].rearrange(
                                "p (r c) -> p r c", c=width)[:, :, lo:hi]
                            nc.gpsimd.affine_select(out=view, in_=view, compare_op=compare, fill=MASKED, base=base,
                                                    pattern=[[0, 3 * GR], [patt, hi - lo]],
                                                    channel_multiplier=mult).then_inc(mask_step, 1)

                    pool.wait_ge(mask_step, step)
                    if half == 0:
                        keep(at_main, 0, HC, ALU.is_ge, WC // 2, -1, 1)
                        pool.wait_ge(mask_step, step + 3)
                        keep(at_main, WC, HC, ALU.is_ge, WC // 2 - 1 - WC, 1, -1)
                        keep(at_side, 0, SC, ALU.is_ge, WC // 2 - 1 - HC, 1, -1)
                    else:
                        keep(at_main, 0, WC, ALU.is_ge, WC // 2, -1, 1)
                        pool.wait_ge(mask_step, step + 3)
                        keep(at_main, 0, HC, ALU.is_ge, WC // 2 - 1, 1, -1)
                        keep(at_side, 0, SC, ALU.is_ge, 0, -1, 1)
                    step += 9
                    pool.wait_ge(mask_step, step)
                    for edge, first in enumerate((GR, qr, 0)):
                        for lo, hi in ((0, first), (first + WR, 3 * GR)):
                            if lo < hi:
                                nc.gpsimd.memset(masks[q, half, edge, lo * HC:hi * HC], MASKED).then_inc(mask_step, 1)
                                nc.gpsimd.memset(masks[q, half, edge, MAIN + lo * SC:MAIN + hi * SC],
                                                 MASKED).then_inc(mask_step, 1)
                                step += 2
            pool.wait_ge(mask_step, step)
            pool.sem_inc(masks_ready, 1)

        @block.tensor
        def _(pe):
            pe.wait_ge(ident_ready, 2)
            pe.wait_ge(rows_in, 64)
            nc.tensor.transpose(p_cols[:, 0:ROWS], rows[:], ident[0:ROWS, 0:ROWS]).then_inc(cols_t, 1)
            pe.wait_ge(cond_ready, 1)
            cond3 = cond[:].rearrange("p (s k) -> p s k", s=2)
            for k in range(KT):
                pe.wait_ge(wada_in[k % 4], 16 * (k // 4 + 1))
                for n in range(NB):
                    last = nc.tensor.matmul(p_mod[n][:], cond3[:, :, k], wada[k % 4][:, n * 512:(n + 1) * 512],
                                            start=(k == 0), stop=(k == KT - 1))
                last.then_inc(wada_used, 1)
            pe.wait_ge(mod_copied, 1)
            for j in range(2 * KT):
                last = nc.tensor.transpose(p_cols[:, 64 + 2 * j:66 + 2 * j], mod[:, j * P:(j + 1) * P], ident[0:2, 0:2])
            last.then_inc(modcols_t, 1)
            pe.wait_ge(consts_ready, 1)
            for n in range(2):
                pe.wait_ge(gate_added, 1)
                if n == 1:
                    pe.wait_ge(gate_copied, 1)
                nc.tensor.matmul(p_gate[:], ones[:], gate_row[:, n * 512:(n + 1) * 512],
                                 start=True, stop=True).then_inc(gate_p, 1)

        @block.vector
        def _(dve):
            dve.wait_ge(cols_t, 1)
            nc.vector.tensor_copy(cols[:], p_cols[:, 0:ROWS]).then_inc(cols_ready, 1)
            dve.wait_ge(cth_ready, 1)
            nc.vector.tensor_scalar(csum[:], cth[:], 1.0, 0.5, ALU.add, ALU.mult).then_inc(csum_ready, 1)
            dve.wait_ge(csum_ready, 1)
            nc.vector.tensor_tensor(cond[:], csum[:], cols[:, 0:2 * KT], ALU.mult).then_inc(cond_ready, 1)
            dve.wait_ge(wada_used, KT)
            for n in range(NB):
                last = nc.vector.tensor_copy(mod[:, n * 512:(n + 1) * 512], p_mod[n][:])
            last.then_inc(mod_copied, 1)
            dve.wait_ge(mod_copied, 1)
            dve.wait_ge(bgate_in, 16)
            nc.vector.tensor_tensor(gate_row[:], mod[0:1, 2 * D:3 * D], bgate[:], ALU.add).then_inc(gate_added, 1)
            dve.wait_ge(modcols_t, 1)
            both = p_cols[:, 64:64 + 4 * KT].rearrange("p (j k s) -> p j s k", j=2, s=2)
            for s in range(2):
                nc.vector.tensor_tensor(b_col[:, s, :], both[:, 0, s, :], cols[:, 3 * KT:4 * KT], ALU.add)
                nc.vector.tensor_tensor(scale1[:, s, :], both[:, 1, s, :], cols[:, 4 * KT:5 * KT],
                                        ALU.add).then_inc(scale_step, 1)
            dve.wait_ge(scale_step, 2)
            nc.vector.tensor_scalar(scale2[:], scale1[:], 1.0, None, ALU.add).then_inc(scale_step, 1)
            dve.wait_ge(scale_step, 3)
            for s in range(2):
                nc.vector.tensor_tensor(a_col[:, s, :], scale2[:, s, :], cols[:, 2 * KT:3 * KT], ALU.mult)
            for n in range(2):
                dve.wait_ge(gate_p, n + 1)
                nc.vector.tensor_copy(gate_bc[:, n * 512:(n + 1) * 512], p_gate[:]).then_inc(gate_copied, 1)


class SplitWeights:

    def __init__(self, nc, cx, name, source, width):
        self.nc, self.source, self.half = nc, source, width // 2
        self.raw = [cx.enter_context(nc.sbuf_tensor(f"{name}_raw{k}", [P, self.half], F32)) for k in range(2)]
        self.hi = cx.enter_context(nc.sbuf_tensor(f"{name}_hi", [P, KT, width], F32R))
        self.lo = cx.enter_context(nc.sbuf_tensor(f"{name}_lo", [P, KT, width], F32R))
        self.loaded = [nc.alloc_semaphore(f"{name}_loaded{k}") for k in range(2)]
        self.hi_done = nc.alloc_semaphore(f"{name}_hi_done")
        self.lo_done = nc.alloc_semaphore(f"{name}_lo_done")

    CHUNKS = 2 * KT

    def part(self, n):
        return n // 2, slice((n % 2) * self.half, (n % 2 + 1) * self.half)

    def load(self, dma):
        for n in range(self.CHUNKS):
            k, cols = self.part(n)
            if n >= 2:
                dma.wait_ge(self.lo_done, n - 1)
            dma.dma_start(self.raw[n % 2][:], self.source[k * P:(k + 1) * P, cols]).then_inc(self.loaded[n % 2], 16)

    def round_hi(self, act):
        for n in range(self.CHUNKS):
            k, cols = self.part(n)
            act.wait_ge(self.loaded[n % 2], 16 * (n // 2 + 1))
            self.nc.scalar.activation(self.hi[:, k, cols], self.raw[n % 2][:], ACT.Copy).then_inc(self.hi_done, 1)

    def take_lo(self, dve):
        for n in range(self.CHUNKS):
            k, cols = self.part(n)
            dve.wait_ge(self.hi_done, n + 1)
            self.nc.vector.tensor_tensor(self.lo[:, k, cols], self.raw[n % 2][:], self.hi[:, k, cols].bitcast(F32),
                                         ALU.subtract).then_inc(self.lo_done, 1)


class NormedInput:

    def __init__(self, nc, cx, stage, ident):
        self.nc, self.ident = nc, ident
        sb = lambda n, s, d=F32: cx.enter_context(nc.sbuf_tensor(f"{stage}_{n}", s, d))
        sem = lambda n: nc.alloc_semaphore(f"{stage}_{n}")
        self.xt = [sb(f"xt{k}", [P, D]) for k in range(2)]
        self.squares = sb("x_squares", [P, D], mybir.dt.bfloat16)
        self.sumsq = sb("x_sumsq", [P, 2])
        self.meansq = sb("x_meansq", [P, 2])
        self.rstd = sb("x_rstd", [P, 2])
        self.minus_half = sb("minus_half", [P, 2 * H])
        self.normed = sb("x_normed", [P, D])
        self.hT = sb("hT", [P, KT, P])
        self.hi = [sb(f"hT_hi{k}", [P, KT, P], F32R) for k in range(2)]
        self.lo = [sb(f"hT_lo{k}", [P, KT, P], F32R) for k in range(2)]
        self.p_t = cx.enter_context(nc.psum_tensor(f"{stage}_p_hT", [P, KT, P], F32))
        self.x_in = [sem(f"x_in{k}") for k in range(2)]
        self.half_ready = sem("half_ready")
        self.sumsq_ready = sem("sumsq_ready")
        self.meansq_ready = sem("meansq_ready")
        self.rstd_ready = sem("rstd_ready")
        self.normed_ready = sem("normed_ready")
        self.transposed = sem("transposed")
        self.modulated = sem("modulated")
        self.hi_ready = sem("hi_ready")
        self.split_ready = sem("split_ready")
        self.tile_done = sem("tile_done")

    def square(self, act, i, u):
        t = 2 * i + u
        act.wait_ge(self.x_in[u], 16 * (i + 1))
        wait(act, self.meansq_ready, t - 1)
        wait(act, self.sumsq_ready, t)
        self.nc.scalar.activation(self.squares[:], self.xt[u][:], ACT.Square,
                                  accum_out=self.sumsq[:, u:u + 1]).then_inc(self.sumsq_ready, 1)

    def mean(self, dve, i, u):
        t = 2 * i + u
        dve.wait_ge(self.sumsq_ready, t + 1)
        wait(dve, self.rstd_ready, t - 1)
        self.nc.vector.tensor_scalar(self.meansq[:, u:u + 1], self.sumsq[:, u:u + 1], 1.0 / D, EPS,
                                     ALU.mult, ALU.add).then_inc(self.meansq_ready, 1)

    def root(self, pool, i, u):
        t = 2 * i + u
        pool.wait_ge(self.meansq_ready, t + 1)
        wait(pool, self.normed_ready, t - 1)
        self.nc.gpsimd.tensor_tensor(self.rstd[:, u:u + 1], self.meansq[:, u:u + 1], self.minus_half[:, 0:1],
                                     ALU.pow).then_inc(self.rstd_ready, 1)

    def normalise(self, dve, i, u):
        t = 2 * i + u
        dve.wait_ge(self.rstd_ready, t + 1)
        wait(dve, self.transposed, t)
        self.nc.vector.tensor_scalar(self.normed[:], self.xt[u][:], self.rstd[:, u:u + 1], None,
                                     ALU.mult).then_inc(self.normed_ready, 1)

    def transpose(self, pe, i, u):
        t = 2 * i + u
        pe.wait_ge(self.normed_ready, t + 1)
        wait(pe, self.modulated, t)
        for k in range(KT):
            last = self.nc.tensor.transpose(self.p_t[:, k, :], self.normed[:, k * P:(k + 1) * P], self.ident[:])
        last.then_inc(self.transposed, 1)

    def modulate(self, act, i, u, a_col, b_col):
        t = 2 * i + u
        act.wait_ge(self.transposed, t + 1)
        wait(act, self.split_ready, t)
        for k in range(KT):
            last = self.nc.scalar.activation(self.hT[:, k, :], self.p_t[:, k, :], ACT.Identity,
                                             scale=a_col[:, k:k + 1], bias=b_col[:, k:k + 1])
        last.then_inc(self.modulated, 1)

    def split(self, dve, i, u):
        t = 2 * i + u
        dve.wait_ge(self.modulated, t + 1)
        wait(dve, self.tile_done, t - 1)
        self.nc.vector.tensor_copy(self.hi[u][:], self.hT[:]).then_inc(self.hi_ready, 1)
        dve.wait_ge(self.hi_ready, t + 1)
        self.nc.vector.tensor_tensor(self.lo[u][:], self.hT[:], self.hi[u][:].bitcast(F32),
                                     ALU.subtract).then_inc(self.split_ready, 1)

    def products(self, u, bank, weights, col, width=512):
        c = slice(col, col + width)
        for k in range(KT):
            self.nc.tensor.matmul(bank, self.hi[u][:, k, :], weights.hi[:, k, c], start=(k == 0), stop=False)
            self.nc.tensor.matmul(bank, self.hi[u][:, k, :], weights.lo[:, k, c], start=False, stop=False)
            last = self.nc.tensor.matmul(bank, self.lo[u][:, k, :], weights.hi[:, k, c],
                                         start=False, stop=(k == KT - 1))
        return last


def gating(nc, ident, a_col, b_col, x2, w_in, sgu_norm_g, w_spatial, b_spatial, outa_d, rpbpad_d, bias_d):
    U, V, G = 0, DA, 2 * DA
    CH = DA // GROUPS
    with nc.cleanup_on_exit(), ExitStack() as cx:
        sb = lambda n, s, d=F32: cx.enter_context(nc.sbuf_tensor("sgu_" + n, s, d))
        ps = lambda n, s: cx.enter_context(nc.psum_tensor("sgu_" + n, s, F32))
        sem = lambda n: nc.alloc_semaphore("sgu_" + n)
        w = SplitWeights(nc, cx, "wa", w_in[0, :, 0:3 * DA], 3 * DA)
        h = NormedInput(nc, cx, "sgu", ident)
        ws_raw = sb("ws_raw", [P, GROUPS, P])
        wsT = sb("wsT", [P, GROUPS, P])
        bs_raw = sb("bs_raw", [GROUPS, P])
        bs = sb("bs", [P, GROUPS])
        sgu_bc = sb("sgu_bc", [P, DA])
        v_act = sb("v_act", [P, DA])
        v_squares = sb("v_squares", [P, DA])
        v_sumsq = sb("v_sumsq", [P, GROUPS])
        v_meansq = sb("v_meansq", [P, GROUPS])
        v_rstd = sb("v_rstd", [P, GROUPS])
        v_normed = sb("v_normed", [P, DA])
        u_act = sb("u_act", [P, DA])
        g_tanh = sb("g_tanh", [P, DA])
        g_silu2 = sb("g_silu2", [P, DA])
        gated = sb("gated", [P, DA])
        outa = [sb(f"outa{k}", [P, DA]) for k in range(2)]
        p_v, p_u, p_g, p_mix = ps("p_v", [P, DA]), ps("p_u", [P, DA]), ps("p_g", [P, DA]), ps("p_mix", [P, DA])

        small_in = sem("small_in")
        half_ready = h.half_ready
        ws_t = sem("ws_t")
        ws_ready = sem("ws_ready")
        bias_out = sem("bias_out")
        v_ready, u_ready = sem("v_ready"), sem("u_ready")
        g_ready = h.tile_done
        v_gelu, u_gelu, g_tanh_ready = sem("v_gelu"), sem("u_gelu"), sem("g_tanh_ready")
        v_sumsq_ready, v_meansq_ready, v_rstd_ready = sem("v_ssq"), sem("v_msq"), sem("v_rstd_ready")
        v_normed_ready = sem("v_normed_ready")
        mix_ready = sem("mix_ready")
        silu_ready = sem("silu_ready")
        gated_ready = sem("gated_ready")
        outa_ready = sem("outa_ready")
        outa_out = [sem(f"outa_out{k}") for k in range(2)]
        block = cx.enter_context(nc.Block())
        PT = TILES // 2

        def load_x(dma, i, u):
            dma.dma_start(h.xt[u][:], x2[bass.ds((2 * i + u) * P, P), :]).then_inc(h.x_in[u], 16)

        @block.sync
        def _(sp):
            load_x(sp, 0, 0)
            load_x(sp, 0, 1)
            w.load(sp)

            def tile(i, u, more):
                t = 2 * i + u
                if more:
                    sp.wait_ge(h.normed_ready, t + 1)
                    load_x(sp, i + 1, u)
                sp.wait_ge(outa_ready, t + 1)
                sp.dma_start(outa_d[bass.ds(t * P, P), :], outa[u][:]).then_inc(outa_out[u], 16)

            for u in range(2):
                tile(0, u, True)
            with sp.Fori(1, PT - 1) as i:
                for u in range(2):
                    tile(i, u, True)
            for u in range(2):
                tile(PT - 1, u, False)
            for u in range(2):
                sp.wait_ge(outa_out[u], 16 * PT)

        @block.gpsimd
        def _(pool):
            nc.gpsimd.memset(h.minus_half[:], -0.5).then_inc(half_ready, 1)
            pool.wait_ge(half_ready, 1)

            def tile(i, u, more):
                t = 2 * i + u
                if more:
                    h.root(pool, i + (u + 1) // 2, (u + 1) % 2)
                pool.wait_ge(v_meansq_ready, t + 1)
                wait(pool, v_normed_ready, t)
                nc.gpsimd.tensor_tensor(v_rstd[:], v_meansq[:], h.minus_half[:, 0:GROUPS],
                                        ALU.pow).then_inc(v_rstd_ready, 1)

            h.root(pool, 0, 0)
            for u in range(2):
                tile(0, u, True)
            with pool.Fori(1, PT - 1) as i:
                for u in range(2):
                    tile(i, u, True)
            for u in range(2):
                tile(PT - 1, u, u == 0)

        @block.scalar
        def _(act):
            act.dma_start(ws_raw[:], w_spatial[0].rearrange("g p q -> p g q")).then_inc(small_in, 16)
            act.dma_start(bs_raw[:], b_spatial[0]).then_inc(small_in, 16)
            act.dma_start(sgu_bc[:], sgu_norm_g.to_broadcast([P, DA])).then_inc(small_in, 16)
            for half in range(2):
                for qr in range(GR):
                    at = PAD + (GR - 1 - qr) * RPC + WC - 1 - half * SC
                    act.dma_start(
                        bias_d[half, qr * HC:(qr + 1) * HC].rearrange("p n r c -> (n r) p c"),
                        bass.AP(rpbpad_d.tensor, at,
                                [[RPC, H * RPR], [-1, HC], [1, HC + SC]])).then_inc(bias_out, 16)
            h.square(act, 0, 0)
            h.modulate(act, 0, 0, a_col[:, 0, :], b_col[:, 0, :])
            w.round_hi(act)

            def tile(i, u, more):
                t = 2 * i + u
                n, m = i + (u + 1) // 2, (u + 1) % 2
                if more:
                    h.square(act, n, m)
                act.wait_ge(v_ready, t + 1)
                wait(act, v_normed_ready, t)
                nc.scalar.activation(v_act[:], p_v[:], ACT.Gelu).then_inc(v_gelu, 1)
                act.wait_ge(v_gelu, t + 1)
                wait(act, v_meansq_ready, t)
                for k in range(GROUPS):
                    last = nc.scalar.activation(v_squares[:, k * CH:(k + 1) * CH], v_act[:, k * CH:(k + 1) * CH], ACT.Square,
                                                accum_out=v_sumsq[:, k:k + 1])
                last.then_inc(v_sumsq_ready, 1)
                act.wait_ge(u_ready, t + 1)
                wait(act, gated_ready, t)
                nc.scalar.activation(u_act[:], p_u[:], ACT.Gelu).then_inc(u_gelu, 1)
                if more:
                    h.modulate(act, n, m, a_col[:, 0, :], b_col[:, 0, :])
                act.wait_ge(g_ready, t + 1)
                wait(act, silu_ready, t)
                nc.scalar.activation(g_tanh[:], p_g[:], ACT.Tanh, scale=0.5).then_inc(g_tanh_ready, 1)

            for u in range(2):
                tile(0, u, True)
            with act.Fori(1, PT - 1) as i:
                for u in range(2):
                    tile(i, u, True)
            for u in range(2):
                tile(PT - 1, u, u == 0)
            act.wait_ge(bias_out, 16 * 2 * GR)

        @block.tensor
        def _(pe):
            h.transpose(pe, 0, 0)
            pe.wait_ge(small_in, 48)
            for k in range(GROUPS):
                nc.tensor.transpose(p_mix[:, k * P:(k + 1) * P], ws_raw[:, k, :], ident[:])
            nc.tensor.transpose(p_g[:, 0:GROUPS], bs_raw[:], ident[0:GROUPS, 0:GROUPS]).then_inc(ws_t, 1)
            pe.wait_ge(w.lo_done, w.CHUNKS)

            def tile(i, u, more):
                t = 2 * i + u
                pe.wait_ge(h.split_ready, t + 1)
                wait(pe, v_gelu, t)
                h.products(u, p_v[:], w, V).then_inc(v_ready, 1)
                wait(pe, u_gelu, t)
                h.products(u, p_u[:], w, U).then_inc(u_ready, 1)
                if more:
                    h.transpose(pe, i + (u + 1) // 2, (u + 1) % 2)
                wait(pe, silu_ready, t)
                if isinstance(t, int) and t == 0:
                    pe.wait_ge(ws_ready, 1)
                h.products(u, p_g[:], w, G).then_inc(h.tile_done, 1)
                pe.wait_ge(v_normed_ready, t + 1)
                wait(pe, gated_ready, t)
                for k in range(GROUPS):
                    last = nc.tensor.matmul(p_mix[:, k * CH:(k + 1) * CH], wsT[:, k, :],
                                            v_normed[:, k * CH:(k + 1) * CH], start=True, stop=True)
                last.then_inc(mix_ready, 1)

            for u in range(2):
                tile(0, u, True)
            with pe.Fori(1, PT - 1) as i:
                for u in range(2):
                    tile(i, u, True)
            for u in range(2):
                tile(PT - 1, u, u == 0)

        @block.vector
        def _(dve):
            h.mean(dve, 0, 0)
            h.normalise(dve, 0, 0)
            h.split(dve, 0, 0)
            dve.wait_ge(ws_t, 1)
            nc.vector.tensor_copy(wsT[:].rearrange("p a b -> p (a b)"), p_mix[:])
            nc.vector.tensor_copy(bs[:], p_g[:, 0:GROUPS]).then_inc(ws_ready, 1)
            w.take_lo(dve)

            def tile(i, u, more):
                t = 2 * i + u
                n, m = i + (u + 1) // 2, (u + 1) % 2
                if more:
                    h.mean(dve, n, m)
                    h.normalise(dve, n, m)
                dve.wait_ge(v_sumsq_ready, t + 1)
                wait(dve, v_rstd_ready, t)
                nc.vector.tensor_scalar(v_meansq[:], v_sumsq[:], 1.0 / CH, EPS, ALU.mult,
                                        ALU.add).then_inc(v_meansq_ready, 1)
                dve.wait_ge(v_rstd_ready, t + 1)
                wait(dve, mix_ready, t)
                for k in range(GROUPS):
                    s = slice(k * CH, (k + 1) * CH)
                    last = nc.vector.scalar_tensor_tensor(out=v_normed[:, s], in0=v_act[:, s],
                                                          scalar=v_rstd[:, k:k + 1], in1=sgu_bc[:, s],
                                                          op0=ALU.mult, op1=ALU.mult)
                last.then_inc(v_normed_ready, 1)
                if more:
                    h.split(dve, n, m)
                dve.wait_ge(g_tanh_ready, t + 1)
                wait(dve, outa_ready, t)
                nc.vector.scalar_tensor_tensor(out=g_silu2[:], in0=g_tanh[:], scalar=1.0, in1=p_g[:],
                                               op0=ALU.add, op1=ALU.mult).then_inc(silu_ready, 1)
                dve.wait_ge(mix_ready, t + 1)
                dve.wait_ge(u_gelu, t + 1)
                for k in range(GROUPS):
                    s = slice(k * CH, (k + 1) * CH)
                    last = nc.vector.scalar_tensor_tensor(out=gated[:, s], in0=p_mix[:, s], scalar=bs[:, k:k + 1],
                                                          in1=u_act[:, s], op0=ALU.add, op1=ALU.mult)
                last.then_inc(gated_ready, 1)
                dve.wait_ge(gated_ready, t + 1)
                dve.wait_ge(silu_ready, t + 1)
                wait(dve, outa_out[u], 16 * i)
                nc.vector.scalar_tensor_tensor(out=outa[u][:], in0=g_silu2[:], scalar=0.5, in1=gated[:],
                                               op0=ALU.mult, op1=ALU.mult).then_inc(outa_ready, 1)

            for u in range(2):
                tile(0, u, True)
            with dve.Fori(1, PT - 1) as i:
                for u in range(2):
                    tile(i, u, True)
            for u in range(2):
                tile(PT - 1, u, u == 0)


def project(nc, ident, a_col, b_col, x2, ctx2, w_in, q_norm_g, k_norm_g,
            qT_d, kT_d, v_d, kside_d, sg_d, kctx_d, vctx_d):
    Q, K, V, G = 0, DA, 2 * DA, 3 * DA
    with nc.cleanup_on_exit(), ExitStack() as cx:
        sb = lambda n, s, d=F32: cx.enter_context(nc.sbuf_tensor("pro_" + n, s, d))
        ps = lambda n, s: cx.enter_context(nc.psum_tensor("pro_" + n, s, F32))
        sem = lambda n: nc.alloc_semaphore("pro_" + n)
        w = SplitWeights(nc, cx, "wb", w_in[0, :, 3 * DA:7 * DA], 4 * DA)
        h = NormedInput(nc, cx, "pro", ident)
        gq = sb("gq", [P, 2])
        gk = sb("gk", [P, 1])
        squares = sb("qk_squares", [P, 2, DA])
        sumsq = sb("qk_sumsq", [P, 2 * H])
        meansq = sb("qk_meansq", [P, 2 * H])
        rstd = sb("qk_rstd", [P, 2 * H])
        qkn = sb("qkn", [P, 2, DA])
        g_tanh = sb("bg_tanh", [P, DA])
        qT = [sb(f"qT{k}", [P, PAIRS, P]) for k in range(2)]
        kT = [sb(f"kT{k}", [P, PAIRS, P]) for k in range(2)]
        kside = [sb(f"kside{k}", [P, PAIRS, GR, SC]) for k in range(2)]
        v_sb = [sb(f"v_sb{k}", [P, DA]) for k in range(2)]
        sg = [sb(f"sg{k}", [P, DA]) for k in range(2)]
        p_q, p_k, p_v, p_g = ps("pb_q", [P, DA]), ps("pb_k", [P, DA]), ps("pb_v", [P, DA]), ps("pb_g", [P, DA])
        p_qT, p_kT = ps("p_qT", [P, PAIRS * P]), ps("p_kT", [P, PAIRS * P])

        gains_in = sem("gains_in")
        gq_ready = sem("gq_ready")
        q_ready, k_ready, v_ready = sem("q_ready"), sem("k_ready"), sem("vb_ready")
        q_squared, k_squared = sem("q_squared"), sem("k_squared")
        sums_ready, means_ready, rstds_ready = sem("qk_sums"), sem("qk_means"), sem("qk_rstds")
        q_normed, k_normed = sem("q_normed"), sem("k_normed")
        qT_ready, kT_ready = sem("qT_ready"), sem("kT_ready")
        q_copied, k_copied, v_copied, g_tanhed, sg_ready = (sem("q_copied"), sem("k_copied"), sem("v_copied"),
                                                            sem("bg_tanhed"), sem("sg_ready"))
        q_out, k_out, ks_out, v_out, sg_out = ([sem(f"{n}_out{k}") for k in range(2)]
                                               for n in ("q", "k", "ks", "vb", "sg"))
        g_ready = sem("bg_ready")
        h.tile_done = kT_ready
        block = cx.enter_context(nc.Block())
        PT = TILES // 2 + 1


        def load_x(dma, i, u):
            if isinstance(i, int) and i == 0:
                dma.dma_start(h.xt[u][:], ctx2[u * P:(u + 1) * P, :]).then_inc(h.x_in[u], 16)
            else:
                rows = x2[bass.ds((i - 1) * (GR * GW), GR * GW), :].rearrange("(r h c) d -> h r c d", r=GR, h=2)
                dma.dma_start(h.xt[u][:], rows[u]).then_inc(h.x_in[u], 16)

        def pairs(e, tile):
            for i in (0, 1):
                for u in range(2):
                    tile(i, u, True)
            with e.Fori(2, PT - 1) as i:
                for u in range(2):
                    tile(i, u, True)
            for u in range(2):
                tile(PT - 1, u, u == 0)

        @block.sync
        def _(sp):
            load_x(sp, 0, 0)
            load_x(sp, 0, 1)
            w.load(sp)

            def tile(i, u, more):
                t = 2 * i + u
                latent = not (isinstance(i, int) and i == 0)
                if not (isinstance(i, int) and i == PT - 1):
                    sp.wait_ge(h.normed_ready, t + 1)
                    load_x(sp, i + 1, u)
                n = (i - 1) + u * GN
                sp.wait_ge(v_copied, t + 1)
                if latent:
                    sp.dma_start(v_d[bass.ds(n + 1, 1)][0], v_sb[u][:]).then_inc(v_out[u], 16)
                    sp.wait_ge(sg_ready, t - 1)
                    sp.dma_start(sg_d[bass.ds(n, 1)][0], sg[u][:]).then_inc(sg_out[u], 16)
                    sp.wait_ge(q_copied, t - 1)
                    sp.dma_start(qT_d[bass.ds(n, 1)][0], qT[u][:]).then_inc(q_out[u], 16)
                    sp.wait_ge(k_copied, t + 1)
                    sp.dma_start(kT_d[bass.ds(n + 1, 1)][0], kT[u][:]).then_inc(k_out[u], 16)
                    sp.dma_start(kside_d[:, :, bass.ds(n + 1, 1), :],
                                 kside[u][:].rearrange("p a r c -> p a (r c)")).then_inc(ks_out[u], 16)
                else:
                    sp.dma_start(vctx_d[u * P:(u + 1) * P, :], v_sb[u][:]).then_inc(v_out[u], 16)
                    sp.wait_ge(k_copied, t + 1)
                    sp.dma_start(kctx_d[:, :, u * P:(u + 1) * P], kT[u][:]).then_inc(k_out[u], 16)

            pairs(sp, tile)
            for u in range(2):
                sp.wait_ge(v_out[u], 16 * PT)
                sp.wait_ge(k_out[u], 16 * PT)
                sp.wait_ge(sg_out[u], 16 * (PT - 1))
                sp.wait_ge(q_out[u], 16 * (PT - 1))
                sp.wait_ge(ks_out[u], 16 * (PT - 1))

        @block.gpsimd
        def _(pool):
            nc.gpsimd.memset(h.minus_half[:], -0.5).then_inc(h.half_ready, 1)
            pool.wait_ge(h.half_ready, 1)

            def tile(i, u, more):
                t = 2 * i + u
                if more:
                    h.root(pool, i + (u + 1) // 2, (u + 1) % 2)
                pool.wait_ge(means_ready, t + 1)
                wait(pool, k_normed, t)
                used = slice(H, 2 * H) if isinstance(i, int) and i == 0 else slice(0, 2 * H)
                nc.gpsimd.tensor_tensor(rstd[:, used], meansq[:, used], h.minus_half[:, used],
                                        ALU.pow).then_inc(rstds_ready, 1)

            h.root(pool, 0, 0)
            pairs(pool, tile)

        @block.scalar
        def _(act):
            for n in range(2):
                half = slice(n * DH, (n + 1) * DH)
                act.dma_start(gq[half, 0:1], q_norm_g.rearrange("b d -> d b")).then_inc(gains_in, 16)
                act.dma_start(gk[half, :], k_norm_g.rearrange("b d -> d b")).then_inc(gains_in, 16)
            h.square(act, 0, 0)
            h.modulate(act, 0, 0, a_col[:, 1, :], b_col[:, 1, :])
            w.round_hi(act)
            act.wait_ge(gq_ready, 1)

            def tile(i, u, more):
                t = 2 * i + u
                latent = not (isinstance(i, int) and i == 0)
                n, m = i + (u + 1) // 2, (u + 1) % 2
                if more:
                    h.square(act, n, m)
                if latent:
                    act.wait_ge(q_ready, t - 1)
                    wait(act, sums_ready, t)
                    nc.scalar.activation(squares[:, 0, :], p_q[:], ACT.Square).then_inc(q_squared, 1)
                act.wait_ge(k_ready, t + 1)
                wait(act, sums_ready, t)
                nc.scalar.activation(squares[:, 1, :], p_k[:], ACT.Square).then_inc(k_squared, 1)
                if more:
                    s = 1 if isinstance(n, int) and n == 0 else 0
                    h.modulate(act, n, m, a_col[:, s, :], b_col[:, s, :])
                act.wait_ge(v_ready, t + 1)
                wait(act, v_out[u], 16 * i)
                nc.scalar.activation(v_sb[u][:], p_v[:], ACT.Copy).then_inc(v_copied, 1)
                if latent:
                    act.wait_ge(g_ready, t - 1)
                    wait(act, sg_ready, t - 2)
                    nc.scalar.activation(g_tanh[:], p_g[:], ACT.Tanh, scale=0.5).then_inc(g_tanhed, 1)
                    act.wait_ge(qT_ready, t - 1)
                    wait(act, q_out[u], 16 * (i - 1))
                    nc.scalar.activation(qT[u][:].rearrange("p a c -> p (a c)"), p_qT[:], ACT.Identity,
                                         scale=gq[:, 1:2]).then_inc(q_copied, 1)
                act.wait_ge(kT_ready, t + 1)
                wait(act, k_out[u], 16 * i)
                last = nc.scalar.activation(kT[u][:].rearrange("p a c -> p (a c)"), p_kT[:], ACT.Identity,
                                            scale=gk[:, 0:1])
                if latent:
                    wait(act, ks_out[u], 16 * (i - 1))
                    first = HC - SC if u == 0 else 0
                    near = p_kT[:].rearrange("p (a r c) -> p (a r) c", a=PAIRS, r=GR)[:, :, first:first + SC]
                    last = nc.scalar.activation(kside[u][:].rearrange("p a r c -> p (a r) c"), near, ACT.Identity,
                                                scale=gk[:, 0:1])
                last.then_inc(k_copied, 1)

            pairs(act, tile)

        @block.tensor
        def _(pe):
            h.transpose(pe, 0, 0)
            pe.wait_ge(w.lo_done, w.CHUNKS)

            def tile(i, u, more):
                t = 2 * i + u
                latent = not (isinstance(i, int) and i == 0)
                pe.wait_ge(h.split_ready, t + 1)
                if latent:
                    wait(pe, q_normed, t - 2)
                    h.products(u, p_q[:], w, Q).then_inc(q_ready, 1)
                wait(pe, k_normed, t)
                h.products(u, p_k[:], w, K).then_inc(k_ready, 1)
                if more:
                    h.transpose(pe, i + (u + 1) // 2, (u + 1) % 2)
                wait(pe, v_copied, t)
                if latent:
                    h.products(u, p_v[:], w, V).then_inc(v_ready, 1)
                    wait(pe, sg_ready, t - 2)
                    h.products(u, p_g[:], w, G).then_inc(g_ready, 1)
                else:
                    h.products(u, p_v[:], w, V).then_inc(v_ready, 1)
                if latent:
                    pe.wait_ge(q_normed, t - 1)
                    wait(pe, q_copied, t - 2)
                    for a in range(PAIRS):
                        last = nc.tensor.transpose(p_qT[:, a * P:(a + 1) * P], qkn[:, 0, a * P:(a + 1) * P], ident[:])
                    last.then_inc(qT_ready, 1)
                pe.wait_ge(k_normed, t + 1)
                wait(pe, k_copied, t)
                for a in range(PAIRS):
                    last = nc.tensor.transpose(p_kT[:, a * P:(a + 1) * P], qkn[:, 1, a * P:(a + 1) * P], ident[:])
                last.then_inc(kT_ready, 1)

            pairs(pe, tile)

        @block.vector
        def _(dve):
            h.mean(dve, 0, 0)
            h.normalise(dve, 0, 0)
            h.split(dve, 0, 0)
            dve.wait_ge(gains_in, 64)
            nc.vector.tensor_scalar(gq[:, 1:2], gq[:, 0:1], DH ** -0.5, None, ALU.mult).then_inc(gq_ready, 1)
            w.take_lo(dve)

            def tile(i, u, more):
                t = 2 * i + u
                latent = not (isinstance(i, int) and i == 0)
                n, m = i + (u + 1) // 2, (u + 1) % 2
                if more:
                    h.mean(dve, n, m)
                    h.normalise(dve, n, m)
                wait(dve, means_ready, t)
                if latent:
                    dve.wait_ge(q_squared, t - 1)
                    nc.vector.tensor_reduce(sumsq[:, 0:H], squares[:, 0, :].rearrange("p (h d) -> p h d", h=H),
                                            AX.X, ALU.add)
                dve.wait_ge(k_squared, t + 1)
                nc.vector.tensor_reduce(sumsq[:, H:2 * H], squares[:, 1, :].rearrange("p (h d) -> p h d", h=H),
                                        AX.X, ALU.add).then_inc(sums_ready, 1)
                dve.wait_ge(sums_ready, t + 1)
                wait(dve, rstds_ready, t)
                used = slice(0, 2 * H) if latent else slice(H, 2 * H)
                nc.vector.tensor_scalar(meansq[:, used], sumsq[:, used], 1.0 / DH, EPS, ALU.mult,
                                        ALU.add).then_inc(means_ready, 1)
                if more:
                    h.split(dve, n, m)
                dve.wait_ge(rstds_ready, t + 1)
                if latent:
                    wait(dve, qT_ready, t - 2)
                    nc.vector.tensor_tensor(qkn[:, 0, :].rearrange("p (h d) -> p h d", h=H),
                                            p_q[:].rearrange("p (h d) -> p h d", h=H),
                                            rstd[:, 0:H].unsqueeze(2).to_broadcast([P, H, DH]),
                                            ALU.mult).then_inc(q_normed, 1)
                wait(dve, kT_ready, t)
                nc.vector.tensor_tensor(qkn[:, 1, :].rearrange("p (h d) -> p h d", h=H),
                                        p_k[:].rearrange("p (h d) -> p h d", h=H),
                                        rstd[:, H:2 * H].unsqueeze(2).to_broadcast([P, H, DH]),
                                        ALU.mult).then_inc(k_normed, 1)
                if latent:
                    dve.wait_ge(g_tanhed, t - 1)
                    wait(dve, sg_out[u], 16 * (i - 1))
                    nc.vector.scalar_tensor_tensor(out=sg[u][:], in0=g_tanh[:], scalar=1.0, in1=p_g[:],
                                                   op0=ALU.add, op1=ALU.mult).then_inc(sg_ready, 1)

            pairs(dve, tile)


def attend(nc, ident, qT_d, kT_d, v_d, kside_d, sg_d, kctx_d, vctx_d, bias_d, mask_d, outb_d):
    STEPS, TURNS = TILES, TILES // RING
    T_LAG, PV_LAG, O_LAG = 2, 5, 7
    with nc.cleanup_on_exit(), ExitStack() as cx:
        sb = lambda n, s, d=F32: cx.enter_context(nc.sbuf_tensor("att_" + n, s, d))
        ps = lambda n, s: cx.enter_context(nc.psum_tensor("att_" + n, s, F32))
        sem = lambda n: nc.alloc_semaphore("att_" + n)
        q_raw = [sb(f"q_raw{k}", [P, PAIRS, 2, P]) for k in range(2)]
        q_hi = [sb(f"q_hi{k}", [P, H, P], F32R) for k in range(2)]
        q_lo = [sb(f"q_lo{k}", [P, H, P], F32R) for k in range(2)]
        k_raw = sb("k_raw", [P, PAIRS, 2, P])
        k_hi = sb("k_hi", [P, H, P], F32R)
        k_ring = sb("k_ring", [P, H, MIRROR * P], F32R)
        s_raw = sb("s_raw", [P, PAIRS, 2, SIDE])
        k_side = [sb(f"k_side{k}", [P, H, SIDECTX], F32R) for k in range(2)]
        v_ring = sb("v_ring", [P, RING, DA])
        v_side = [sb(f"v_side{k}", [P, DA]) for k in range(2)]
        v_ctx = sb("v_ctx", [P, 2, DA])
        sg = [sb(f"sgl{k}", [P, DA]) for k in range(2)]
        raw_bias = sb("raw_bias", [P, 2, H, 3 * GR, HC + SC])
        mask = sb("mask", [P, 2, 3, LAT])
        bias = sb("bias", [P, H, KEYS])
        scores = [sb(f"scores{k}", [P, KEYS]) for k in range(2)]
        probs = [sb(f"probs{k}", [P, KCH * P]) for k in range(2)]
        max1, max2, negmax = sb("max1", [P, 2]), sb("max2", [P, 2]), sb("negmax", [P, 2])
        den, rden = sb("den", [P, 2, H]), sb("rden", [P, H])
        pT = sb("pT", [P, 4, KCH * P])
        c_raw = pT[:].rearrange("p a b -> p (a b)")[:, 0:H * CTX].rearrange("p (a b c) -> p a b c", a=PAIRS, b=2)
        oT = [sb(f"oT{k}", [P, P]) for k in range(2)]
        o_div = sb("o_div", [P, DA])
        outb = [sb(f"outb{k}", [P, DA]) for k in range(2)]
        p_main = [ps(f"p_main{k}", [P, 512]) for k in range(2)]
        p_side = [ps(f"p_side{k}", [P, 512]) for k in range(2)]
        p_pT4, p_pT2 = ps("p_pT4", [P, 4 * P]), ps("p_pT2", [P, 4 * P])
        p_oT, p_o = ps("p_oT", [P, PAIRS * P]), ps("p_o", [P, DA])

        q_in, vs_in, sg_in = ([sem(f"{n}_in{k}") for k in range(2)] for n in ("q", "vs", "sgl"))
        k_in, side_in = sem("k_in"), sem("side_in")
        v_in = [sem(f"v_in{k}") for k in range(RING)]
        kctx_in, vctx_in, tables_in = sem("kctx_in"), sem("vctx_in"), sem("tables_in")
        consts = sem("attend_consts")
        ctx_hi_ready, ctx_lo_ready, ctx_split = sem("ctx_hi_ready"), sem("ctx_lo_ready"), sem("ctx_split")
        q_hi_ready, q_split = sem("q_hi_ready"), sem("q_split")
        k_hi_ready, k_lo_ready, k_stacked, k_split = (sem("k_hi_ready"), sem("k_lo_ready"), sem("k_stacked"),
                                                      sem("k_split"))
        s_hi_ready, s_lo_ready, s_split = sem("s_hi_ready"), sem("s_lo_ready"), sem("s_split")
        bias_ready = [sem(f"bias_ready{k}") for k in range(H)]
        bias_made = sem("bias_made")
        main_begun, side_begun, copy_begun = sem("main_begun"), sem("side_begun"), sem("copy_begun")
        scored, main_added, added, negated, exped = (sem("scored"), sem("main_added"), sem("added"),
                                                     sem("negated"), sem("exped"))
        pT_ready, pT4_copied, pT2_copied = sem("pT_ready"), sem("pT4_copied"), sem("pT2_copied")
        oT_ready, oT_copied, o_ready = sem("oT_ready"), sem("oT_copied"), sem("o_ready")
        recip_ready, divided, outb_ready = sem("recip_ready"), sem("divided"), sem("outb_ready")
        outb_out = [sem(f"outb_out{k}") for k in range(2)]
        block = cx.enter_context(nc.Block())

        def back(i, u, n, lag):
            at = H * u + n - lag
            if at < 0:
                i, at = i - 1, at + H * RING
            return None if isinstance(i, int) and i < 0 else (i, at // H, at % H)

        def run(e, slot):
            for u in range(RING):
                for n in range(H):
                    slot(0, u, n, True)
            with e.Fori(1, TURNS) as i:
                for u in range(RING):
                    for n in range(H):
                        slot(i, u, n, True)
            for n in range(O_LAG + 1):
                slot(TURNS, 0, n, False)

        def twice(dma, dst, src, done):
            for half in range(2):
                for head in range(2):
                    dma.dma_start(dst[half * DH:(half + 1) * DH, :, head, :],
                                  src[head * DH:(head + 1) * DH]).then_inc(done, 16)

        @block.sync
        def _(sp):
            def load_k(seq):
                wait(sp, k_split, seq)
                twice(sp, k_raw, kT_d[bass.ds(seq + 1, 1)][0], k_in)

            def load_q(i, u, half):
                s, b = RING * i + u, u % 2
                wait(sp, q_split, s - 1)
                twice(sp, q_raw[b], qT_d[bass.ds(s, 1)][0], q_in[b])
                wait(sp, s_split, s)
                n = s + GN if half == 0 else s - GN
                twice(sp, s_raw, kside_d[:, :, bass.ds(n, 3), :].rearrange("p a t c -> p a (t c)"), side_in)
                load_k(s + 1)

            def load_v(i, u, half):
                s, b = RING * i + u, u % 2
                wait(sp, oT_ready, PAIRS * (s - 1))
                sp.dma_start(v_ring[:, (u + 1) % RING, :],
                             v_d[bass.ds(s + 2, 1)][0]).then_inc(v_in[(u + 1) % RING], 16)
                n = s + GN if half == 0 else s - GN
                first = 0 if half == 0 else HC - SC
                for j in range(3):
                    rows = v_d[bass.ds(n + j, 1)][0].rearrange("(r c) d -> r c d", r=GR)[:, first:first + SC, :]
                    sp.dma_start(v_side[b][j * GR * SC:(j + 1) * GR * SC, :], rows).then_inc(vs_in[b], 16)
                wait(sp, outb_ready, s - 1)
                sp.dma_start(sg[b][:], sg_d[bass.ds(s, 1)][0]).then_inc(sg_in[b], 16)

            twice(sp, c_raw, kctx_d, kctx_in)
            load_k(0)
            sp.dma_start(mask[:], mask_d).then_inc(tables_in, 16)
            for half in range(2):
                sp.dma_start(raw_bias[:, half].rearrange("p n r c -> p n (r c)"),
                             bias_d[half, :, :, 0:3 * GR, :].rearrange("p n r c -> p n (r c)")).then_inc(tables_in, 16)
            for b in range(2):
                sp.dma_start(v_side[b][SIDE:P, :], vctx_d[0:P - SIDE, :]).then_inc(vctx_in, 16)
            sp.dma_start(v_ctx[:, 0, :], vctx_d[P - SIDE:2 * P - SIDE, :]).then_inc(vctx_in, 16)
            sp.wait_ge(consts, 6)
            sp.dma_start(v_ctx[0:SIDE, 1, :], vctx_d[2 * P - SIDE:CTX, :]).then_inc(vctx_in, 16)
            sp.dma_start(v_ring[:, 0, :], v_d[1]).then_inc(v_in[0], 16)
            HT = TURNS // 2
            for half in range(2):
                def turn(i, first, half=half):
                    for u in range(RING):
                        load_q(i, u, half)
                        if u > 0:
                            load_v(i, u - 1, half)
                        elif not (first and half == 0):
                            load_v(i - 1, RING - 1, 0 if first else half)

                turn(half * HT, True)
                with sp.Fori(half * HT + 1, (half + 1) * HT) as i:
                    turn(i, False)
            load_v(TURNS - 1, RING - 1, 1)

        @block.gpsimd
        def _(pool):
            nc.gpsimd.memset(k_ring[:].bitcast(F32), 0.0).then_inc(consts, 1)
            nc.gpsimd.memset(v_ctx[:, 1, :], 0.0).then_inc(consts, 1)
            nc.gpsimd.memset(v_ring[:, RING - 1, :], 0.0).then_inc(consts, 1)
            nc.gpsimd.memset(bias[:, :, LAT:KEYS], 0.0).then_inc(consts, 1)
            for b in range(2):
                nc.gpsimd.memset(probs[b][:, KEYS:KCH * P], 0.0).then_inc(consts, 1)

            def merged(raw):
                return raw.rearrange("p a b c -> p (a b) c")

            def split_stacked(raw, width, dst, rounded, count, lo_done, done):
                hi = k_hi[:, :, 0:width]
                pool.sem_inc(copy_begun, 1)
                nc.gpsimd.tensor_copy(hi, merged(raw)).then_inc(rounded, 1)
                pool.wait_ge(rounded, count)
                nc.gpsimd.tensor_tensor(dst, merged(raw), hi.bitcast(F32), ALU.subtract).then_inc(lo_done, 1)
                pool.wait_ge(lo_done, count)
                pool.sem_inc(copy_begun, 1)
                nc.gpsimd.tensor_copy(dst[0:DH], hi[0:DH]).then_inc(done, 1)

            def split_k(seq, i, slot):
                pool.wait_ge(k_in, 64 * (seq + 1))
                wait(pool, scored, H * (seq - 2))
                mirrored = slot < MIRROR - RING
                at = k_ring[:, :, slot * P:(slot + 1) * P]
                split_stacked(k_raw, P, at, k_hi_ready, seq + 1, k_lo_ready, k_stacked if mirrored else k_split)
                if mirrored:
                    pool.wait_ge(k_stacked, 2 * i + slot + 1)
                    m = (RING + slot) * P
                    pool.sem_inc(copy_begun, 1)
                    nc.gpsimd.tensor_copy(k_ring[:, :, m:m + P], at).then_inc(k_split, 1)
                pool.wait_ge(k_split, seq + 1)

            def step(i, u):
                s, b = RING * i + u, u % 2
                pool.wait_ge(q_in[b], 64 * (2 * i + u // 2 + 1))
                wait(pool, scored, H * (s - 1))
                pool.sem_inc(copy_begun, 1)
                nc.gpsimd.tensor_copy(q_hi[b][:], merged(q_raw[b])).then_inc(q_hi_ready, 1)
                pool.wait_ge(q_hi_ready, s + 1)
                nc.gpsimd.tensor_tensor(q_lo[b][:], merged(q_raw[b]), q_hi[b][:].bitcast(F32),
                                        ALU.subtract).then_inc(q_split, 1)
                pool.wait_ge(q_split, s + 1)
                pool.wait_ge(side_in, 64 * (s + 1))
                split_stacked(s_raw, SIDE, k_side[b][:, :, 0:SIDE], s_hi_ready, s + 1, s_lo_ready, s_split)
                pool.wait_ge(s_split, s + 1)
                split_k(s + 1, i + (u + 1) // RING, (u + 1) % RING)

            made = [0]

            def make_bias(s, until):
                half, edge = s // GN, {0: 0, 1: 1, GN - 1: 2}[s % GN]
                for n in range(H):
                    wait(pool, added, H * (s - 1) + n + 1 if s else 0)
                    for at, width, first in ((0, HC, half * SC), (MAIN, SC, 0 if half else HC)):
                        part = slice(at, at + 3 * GR * width)
                        last = nc.gpsimd.tensor_tensor(
                            bias[:, n, part].rearrange("p (r c) -> p r c", c=width),
                            raw_bias[:, half, n, :, first:first + width],
                            mask[:, half, edge, part].rearrange("p (r c) -> p r c", c=width), ALU.add)
                    last.then_inc(bias_made, 1)
                    made[0] += 1
                    pool.wait_ge(bias_made, made[0])
                    pool.sem_inc(bias_ready[n], until - s)

            pool.wait_ge(consts, 6)
            pool.wait_ge(kctx_in, 64)
            for j in range(2):
                split_stacked(c_raw[:, :, :, j * P:(j + 1) * P], P,
                              k_side[0][:, :, SIDE + j * P:SIDE + (j + 1) * P], ctx_hi_ready, j + 1, ctx_lo_ready,
                              ctx_split)
                pool.wait_ge(ctx_split, j + 1)
            nc.gpsimd.tensor_copy(k_side[1][:, :, SIDE:SIDECTX], k_side[0][:, :, SIDE:SIDECTX]).then_inc(ctx_split, 1)
            pool.wait_ge(ctx_split, 3)
            split_k(0, 0, 0)
            HT = TURNS // 2
            for half in range(2):
                base = half * GN
                for u in range(RING):
                    step(half * HT, u)
                    if half == 0 and u == 0:
                        pool.wait_ge(tables_in, 48)
                    if u == 0:
                        make_bias(base, base + 1)
                    if u == 1:
                        make_bias(base + 1, base + GN - 1)
                with pool.Fori(half * HT + 1, (half + 1) * HT - 1) as i:
                    for u in range(RING):
                        step(i, u)
                for u in range(RING):
                    step((half + 1) * HT - 1, u)
                make_bias(base + GN - 1, base + GN)

        @block.tensor
        def _(pe):
            pe.wait_ge(ctx_split, 3)

            def score(i, u, n):
                s, b = RING * i + u, u % 2
                t = H * s + n
                if n == 0:
                    pe.wait_ge(q_split, s + 1)
                    pe.wait_ge(s_split, s + 1)
                    pe.wait_ge(k_split, s + 2)
                wait(pe, added, t - 1)
                first = ((u + RING - 1) % RING) * P
                main = k_ring[:, n, first:first + MAIN]
                side = k_side[b][:, n, :]
                m = n % 2
                nc.tensor.matmul(p_main[m][:, 0:MAIN], q_hi[b][:, n, :], main, start=True, stop=False)
                nc.tensor.matmul(p_main[m][:, 0:MAIN], q_lo[b][:, n, :], main, start=False, stop=True)
                nc.tensor.matmul(p_side[m][:, 0:SIDECTX], q_hi[b][:, n, :], side, start=True, stop=False)
                nc.tensor.matmul(p_side[m][:, 0:SIDECTX], q_lo[b][:, n, :], side, start=False,
                                 stop=True).then_inc(scored, 1)

            def transpose(i, u, n):
                t = H * (RING * i + u) + n
                pe.wait_ge(exped, t + 1)
                wait(pe, pT4_copied, t)
                wait(pe, pT2_copied, t)
                for j in range(KCH):
                    bank, at = (p_pT4, j) if j < 4 else (p_pT2, j - 4)
                    last = nc.tensor.transpose(bank[:, at * P:(at + 1) * P], probs[n % 2][:, j * P:(j + 1) * P],
                                               ident[:])
                last.then_inc(pT_ready, 1)

            def values(i, u, a):
                s, b = RING * i + u, u % 2
                t = H * s + 2 * a
                if a == 0:
                    pe.wait_ge(v_in[(u + 1) % RING], 16 * (i + (u + 1) // RING + 1))
                    pe.wait_ge(vs_in[b], 48 * (2 * i + u // 2 + 1))
                    if isinstance(i, int) and i == 0 and u == 0:
                        pe.wait_ge(v_in[0], 16)
                        pe.wait_ge(vctx_in, 64)
                pe.wait_ge(pT4_copied, t + 2)
                pe.wait_ge(pT2_copied, t + 2)
                wait(pe, oT_copied, PAIRS * s + a)
                for j in range(KCH):
                    v = (v_ring[:, (u + RING - 1 + j) % RING, :] if j < 3 else
                         v_side[b][:] if j == 3 else v_ctx[:, j - 4, :])
                    for k in range(2):
                        n = 2 * a + k
                        last = nc.tensor.matmul(p_oT[k * DH:(k + 1) * DH, a * P:(a + 1) * P],
                                                v[:, n * DH:(n + 1) * DH], pT[:, n % 4, j * P:(j + 1) * P],
                                                start=(j == 0), stop=(j == KCH - 1))
                last.then_inc(oT_ready, 1)

            def untranspose(i, u, a):
                s = RING * i + u
                pe.wait_ge(oT_copied, PAIRS * s + a + 1)
                if a == 0:
                    wait(pe, divided, s)
                nc.tensor.transpose(p_o[:, a * P:(a + 1) * P], oT[a % 2][:], ident[:]).then_inc(o_ready, 1)

            def slot(i, u, n, live):
                if live:
                    score(i, u, n)
                t2 = back(i, u, n, T_LAG)
                if t2 and (live or n < T_LAG):
                    transpose(*t2)
                if n % 2:
                    pv, o = back(i, u, n, PV_LAG), back(i, u, n, O_LAG)
                    if pv and (live or n < PV_LAG):
                        values(pv[0], pv[1], pv[2] // 2)
                    if o and (live or n < O_LAG):
                        untranspose(o[0], o[1], o[2] // 2)

            run(pe, slot)

        @block.scalar
        def _(act):
            def copy_pT(i, u, n):
                t = H * (RING * i + u) + n
                act.wait_ge(pT_ready, t + 1)
                wait(act, oT_ready, PAIRS * (RING * i + u) + n // 2 - 1)
                nc.scalar.activation(pT[:, n % 4, 0:4 * P], p_pT4[:], ACT.Copy).then_inc(pT4_copied, 1)

            def softmax(i, u, n):
                s, b = RING * i + u, n % 2
                t = H * s + n
                act.wait_ge(negated, t + 1)
                wait(act, pT_ready, t - 1)
                if n == 0:
                    wait(act, divided, s - 1)
                if isinstance(i, int) and i == 0 and u == 0 and n == 0:
                    act.wait_ge(consts, 6)
                nc.scalar.activation(probs[b][:, 0:KEYS], scores[b][:], ACT.Exp, bias=negmax[:, b:b + 1],
                                     accum_out=den[:, u % 2, n:n + 1]).then_inc(exped, 1)

            def copy_oT(i, u, a):
                m = PAIRS * (RING * i + u) + a
                act.wait_ge(oT_ready, m + 1)
                wait(act, o_ready, m - 1)
                nc.scalar.activation(oT[a % 2][:], p_oT[:, a * P:(a + 1) * P], ACT.Copy).then_inc(oT_copied, 1)

            def store(i, u):
                s, b = RING * i + u, u % 2
                act.wait_ge(outb_ready, s + 1)
                act.dma_start(outb_d[bass.ds(s, 1)][0], outb[b][:]).then_inc(outb_out[b], 16)

            def slot(i, u, n, live):
                t2 = back(i, u, n, T_LAG)
                if t2 and (live or n < T_LAG):
                    copy_pT(*t2)
                if live:
                    softmax(i, u, n)
                pv, o = back(i, u, n, PV_LAG), back(i, u, n, O_LAG)
                if n % 2 and pv and (live or n < PV_LAG):
                    copy_oT(pv[0], pv[1], pv[2] // 2)
                if n == H - 1 and back(i, u, n, H):
                    store(*back(i, u, n, H)[0:2])

            run(act, slot)
            for b in range(2):
                act.wait_ge(outb_out[b], 16 * STEPS // 2)

        @block.vector
        def _(dve):
            def add_bias(i, u, n):
                s, b = RING * i + u, n % 2
                t = H * s + n
                dve.wait_ge(scored, t + 1)
                dve.wait_ge(bias_ready[n], s + 1)
                wait(dve, exped, t - 1)
                dve.sem_inc(main_begun, 1)
                nc.vector.tensor_tensor_reduce(
                    out=scores[b][:, 0:MAIN], in0=p_main[b][:, 0:MAIN], in1=bias[:, n, 0:MAIN], scale=1.0,
                    scalar=LOWEST, op0=ALU.add, op1=ALU.max, accum_out=max1[:, b:b + 1]).then_inc(main_added, 1)
                dve.wait_ge(main_added, t + 1)
                if isinstance(i, int) and t == 0:
                    dve.wait_ge(consts, 6)
                dve.sem_inc(side_begun, 1)
                nc.vector.tensor_tensor_reduce(
                    out=scores[b][:, MAIN:KEYS], in0=p_side[b][:, 0:SIDECTX], in1=bias[:, n, MAIN:KEYS], scale=1.0,
                    scalar=max1[:, b:b + 1], op0=ALU.add, op1=ALU.max, accum_out=max2[:, b:b + 1]).then_inc(added, 1)
                dve.wait_ge(added, t + 1)
                nc.vector.tensor_scalar(negmax[:, b:b + 1], max2[:, b:b + 1], -1.0, None,
                                        ALU.mult).then_inc(negated, 1)

            def copy_pT(i, u, n):
                t = H * (RING * i + u) + n
                dve.wait_ge(pT_ready, t + 1)
                wait(dve, oT_ready, PAIRS * (RING * i + u) + n // 2 - 1)
                nc.vector.tensor_copy(pT[:, n % 4, 4 * P:KCH * P], p_pT2[:, 0:2 * P]).then_inc(pT2_copied, 1)

            def finish(i, u):
                s, b = RING * i + u, u % 2
                dve.wait_ge(exped, H * (s + 1))
                nc.vector.reciprocal(rden[:], den[:, b, :]).then_inc(recip_ready, 1)
                dve.wait_ge(recip_ready, s + 1)
                dve.wait_ge(o_ready, PAIRS * (s + 1))
                nc.vector.tensor_tensor(o_div[:].rearrange("p (h d) -> p h d", h=H),
                                        p_o[:].rearrange("p (h d) -> p h d", h=H),
                                        rden[:].unsqueeze(2).to_broadcast([P, H, DH]), ALU.mult).then_inc(divided, 1)
                dve.wait_ge(divided, s + 1)
                dve.wait_ge(sg_in[b], 16 * (2 * i + u // 2 + 1))
                wait(dve, outb_out[b], 16 * (2 * i + u // 2))
                nc.vector.scalar_tensor_tensor(out=outb[b][:], in0=sg[b][:], scalar=0.5, in1=o_div[:],
                                               op0=ALU.mult, op1=ALU.mult).then_inc(outb_ready, 1)

            def slot(i, u, n, live):
                if live:
                    add_bias(i, u, n)
                t2 = back(i, u, n, T_LAG)
                if t2 and (live or n < T_LAG):
                    copy_pT(*t2)
                if n == O_LAG - 1 and back(i, u, n, H):
                    finish(*back(i, u, n, H)[0:2])

            run(dve, slot)


def combine(nc, ident, gate_bc, x2, w_out, outa_d, outb_d, out2):
    with nc.cleanup_on_exit(), ExitStack() as cx:
        sb = lambda n, s, d=F32: cx.enter_context(nc.sbuf_tensor("com_" + n, s, d))
        ps = lambda n, s: cx.enter_context(nc.psum_tensor("com_" + n, s, F32))
        sem = lambda n: nc.alloc_semaphore("com_" + n)
        w = SplitWeights(nc, cx, "wo", w_out[0], D)
        mix = [sb(f"mix{k}", [P, D]) for k in range(2)]
        xt = [sb(f"xr{k}", [P, D]) for k in range(2)]
        hi = [sb(f"mixT_hi{k}", [P, KT, P], F32R) for k in range(2)]
        lo = [sb(f"mixT_lo{k}", [P, KT, P], F32R) for k in range(2)]
        gated = sb("out_gated", [P, D])
        result = [sb(f"result{k}", [P, D]) for k in range(2)]
        p_t = [ps(f"p_mixT{k}", [P, KT, P]) for k in range(2)]
        p_o = [ps(f"p_out{k}", [P, 512]) for k in range(4)]
        mix_in = [sem(f"mix_in{k}") for k in range(2)]
        x_in = [sem(f"xr_in{k}") for k in range(2)]
        transposed, hi_ready, split_ready = sem("mix_transposed"), sem("mix_hi"), sem("mix_split")
        product = sem("product")
        gated_ready, result_ready = sem("out_gated_ready"), sem("result_ready")
        out_out = [sem(f"out_out{k}") for k in range(2)]
        block = cx.enter_context(nc.Block())
        PT = TILES // 2

        @block.sync
        def _(sp):
            def load_mix(i, u):
                sp.dma_start(mix[u][:, 0:DA], outa_d[bass.ds((2 * i + u) * P, P), :]).then_inc(mix_in[u], 16)
                for half in range(2):
                    for r in range(2):
                        src = outb_d[bass.ds(i + half * GN, 1)][0]
                        row = (2 * u + r) * HC
                        sp.dma_start(mix[u][r * GW + half * HC:r * GW + (half + 1) * HC, DA:D],
                                     src[row:row + HC, :]).then_inc(mix_in[u], 16)

            def load_x(i, u):
                sp.dma_start(xt[u][:], x2[bass.ds((2 * i + u) * P, P), :]).then_inc(x_in[u], 16)

            for u in range(2):
                load_mix(0, u)
            w.load(sp)
            for u in range(2):
                load_x(0, u)

            def tile(i, u, more):
                t = 2 * i + u
                if more:
                    sp.wait_ge(transposed, t + 1)
                    load_mix(i + 1, u)
                sp.wait_ge(result_ready, t + 1)
                sp.dma_start(out2[bass.ds(t * P, P), :], result[u][:]).then_inc(out_out[u], 16)
                if more:
                    load_x(i + 1, u)

            with sp.Fori(0, PT - 1) as i:
                for u in range(2):
                    tile(i, u, True)
            for u in range(2):
                tile(PT - 1, u, False)
            for u in range(2):
                sp.wait_ge(out_out[u], 16 * PT)

        def tiles(e, tile):
            for u in range(2):
                tile(0, u, True)
            with e.Fori(1, PT - 1) as i:
                for u in range(2):
                    tile(i, u, True)
            for u in range(2):
                tile(PT - 1, u, u == 0)

        @block.scalar
        def _(act):
            def round_hi(i, u):
                t = 2 * i + u
                act.wait_ge(transposed, t + 1)
                wait(act, product, 2 * (t - 1))
                nc.scalar.activation(hi[u][:], p_t[u][:], ACT.Copy).then_inc(hi_ready, 1)

            round_hi(0, 0)
            w.round_hi(act)

            def tile(i, u, more):
                if more:
                    round_hi(i + (u + 1) // 2, (u + 1) % 2)

            tiles(act, tile)

        @block.tensor
        def _(pe):
            def transpose(i, u):
                t = 2 * i + u
                pe.wait_ge(mix_in[u], 80 * (i + 1))
                wait(pe, split_ready, t - 1)
                for k in range(KT):
                    last = nc.tensor.transpose(p_t[u][:, k, :], mix[u][:, k * P:(k + 1) * P], ident[:])
                last.then_inc(transposed, 1)

            transpose(0, 0)
            pe.wait_ge(w.lo_done, w.CHUNKS)

            def tile(i, u, more):
                t = 2 * i + u
                pe.wait_ge(split_ready, t + 1)
                for n in range(2):
                    bank, c = p_o[2 * u + n], slice(n * 512, (n + 1) * 512)
                    wait(pe, gated_ready, 2 * (t - 2) + n + 1)
                    for k in range(KT):
                        nc.tensor.matmul(bank[:], hi[u][:, k, :], w.hi[:, k, c], start=(k == 0), stop=False)
                        nc.tensor.matmul(bank[:], hi[u][:, k, :], w.lo[:, k, c], start=False, stop=False)
                        last = nc.tensor.matmul(bank[:], lo[u][:, k, :], w.hi[:, k, c], start=False,
                                                stop=(k == KT - 1))
                    last.then_inc(product, 1)
                    if n == 0 and more:
                        transpose(i + (u + 1) // 2, (u + 1) % 2)

            tiles(pe, tile)

        @block.vector
        def _(dve):
            def take_lo(i, u):
                t = 2 * i + u
                dve.wait_ge(hi_ready, t + 1)
                nc.vector.tensor_tensor(lo[u][:], p_t[u][:], hi[u][:].bitcast(F32),
                                        ALU.subtract).then_inc(split_ready, 1)

            take_lo(0, 0)
            w.take_lo(dve)

            def tile(i, u, more):
                t = 2 * i + u
                if more:
                    take_lo(i + (u + 1) // 2, (u + 1) % 2)
                wait(dve, result_ready, t)
                for n in range(2):
                    c = slice(n * 512, (n + 1) * 512)
                    dve.wait_ge(product, 2 * t + n + 1)
                    nc.vector.tensor_tensor(gated[:, c], p_o[2 * u + n][:], gate_bc[:, c],
                                            ALU.mult).then_inc(gated_ready, 1)
                dve.wait_ge(gated_ready, 2 * t + 2)
                dve.wait_ge(x_in[u], 16 * (i + 1))
                wait(dve, out_out[u], 16 * i)
                nc.vector.tensor_tensor(result[u][:], gated[:], xt[u][:], ALU.add).then_inc(result_ready, 1)

            tiles(dve, tile)


_INS = ["x", "c", "ctx", "c_ctx", "w_ada", "b_ada", "norm_g", "w_in", "sgu_norm_g", "w_spatial", "b_spatial",
        "q_norm_g", "k_norm_g", "rpb", "w_out"]


def kernel(**inputs):
    import numpy as np
    from concourse import bacc
    from concourse.bass_utils import run_bass_kernel_spmd

    nc = bacc.Bacc("TRN2", target_bir_lowering=False, num_devices=1)
    arrays, args = {}, []
    for name in _INS:
        a = np.ascontiguousarray(inputs[name])
        arrays[f"in_{name}"] = a
        args.append(nc.dram_tensor(f"in_{name}", a.shape, mybir.dt.from_np(a.dtype), kind="ExternalInput").ap())
    args.append(nc.dram_tensor("out_x", inputs["x"].shape, F32, kind="ExternalOutput").ap())
    build(nc, *args)
    r = run_bass_kernel_spmd(nc, [arrays], core_ids=[0])
    return r.results[0]["out_x"]
```

```python
import concourse.bass as bass
from concourse import mybir
from contextlib import ExitStack

F32 = mybir.dt.float32
F32R = mybir.dt.float32r
ACT = mybir.ActivationFunctionType
ALU = mybir.AluOpType
AX = mybir.AxisListType

P = 128
D = 1024
KT = D // P
L = 4096
CTX = 256
DA = 512
GROUPS = 4
H = 8
DH = 64
PAIRS = H // 2
GW = 64
GR = 4
HC = 32
GN = L // (GR * GW)
TILES = L // P
WR, WC = 8, 16
RPR, RPC = 2 * WR - 1, 2 * WC - 1
SC = 8
MAIN = 3 * P
SIDE = 3 * GR * SC
LAT = MAIN + SIDE
KEYS = LAT + CTX
SIDECTX = SIDE + CTX
KCH = 6
RING = 4
MIRROR = RING + 2
EPS = 1e-6
MASKED = 1e30
HIGHEST = 3.0e38
PAD, PAD_END = 64, 192
MODS = 3 * D


def wait(e, sem, count):
    if not (isinstance(count, int) and count <= 0):
        e.wait_ge(sem, count)


def build(nc, x, c, ctx_in, c_ctx, w_ada, b_ada, norm_g, w_in, sgu_norm_g, w_spatial, b_spatial,
          q_norm_g, k_norm_g, rpb, w_out, out):
    x2, ctx2, out2 = x[0], ctx_in[0], out[0]
    with ExitStack() as top:
        def dram(name, shape, dt=F32):
            return nc.dram_tensor(name, shape, dt, kind="Internal").ap()

        outa_d = dram("outa_d", [L, DA])
        outb_d = dram("outb_d", [TILES, P, DA])
        kT_d = dram("kT_d", [TILES + 2, 2, DH, H, P], F32R)
        v_d = dram("v_d", [TILES + 2, P, DA])
        kside_d = dram("kside_d", [2, DH, H, TILES + 2, GR * SC], F32R)
        qT_d = dram("qT_d", [TILES, DH, 2, H, P], F32R)
        sg_d = dram("sg_d", [TILES, P, DA])
        kctx_d = dram("kctx_d", [2, DH, H, CTX], F32R)
        vctx_d = dram("vctx_d", [CTX, DA])
        rpbpad_d = dram("rpbpad_d", [1, PAD + H * RPR * RPC + PAD_END])
        bias_d = dram("bias_d", [2, P, H, RPR, HC + SC])
        mask_d = dram("mask_d", [P, 2, 3, LAT])

        def sbt(name, shape, dt=F32):
            return top.enter_context(nc.sbuf_tensor(name, shape, dt))

        ident = sbt("ident", [P, P])
        a_col = sbt("a_col", [P, 2, KT])
        b_col = sbt("b_col", [P, 2, KT])
        gate_bc = sbt("gate_bc", [P, D])

        modulate(nc, ident, a_col, b_col, gate_bc, c, c_ctx, w_ada, b_ada, norm_g, rpb,
                 rpbpad_d, mask_d, kT_d, v_d, kside_d)
        gating(nc, ident, a_col, b_col, x2, w_in, sgu_norm_g, w_spatial, b_spatial, outa_d,
               rpbpad_d, bias_d)
        project(nc, ident, a_col, b_col, x2, ctx2, w_in, q_norm_g, k_norm_g,
                qT_d, kT_d, v_d, kside_d, sg_d, kctx_d, vctx_d)
        attend(nc, ident, qT_d, kT_d, v_d, kside_d, sg_d, kctx_d, vctx_d, bias_d, mask_d, outb_d)
        combine(nc, ident, gate_bc, x2, w_out, outa_d, outb_d, out2)


def modulate(nc, ident, a_col, b_col, gate_bc, c, c_ctx, w_ada, b_ada, norm_g, rpb,
             rpbpad_d, mask_d, kT_d, v_d, kside_d):
    NB = MODS // 512
    ROWS = 5 * KT
    with nc.cleanup_on_exit(), ExitStack() as cx:
        sb = lambda n, s, d=F32: cx.enter_context(nc.sbuf_tensor("mod_" + n, s, d))
        ps = lambda n, s: cx.enter_context(nc.psum_tensor("mod_" + n, s, F32))
        sem = lambda n: nc.alloc_semaphore("mod_" + n)
        rows = sb("rows", [ROWS, P])
        cols = sb("cols", [P, ROWS])
        cth = sb("cth", [P, 2 * KT])
        csum = sb("csum", [P, 2 * KT])
        cond = sb("cond", [P, 2 * KT])
        wada = [sb(f"wada{k}", [P, MODS]) for k in range(4)]
        mod = sb("mod", [2, MODS])
        ones = sb("ones", [1, P])
        bgate = sb("bgate", [1, D])
        gate_row = sb("gate_row", [1, D])
        scale1 = sb("scale1", [P, 2, KT])
        scale2 = sb("scale2", [P, 2, KT])
        rpb_raw = sb("rpb_raw", [1, H * RPR * RPC])
        rpb_row = sb("rpb_row", [1, PAD + H * RPR * RPC + PAD_END])
        masks = sb("masks", [P, 2, 3, LAT])
        zeros = sb("zeros", [P, D])
        p_mod = [ps(f"p_mod{n}", [2, 512]) for n in range(NB)]
        p_cols = ps("p_cols", [P, 512])
        p_gate = ps("p_gate", [P, 512])

        rows_in = sem("rows_in")
        wada_in = [sem(f"wada_in{k}") for k in range(4)]
        wada_used = sem("wada_used")
        bgate_in = sem("bgate_in")
        ident_ready = sem("ident_ready")
        consts_ready = sem("consts_ready")
        cols_t = sem("cols_t")
        cols_ready = sem("cols_ready")
        cth_ready = sem("cth_ready")
        csum_ready = sem("csum_ready")
        cond_ready = sem("cond_ready")
        mods_ready = sem("mods_ready")
        mod_copied = sem("mod_copied")
        modcols_t = sem("modcols_t")
        scale_step = sem("scale_step")
        gate_added = sem("gate_added")
        gate_p = sem("gate_p")
        gate_copied = sem("gate_copied")
        rpb_zeroed = sem("rpb_zeroed")
        rpb_in = sem("rpb_in")
        rpb_turned = sem("rpb_turned")
        rpb_out = sem("rpb_out")
        mask_step = sem("mask_step")
        masks_ready = sem("masks_ready")
        zeros_ready = sem("zeros_ready")
        side_out = sem("side_out")
        block = cx.enter_context(nc.Block())

        @block.sync
        def _(sp):
            sp.dma_start(rows[0:KT, :], c.rearrange("b (k p) -> (b k) p", p=P)).then_inc(rows_in, 16)
            sp.dma_start(rows[KT:2 * KT, :], c_ctx.rearrange("(k p) -> k p", p=P)).then_inc(rows_in, 16)
            sp.dma_start(rows[2 * KT:3 * KT, :], norm_g.rearrange("b (k p) -> (b k) p", p=P)).then_inc(rows_in, 16)
            sp.dma_start(rows[3 * KT:5 * KT, :],
                         b_ada[:, 0:2 * D].rearrange("b (k p) -> (b k) p", p=P)).then_inc(rows_in, 16)
            for k in range(KT):
                if k >= 4:
                    sp.wait_ge(wada_used, k - 3)
                sp.dma_start(wada[k % 4][:], w_ada[0, k * P:(k + 1) * P, :]).then_inc(wada_in[k % 4], 16)
            sp.dma_start(bgate[:], b_ada[:, 2 * D:3 * D]).then_inc(bgate_in, 16)

        @block.scalar
        def _(act):
            act.wait_ge(zeros_ready, 1)
            for n in (0, TILES + 1):
                act.dma_start(kT_d[n].rearrange("s d h t -> (s d) (h t)").bitcast(F32),
                              zeros[:]).then_inc(side_out, 16)
                act.dma_start(v_d[n], zeros[:, 0:DA]).then_inc(side_out, 16)
                act.dma_start(kside_d[:, :, :, n, :].rearrange("s d h t -> (s d) h t").bitcast(F32),
                              zeros[:, 0:H * GR * SC].rearrange("p (h t) -> p h t", h=H)).then_inc(side_out, 16)
            act.dma_start(rpb_raw[:], rpb.rearrange("b h r c -> b (h r c)")).then_inc(rpb_in, 16)
            act.wait_ge(cols_ready, 1)
            nc.scalar.activation(cth[:], cols[:, 0:2 * KT], ACT.Tanh, scale=0.5).then_inc(cth_ready, 1)
            act.wait_ge(rpb_zeroed, 1)
            act.wait_ge(rpb_in, 16)
            nc.scalar.activation(rpb_row[:, PAD:PAD + H * RPR * RPC], rpb_raw[:], ACT.Copy,
                                 scale=-1.0).then_inc(rpb_turned, 1)
            act.wait_ge(rpb_turned, 1)
            act.dma_start(rpbpad_d, rpb_row[:]).then_inc(rpb_out, 16)
            act.wait_ge(masks_ready, 1)
            act.dma_start(mask_d, masks[:]).then_inc(side_out, 16)
            act.wait_ge(rpb_out, 16)
            act.wait_ge(side_out, 7 * 16)

        @block.gpsimd
        def _(pool):
            nc.gpsimd.memset(ident[:], 0.0).then_inc(ident_ready, 1)
            nc.gpsimd.memset(ones[:], 1.0).then_inc(consts_ready, 1)
            pool.wait_ge(ident_ready, 1)
            nc.gpsimd.affine_select(out=ident[:], in_=ident[:], compare_op=ALU.not_equal, fill=1.0, base=0,
                                    pattern=[[-1, P]], channel_multiplier=1).then_inc(ident_ready, 1)
            nc.gpsimd.memset(zeros[:], 0.0).then_inc(zeros_ready, 1)
            nc.gpsimd.memset(rpb_row[:], 0.0).then_inc(rpb_zeroed, 1)
            step = 1
            nc.gpsimd.memset(masks[:], 0.0).then_inc(mask_step, 1)
            for half in range(2):
                for qr in range(GR):
                    q = slice(qr * HC, (qr + 1) * HC)
                    at_main, at_side = (0, HC), (MAIN, SC)

                    def keep(part, lo, hi, compare, base, mult, patt):
                        first, width = part
                        for edge in range(3):
                            view = masks[q, half, edge, first:first + 3 * GR * width].rearrange(
                                "p (r c) -> p r c", c=width)[:, :, lo:hi]
                            nc.gpsimd.affine_select(out=view, in_=view, compare_op=compare, fill=MASKED, base=base,
                                                    pattern=[[0, 3 * GR], [patt, hi - lo]],
                                                    channel_multiplier=mult).then_inc(mask_step, 1)

                    pool.wait_ge(mask_step, step)
                    if half == 0:
                        keep(at_main, 0, HC, ALU.is_ge, WC // 2, -1, 1)
                        pool.wait_ge(mask_step, step + 3)
                        keep(at_main, WC, HC, ALU.is_ge, WC // 2 - 1 - WC, 1, -1)
                        keep(at_side, 0, SC, ALU.is_ge, WC // 2 - 1 - HC, 1, -1)
                    else:
                        keep(at_main, 0, WC, ALU.is_ge, WC // 2, -1, 1)
                        pool.wait_ge(mask_step, step + 3)
                        keep(at_main, 0, HC, ALU.is_ge, WC // 2 - 1, 1, -1)
                        keep(at_side, 0, SC, ALU.is_ge, 0, -1, 1)
                    step += 9
                    pool.wait_ge(mask_step, step)
                    for edge, first in enumerate((GR, qr, 0)):
                        for lo, hi in ((0, first), (first + WR, 3 * GR)):
                            if lo < hi:
                                nc.gpsimd.memset(masks[q, half, edge, lo * HC:hi * HC], MASKED).then_inc(mask_step, 1)
                                nc.gpsimd.memset(masks[q, half, edge, MAIN + lo * SC:MAIN + hi * SC],
                                                 MASKED).then_inc(mask_step, 1)
                                step += 2
            pool.wait_ge(mask_step, step)
            pool.sem_inc(masks_ready, 1)

        @block.tensor
        def _(pe):
            pe.wait_ge(ident_ready, 2)
            pe.wait_ge(rows_in, 64)
            nc.tensor.transpose(p_cols[:, 0:ROWS], rows[:], ident[0:ROWS, 0:ROWS]).then_inc(cols_t, 1)
            pe.wait_ge(cond_ready, 1)
            cond3 = cond[:].rearrange("p (s k) -> p s k", s=2)
            for k in range(KT):
                pe.wait_ge(wada_in[k % 4], 16 * (k // 4 + 1))
                for n in range(NB):
                    last = nc.tensor.matmul(p_mod[n][:], cond3[:, :, k], wada[k % 4][:, n * 512:(n + 1) * 512],
                                            start=(k == 0), stop=(k == KT - 1))
                last.then_inc(wada_used, 1)
            pe.wait_ge(mod_copied, 1)
            for j in range(2 * KT):
                last = nc.tensor.transpose(p_cols[:, 64 + 2 * j:66 + 2 * j], mod[:, j * P:(j + 1) * P], ident[0:2, 0:2])
            last.then_inc(modcols_t, 1)
            pe.wait_ge(consts_ready, 1)
            for n in range(2):
                pe.wait_ge(gate_added, 1)
                if n == 1:
                    pe.wait_ge(gate_copied, 1)
                nc.tensor.matmul(p_gate[:], ones[:], gate_row[:, n * 512:(n + 1) * 512],
                                 start=True, stop=True).then_inc(gate_p, 1)

        @block.vector
        def _(dve):
            dve.wait_ge(cols_t, 1)
            nc.vector.tensor_copy(cols[:], p_cols[:, 0:ROWS]).then_inc(cols_ready, 1)
            dve.wait_ge(cth_ready, 1)
            nc.vector.tensor_scalar(csum[:], cth[:], 1.0, 0.5, ALU.add, ALU.mult).then_inc(csum_ready, 1)
            dve.wait_ge(csum_ready, 1)
            nc.vector.tensor_tensor(cond[:], csum[:], cols[:, 0:2 * KT], ALU.mult).then_inc(cond_ready, 1)
            dve.wait_ge(wada_used, KT)
            for n in range(NB):
                last = nc.vector.tensor_copy(mod[:, n * 512:(n + 1) * 512], p_mod[n][:])
            last.then_inc(mod_copied, 1)
            dve.wait_ge(mod_copied, 1)
            dve.wait_ge(bgate_in, 16)
            nc.vector.tensor_tensor(gate_row[:], mod[0:1, 2 * D:3 * D], bgate[:], ALU.add).then_inc(gate_added, 1)
            dve.wait_ge(modcols_t, 1)
            both = p_cols[:, 64:64 + 4 * KT].rearrange("p (j k s) -> p j s k", j=2, s=2)
            for s in range(2):
                nc.vector.tensor_tensor(b_col[:, s, :], both[:, 0, s, :], cols[:, 3 * KT:4 * KT], ALU.add)
                nc.vector.tensor_tensor(scale1[:, s, :], both[:, 1, s, :], cols[:, 4 * KT:5 * KT],
                                        ALU.add).then_inc(scale_step, 1)
            dve.wait_ge(scale_step, 2)
            nc.vector.tensor_scalar(scale2[:], scale1[:], 1.0, None, ALU.add).then_inc(scale_step, 1)
            dve.wait_ge(scale_step, 3)
            for s in range(2):
                nc.vector.tensor_tensor(a_col[:, s, :], scale2[:, s, :], cols[:, 2 * KT:3 * KT], ALU.mult)
            for n in range(2):
                dve.wait_ge(gate_p, n + 1)
                nc.vector.tensor_copy(gate_bc[:, n * 512:(n + 1) * 512], p_gate[:]).then_inc(gate_copied, 1)


class SplitWeights:

    def __init__(self, nc, cx, name, source, blocks):
        self.nc, self.blocks = nc, blocks
        self.source = source.rearrange("(k p) n -> p k n", p=P)
        self.raw = [cx.enter_context(nc.sbuf_tensor(f"{name}_raw{k}", [P, 2, 512], F32)) for k in range(2)]
        self.hi = cx.enter_context(nc.sbuf_tensor(f"{name}_hi", [P, KT, 512 * len(blocks)], F32R))
        self.lo = cx.enter_context(nc.sbuf_tensor(f"{name}_lo", [P, KT, 512 * len(blocks)], F32R))
        self.loaded = [nc.alloc_semaphore(f"{name}_loaded{k}") for k in range(2)]
        self.hi_done = nc.alloc_semaphore(f"{name}_hi_done")
        self.lo_done = nc.alloc_semaphore(f"{name}_lo_done")
        self.per_block = KT // 2
        self.chunks = self.per_block * len(blocks)

    def part(self, n):
        k, col = 2 * (n % self.per_block), self.blocks[n // self.per_block]
        return slice(k, k + 2), slice(col, col + 512)

    def ready(self, pe, col):
        pe.wait_ge(self.lo_done, self.per_block * (self.blocks.index(col) + 1))

    def load(self, dma, chunks=None):
        for n in chunks or range(self.chunks):
            if n >= 2:
                dma.wait_ge(self.lo_done, n - 1)
            dma.dma_start(self.raw[n % 2][:], self.source[:, *self.part(n)]).then_inc(self.loaded[n % 2], 16)

    def round_hi(self, act, chunks=None):
        for n in chunks or range(self.chunks):
            act.wait_ge(self.loaded[n % 2], 16 * (n // 2 + 1))
            self.nc.scalar.activation(self.hi[:, *self.part(n)], self.raw[n % 2][:], ACT.Copy).then_inc(self.hi_done, 1)

    def take_lo(self, dve, chunks=None):
        for n in chunks or range(self.chunks):
            dve.wait_ge(self.hi_done, n + 1)
            self.nc.vector.tensor_tensor(self.lo[:, *self.part(n)], self.raw[n % 2][:],
                                         self.hi[:, *self.part(n)].bitcast(F32), ALU.subtract).then_inc(self.lo_done, 1)


class NormedInput:

    def __init__(self, nc, cx, stage, ident):
        self.nc, self.ident = nc, ident
        sb = lambda n, s, d=F32: cx.enter_context(nc.sbuf_tensor(f"{stage}_{n}", s, d))
        sem = lambda n: nc.alloc_semaphore(f"{stage}_{n}")
        self.xt = [sb(f"xt{k}", [P, D]) for k in range(2)]
        self.squares = sb("x_squares", [P, D], mybir.dt.bfloat16)
        self.sumsq = sb("x_sumsq", [P, 2])
        self.meansq = sb("x_meansq", [P, 2])
        self.rstd = sb("x_rstd", [P, 2])
        self.minus_half = sb("minus_half", [P, 2 * H])
        self.normed = sb("x_normed", [P, D])
        self.hT = sb("hT", [P, KT, P])
        self.hi = [sb(f"hT_hi{k}", [P, KT, P], F32R) for k in range(2)]
        self.lo = [sb(f"hT_lo{k}", [P, KT, P], F32R) for k in range(2)]
        self.p_t = cx.enter_context(nc.psum_tensor(f"{stage}_p_hT", [P, KT, P], F32))
        self.x_in = [sem(f"x_in{k}") for k in range(2)]
        self.half_ready = sem("half_ready")
        self.sumsq_ready = sem("sumsq_ready")
        self.meansq_ready = sem("meansq_ready")
        self.rstd_ready = sem("rstd_ready")
        self.normed_ready = sem("normed_ready")
        self.transposed = sem("transposed")
        self.modulated = sem("modulated")
        self.hi_ready = sem("hi_ready")
        self.split_ready = sem("split_ready")
        self.tile_done = sem("tile_done")

    def square(self, act, i, u):
        t = 2 * i + u
        act.wait_ge(self.x_in[u], 16 * (i + 1))
        wait(act, self.meansq_ready, t - 1)
        wait(act, self.sumsq_ready, t)
        self.nc.scalar.activation(self.squares[:], self.xt[u][:], ACT.Square,
                                  accum_out=self.sumsq[:, u:u + 1]).then_inc(self.sumsq_ready, 1)

    def mean(self, dve, i, u):
        t = 2 * i + u
        dve.wait_ge(self.sumsq_ready, t + 1)
        wait(dve, self.rstd_ready, t - 1)
        self.nc.vector.tensor_scalar(self.meansq[:, u:u + 1], self.sumsq[:, u:u + 1], 1.0 / D, EPS,
                                     ALU.mult, ALU.add).then_inc(self.meansq_ready, 1)

    def root(self, pool, i, u):
        t = 2 * i + u
        pool.wait_ge(self.meansq_ready, t + 1)
        wait(pool, self.normed_ready, t - 1)
        self.nc.gpsimd.tensor_tensor(self.rstd[:, u:u + 1], self.meansq[:, u:u + 1], self.minus_half[:, 0:1],
                                     ALU.pow).then_inc(self.rstd_ready, 1)

    def normalise(self, dve, i, u):
        t = 2 * i + u
        dve.wait_ge(self.rstd_ready, t + 1)
        wait(dve, self.transposed, t)
        self.nc.vector.tensor_scalar(self.normed[:], self.xt[u][:], self.rstd[:, u:u + 1], None,
                                     ALU.mult).then_inc(self.normed_ready, 1)

    def transpose(self, pe, i, u):
        t = 2 * i + u
        pe.wait_ge(self.normed_ready, t + 1)
        wait(pe, self.modulated, t)
        for k in range(KT):
            last = self.nc.tensor.transpose(self.p_t[:, k, :], self.normed[:, k * P:(k + 1) * P], self.ident[:])
        last.then_inc(self.transposed, 1)

    def modulate(self, act, i, u, a_col, b_col):
        t = 2 * i + u
        act.wait_ge(self.transposed, t + 1)
        wait(act, self.split_ready, t)
        for k in range(KT):
            last = self.nc.scalar.activation(self.hT[:, k, :], self.p_t[:, k, :], ACT.Identity,
                                             scale=a_col[:, k:k + 1], bias=b_col[:, k:k + 1])
        last.then_inc(self.modulated, 1)

    def split(self, dve, i, u):
        t = 2 * i + u
        dve.wait_ge(self.modulated, t + 1)
        wait(dve, self.tile_done, t - 1)
        self.nc.vector.tensor_copy(self.hi[u][:], self.hT[:]).then_inc(self.hi_ready, 1)
        dve.wait_ge(self.hi_ready, t + 1)
        self.nc.vector.tensor_tensor(self.lo[u][:], self.hT[:], self.hi[u][:].bitcast(F32),
                                     ALU.subtract).then_inc(self.split_ready, 1)

    def products(self, u, bank, weights, col, width=512):
        c = slice(col, col + width)
        for k in range(KT):
            self.nc.tensor.matmul(bank, self.hi[u][:, k, :], weights.hi[:, k, c], start=(k == 0), stop=False)
            self.nc.tensor.matmul(bank, self.hi[u][:, k, :], weights.lo[:, k, c], start=False, stop=False)
            last = self.nc.tensor.matmul(bank, self.lo[u][:, k, :], weights.hi[:, k, c],
                                         start=False, stop=(k == KT - 1))
        return last


def gating(nc, ident, a_col, b_col, x2, w_in, sgu_norm_g, w_spatial, b_spatial, outa_d, rpbpad_d, bias_d):
    U, V, G = 0, DA, 2 * DA
    CH = DA // GROUPS
    with nc.cleanup_on_exit(), ExitStack() as cx:
        sb = lambda n, s, d=F32: cx.enter_context(nc.sbuf_tensor("sgu_" + n, s, d))
        ps = lambda n, s: cx.enter_context(nc.psum_tensor("sgu_" + n, s, F32))
        sem = lambda n: nc.alloc_semaphore("sgu_" + n)
        w = SplitWeights(nc, cx, "wa", w_in[0, :, 0:3 * DA], [V, U, G])
        h = NormedInput(nc, cx, "sgu", ident)
        ws_raw = sb("ws_raw", [P, GROUPS, P])
        wsT = sb("wsT", [P, GROUPS, P])
        bs_raw = sb("bs_raw", [GROUPS, P])
        bs = sb("bs", [P, GROUPS])
        sgu_bc = sb("sgu_bc", [P, DA])
        v_act = sb("v_act", [P, DA])
        v_squares = sb("v_squares", [P, DA])
        v_sumsq = sb("v_sumsq", [P, GROUPS])
        v_meansq = sb("v_meansq", [P, GROUPS])
        v_rstd = sb("v_rstd", [P, GROUPS])
        v_normed = sb("v_normed", [P, DA])
        u_act = sb("u_act", [P, DA])
        g_tanh = sb("g_tanh", [P, DA])
        g_silu2 = sb("g_silu2", [P, DA])
        gated = sb("gated", [P, DA])
        outa = [sb(f"outa{k}", [P, DA]) for k in range(2)]
        p_v, p_u, p_g, p_mix = ps("p_v", [P, DA]), ps("p_u", [P, DA]), ps("p_g", [P, DA]), ps("p_mix", [P, DA])

        small_in = sem("small_in")
        half_ready = h.half_ready
        ws_t = sem("ws_t")
        ws_ready = sem("ws_ready")
        bias_out = sem("bias_out")
        v_ready, u_ready = sem("v_ready"), sem("u_ready")
        g_ready = h.tile_done
        v_gelu, u_gelu, g_tanh_ready = sem("v_gelu"), sem("u_gelu"), sem("g_tanh_ready")
        v_sumsq_ready, v_meansq_ready, v_rstd_ready = sem("v_ssq"), sem("v_msq"), sem("v_rstd_ready")
        v_normed_ready = sem("v_normed_ready")
        mix_ready = sem("mix_ready")
        silu_ready = sem("silu_ready")
        gated_ready = sem("gated_ready")
        outa_ready = sem("outa_ready")
        outa_out = [sem(f"outa_out{k}") for k in range(2)]
        block = cx.enter_context(nc.Block())
        PT = TILES // 2

        def load_x(dma, i, u):
            dma.dma_start(h.xt[u][:], x2[bass.ds((2 * i + u) * P, P), :]).then_inc(h.x_in[u], 16)

        @block.sync
        def _(sp):
            load_x(sp, 0, 0)
            load_x(sp, 0, 1)
            w.load(sp)

            def tile(i, u, more):
                t = 2 * i + u
                if more:
                    sp.wait_ge(h.normed_ready, t + 1)
                    load_x(sp, i + 1, u)
                sp.wait_ge(outa_ready, t + 1)
                sp.dma_start(outa_d[bass.ds(t * P, P), :], outa[u][:]).then_inc(outa_out[u], 16)

            for u in range(2):
                tile(0, u, True)
            with sp.Fori(1, PT - 1) as i:
                for u in range(2):
                    tile(i, u, True)
            for u in range(2):
                tile(PT - 1, u, False)
            for u in range(2):
                sp.wait_ge(outa_out[u], 16 * PT)

        @block.gpsimd
        def _(pool):
            nc.gpsimd.memset(h.minus_half[:], -0.5).then_inc(half_ready, 1)
            pool.wait_ge(half_ready, 1)

            def tile(i, u, more):
                t = 2 * i + u
                if more:
                    h.root(pool, i + (u + 1) // 2, (u + 1) % 2)
                pool.wait_ge(v_meansq_ready, t + 1)
                wait(pool, v_normed_ready, t)
                nc.gpsimd.tensor_tensor(v_rstd[:], v_meansq[:], h.minus_half[:, 0:GROUPS],
                                        ALU.pow).then_inc(v_rstd_ready, 1)

            h.root(pool, 0, 0)
            for u in range(2):
                tile(0, u, True)
            with pool.Fori(1, PT - 1) as i:
                for u in range(2):
                    tile(i, u, True)
            for u in range(2):
                tile(PT - 1, u, u == 0)

        @block.scalar
        def _(act):
            act.dma_start(ws_raw[:], w_spatial[0].rearrange("g p q -> p g q")).then_inc(small_in, 16)
            act.dma_start(bs_raw[:], b_spatial[0]).then_inc(small_in, 16)
            act.dma_start(sgu_bc[:], sgu_norm_g.to_broadcast([P, DA])).then_inc(small_in, 16)
            for half in range(2):
                for qr in range(GR):
                    at = PAD + (GR - 1 - qr) * RPC + WC - 1 - half * SC
                    act.dma_start(
                        bias_d[half, qr * HC:(qr + 1) * HC].rearrange("p n r c -> (n r) p c"),
                        bass.AP(rpbpad_d.tensor, at,
                                [[RPC, H * RPR], [-1, HC], [1, HC + SC]])).then_inc(bias_out, 16)
            h.square(act, 0, 0)
            h.modulate(act, 0, 0, a_col[:, 0, :], b_col[:, 0, :])
            w.round_hi(act)

            def tile(i, u, more):
                t = 2 * i + u
                n, m = i + (u + 1) // 2, (u + 1) % 2
                if more:
                    h.square(act, n, m)
                act.wait_ge(v_ready, t + 1)
                wait(act, v_normed_ready, t)
                nc.scalar.activation(v_act[:], p_v[:], ACT.Gelu).then_inc(v_gelu, 1)
                act.wait_ge(v_gelu, t + 1)
                wait(act, v_meansq_ready, t)
                for k in range(GROUPS):
                    last = nc.scalar.activation(v_squares[:, k * CH:(k + 1) * CH], v_act[:, k * CH:(k + 1) * CH], ACT.Square,
                                                accum_out=v_sumsq[:, k:k + 1])
                last.then_inc(v_sumsq_ready, 1)
                act.wait_ge(u_ready, t + 1)
                wait(act, gated_ready, t)
                nc.scalar.activation(u_act[:], p_u[:], ACT.Gelu).then_inc(u_gelu, 1)
                if more:
                    h.modulate(act, n, m, a_col[:, 0, :], b_col[:, 0, :])
                act.wait_ge(g_ready, t + 1)
                wait(act, silu_ready, t)
                nc.scalar.activation(g_tanh[:], p_g[:], ACT.Tanh, scale=0.5).then_inc(g_tanh_ready, 1)

            for u in range(2):
                tile(0, u, True)
            with act.Fori(1, PT - 1) as i:
                for u in range(2):
                    tile(i, u, True)
            for u in range(2):
                tile(PT - 1, u, u == 0)
            act.wait_ge(bias_out, 16 * 2 * GR)

        @block.tensor
        def _(pe):
            h.transpose(pe, 0, 0)
            pe.wait_ge(small_in, 48)
            for k in range(GROUPS):
                nc.tensor.transpose(p_mix[:, k * P:(k + 1) * P], ws_raw[:, k, :], ident[:])
            nc.tensor.transpose(p_g[:, 0:GROUPS], bs_raw[:], ident[0:GROUPS, 0:GROUPS]).then_inc(ws_t, 1)

            def tile(i, u, more):
                t = 2 * i + u
                pe.wait_ge(h.split_ready, t + 1)
                wait(pe, v_gelu, t)
                if isinstance(t, int) and t == 0:
                    w.ready(pe, V)
                h.products(u, p_v[:], w, V).then_inc(v_ready, 1)
                wait(pe, u_gelu, t)
                if isinstance(t, int) and t == 0:
                    w.ready(pe, U)
                h.products(u, p_u[:], w, U).then_inc(u_ready, 1)
                if more:
                    h.transpose(pe, i + (u + 1) // 2, (u + 1) % 2)
                wait(pe, silu_ready, t)
                if isinstance(t, int) and t == 0:
                    pe.wait_ge(ws_ready, 1)
                    w.ready(pe, G)
                h.products(u, p_g[:], w, G).then_inc(h.tile_done, 1)
                pe.wait_ge(v_normed_ready, t + 1)
                wait(pe, gated_ready, t)
                for k in range(GROUPS):
                    last = nc.tensor.matmul(p_mix[:, k * CH:(k + 1) * CH], wsT[:, k, :],
                                            v_normed[:, k * CH:(k + 1) * CH], start=True, stop=True)
                last.then_inc(mix_ready, 1)

            for u in range(2):
                tile(0, u, True)
            with pe.Fori(1, PT - 1) as i:
                for u in range(2):
                    tile(i, u, True)
            for u in range(2):
                tile(PT - 1, u, u == 0)

        @block.vector
        def _(dve):
            h.mean(dve, 0, 0)
            h.normalise(dve, 0, 0)
            h.split(dve, 0, 0)
            dve.wait_ge(ws_t, 1)
            nc.vector.tensor_copy(wsT[:].rearrange("p a b -> p (a b)"), p_mix[:])
            nc.vector.tensor_copy(bs[:], p_g[:, 0:GROUPS]).then_inc(ws_ready, 1)
            w.take_lo(dve)

            def tile(i, u, more):
                t = 2 * i + u
                n, m = i + (u + 1) // 2, (u + 1) % 2
                if more:
                    h.mean(dve, n, m)
                    h.normalise(dve, n, m)
                dve.wait_ge(v_sumsq_ready, t + 1)
                wait(dve, v_rstd_ready, t)
                nc.vector.tensor_scalar(v_meansq[:], v_sumsq[:], 1.0 / CH, EPS, ALU.mult,
                                        ALU.add).then_inc(v_meansq_ready, 1)
                dve.wait_ge(v_rstd_ready, t + 1)
                wait(dve, mix_ready, t)
                for k in range(GROUPS):
                    s = slice(k * CH, (k + 1) * CH)
                    last = nc.vector.scalar_tensor_tensor(out=v_normed[:, s], in0=v_act[:, s],
                                                          scalar=v_rstd[:, k:k + 1], in1=sgu_bc[:, s],
                                                          op0=ALU.mult, op1=ALU.mult)
                last.then_inc(v_normed_ready, 1)
                if more:
                    h.split(dve, n, m)
                dve.wait_ge(g_tanh_ready, t + 1)
                wait(dve, outa_ready, t)
                nc.vector.scalar_tensor_tensor(out=g_silu2[:], in0=g_tanh[:], scalar=1.0, in1=p_g[:],
                                               op0=ALU.add, op1=ALU.mult).then_inc(silu_ready, 1)
                dve.wait_ge(mix_ready, t + 1)
                dve.wait_ge(u_gelu, t + 1)
                for k in range(GROUPS):
                    s = slice(k * CH, (k + 1) * CH)
                    last = nc.vector.scalar_tensor_tensor(out=gated[:, s], in0=p_mix[:, s], scalar=bs[:, k:k + 1],
                                                          in1=u_act[:, s], op0=ALU.add, op1=ALU.mult)
                last.then_inc(gated_ready, 1)
                dve.wait_ge(gated_ready, t + 1)
                dve.wait_ge(silu_ready, t + 1)
                wait(dve, outa_out[u], 16 * i)
                nc.vector.scalar_tensor_tensor(out=outa[u][:], in0=g_silu2[:], scalar=0.5, in1=gated[:],
                                               op0=ALU.mult, op1=ALU.mult).then_inc(outa_ready, 1)

            for u in range(2):
                tile(0, u, True)
            with dve.Fori(1, PT - 1) as i:
                for u in range(2):
                    tile(i, u, True)
            for u in range(2):
                tile(PT - 1, u, u == 0)


def project(nc, ident, a_col, b_col, x2, ctx2, w_in, q_norm_g, k_norm_g,
            qT_d, kT_d, v_d, kside_d, sg_d, kctx_d, vctx_d):
    Q, K, V, G = 0, DA, 2 * DA, 3 * DA
    with nc.cleanup_on_exit(), ExitStack() as cx:
        sb = lambda n, s, d=F32: cx.enter_context(nc.sbuf_tensor("pro_" + n, s, d))
        ps = lambda n, s: cx.enter_context(nc.psum_tensor("pro_" + n, s, F32))
        sem = lambda n: nc.alloc_semaphore("pro_" + n)
        w = SplitWeights(nc, cx, "wb", w_in[0, :, 3 * DA:7 * DA], [K, V, Q, G])
        h = NormedInput(nc, cx, "pro", ident)
        gq = sb("gq", [P, 2])
        gk = sb("gk", [P, 1])
        squares = sb("qk_squares", [P, 2, DA])
        sumsq = sb("qk_sumsq", [P, 2 * H])
        meansq = sb("qk_meansq", [P, 2 * H])
        rstd = sb("qk_rstd", [P, 2 * H])
        qkn = sb("qkn", [P, 2, DA])
        g_tanh = sb("bg_tanh", [P, DA])
        qT = [sb(f"qT{k}", [P, 2, PAIRS * P], F32R) for k in range(2)]
        kT = [sb(f"kT{k}", [P, 2, PAIRS * P], F32R) for k in range(2)]
        kside = [sb(f"kside{k}", [P, 2, PAIRS * GR, SC], F32R) for k in range(2)]
        v_sb, sg = sb("v_sb", [P, DA]), sb("sg", [P, DA])
        p_q, p_k, p_v, p_g = ps("pb_q", [P, DA]), ps("pb_k", [P, DA]), ps("pb_v", [P, DA]), ps("pb_g", [P, DA])
        p_qT, p_kT = ps("p_qT", [P, PAIRS * P]), ps("p_kT", [P, PAIRS * P])

        gains_in = sem("gains_in")
        gq_ready = sem("gq_ready")
        q_ready, k_ready, v_ready = sem("q_ready"), sem("k_ready"), sem("vb_ready")
        q_squared, k_squared = sem("q_squared"), sem("k_squared")
        sums_ready, means_ready, rstds_ready = sem("qk_sums"), sem("qk_means"), sem("qk_rstds")
        q_normed, k_normed = sem("q_normed"), sem("k_normed")
        qT_ready, kT_ready = sem("qT_ready"), sem("kT_ready")
        q_rounded, k_rounded, q_split, k_split = (sem("q_rounded"), sem("k_rounded"), sem("qT_split"),
                                                  sem("kT_split"))
        v_copied, g_tanhed, sg_ready = sem("v_copied"), sem("bg_tanhed"), sem("sg_ready")
        q_out, k_out, ks_out = ([sem(f"{n}_out{k}") for k in range(2)] for n in ("q", "k", "ks"))
        v_out, sg_out = sem("vb_out"), sem("sg_out")
        g_ready = sem("bg_ready")
        h.tile_done = kT_ready
        block = cx.enter_context(nc.Block())
        PT = TILES // 2 + 1


        def load_x(dma, i, u):
            if isinstance(i, int) and i == 0:
                dma.dma_start(h.xt[u][:], ctx2[u * P:(u + 1) * P, :]).then_inc(h.x_in[u], 16)
            else:
                rows = x2[bass.ds((i - 1) * (GR * GW), GR * GW), :].rearrange("(r h c) d -> h r c d", r=GR, h=2)
                dma.dma_start(h.xt[u][:], rows[u]).then_inc(h.x_in[u], 16)

        def near(u):
            first = HC - SC if u == 0 else 0
            return p_kT[:].rearrange("p (x c) -> p x c", c=HC)[:, :, first:first + SC]

        def pairs(e, tile):
            for i in (0, 1):
                for u in range(2):
                    tile(i, u, True)
            with e.Fori(2, PT - 1) as i:
                for u in range(2):
                    tile(i, u, True)
            for u in range(2):
                tile(PT - 1, u, u == 0)

        def store_parts(dma, dst, src, width, done):
            for part in range(2):
                for n in range(2):
                    heads = dst[part].rearrange("d (a n) t -> d n a t", n=2)[:, n].bitcast(F32)
                    tile = src[n * DH:(n + 1) * DH, part].bitcast(F32)
                    if width != P:
                        tile = tile.rearrange("p x c -> p (x c)")
                    dma.dma_start(heads, tile.rearrange("p (a t) -> p a t", t=width)).then_inc(done, 16)

        @block.sync
        def _(sp):
            load_x(sp, 0, 0)
            load_x(sp, 0, 1)
            w.load(sp)

            def tile(i, u, more):
                t = 2 * i + u
                latent = not (isinstance(i, int) and i == 0)
                if not (isinstance(i, int) and i == PT - 1):
                    sp.wait_ge(h.normed_ready, t + 1)
                    load_x(sp, i + 1, u)
                n = (i - 1) + u * GN
                sp.wait_ge(v_copied, t + 1)
                if latent:
                    sp.dma_start(v_d[bass.ds(n + 1, 1)][0], v_sb[:]).then_inc(v_out, 16)
                    sp.wait_ge(sg_ready, t - 1)
                    sp.dma_start(sg_d[bass.ds(n, 1)][0], sg[:]).then_inc(sg_out, 16)
                    sp.wait_ge(q_split, t - 1)
                    for half in range(2):
                        dst = qT_d[bass.ds(n, 1)][0].rearrange("d s (a n) t -> d n (s a) t", n=2)[:, half]
                        sp.dma_start(dst.bitcast(F32), qT[u][half * DH:(half + 1) * DH].bitcast(F32).rearrange(
                            "p s (a t) -> p (s a) t", t=P)).then_inc(q_out[u], 16)
                    sp.wait_ge(k_split, t + 1)
                    store_parts(sp, kT_d[bass.ds(n + 1, 1)][0], kT[u], P, k_out[u])
                    store_parts(sp, kside_d[:, :, :, bass.ds(n + 1, 1), :].rearrange("s d h o t -> s d h (o t)"),
                                kside[u], GR * SC, ks_out[u])
                else:
                    sp.dma_start(vctx_d[u * P:(u + 1) * P, :], v_sb[:]).then_inc(v_out, 16)
                    sp.wait_ge(k_split, t + 1)
                    store_parts(sp, kctx_d[:, :, :, u * P:(u + 1) * P], kT[u], P, k_out[u])

            pairs(sp, tile)
            sp.wait_ge(v_out, 16 * (TILES + 2))
            sp.wait_ge(sg_out, 16 * TILES)
            for u in range(2):
                sp.wait_ge(k_out[u], 64 * PT)
                sp.wait_ge(q_out[u], 32 * (PT - 1))
                sp.wait_ge(ks_out[u], 64 * (PT - 1))

        @block.gpsimd
        def _(pool):
            nc.gpsimd.memset(h.minus_half[:], -0.5).then_inc(h.half_ready, 1)
            pool.wait_ge(h.half_ready, 1)

            def tile(i, u, more):
                t = 2 * i + u
                if more:
                    h.root(pool, i + (u + 1) // 2, (u + 1) % 2)
                pool.wait_ge(means_ready, t + 1)
                wait(pool, k_normed, t)
                used = slice(H, 2 * H) if isinstance(i, int) and i == 0 else slice(0, 2 * H)
                nc.gpsimd.tensor_tensor(rstd[:, used], meansq[:, used], h.minus_half[:, used],
                                        ALU.pow).then_inc(rstds_ready, 1)

            h.root(pool, 0, 0)
            pairs(pool, tile)

        @block.scalar
        def _(act):
            for n in range(2):
                half = slice(n * DH, (n + 1) * DH)
                act.dma_start(gq[half, 0:1], q_norm_g.rearrange("b d -> d b")).then_inc(gains_in, 16)
                act.dma_start(gk[half, :], k_norm_g.rearrange("b d -> d b")).then_inc(gains_in, 16)
            h.square(act, 0, 0)
            h.modulate(act, 0, 0, a_col[:, 1, :], b_col[:, 1, :])
            w.round_hi(act)
            act.wait_ge(gq_ready, 1)

            def tile(i, u, more):
                t = 2 * i + u
                latent = not (isinstance(i, int) and i == 0)
                n, m = i + (u + 1) // 2, (u + 1) % 2
                if more:
                    h.square(act, n, m)
                if latent:
                    act.wait_ge(q_ready, t - 1)
                    wait(act, sums_ready, t)
                    nc.scalar.activation(squares[:, 0, :], p_q[:], ACT.Square).then_inc(q_squared, 1)
                act.wait_ge(k_ready, t + 1)
                wait(act, sums_ready, t)
                nc.scalar.activation(squares[:, 1, :], p_k[:], ACT.Square).then_inc(k_squared, 1)
                if more:
                    s = 1 if isinstance(n, int) and n == 0 else 0
                    h.modulate(act, n, m, a_col[:, s, :], b_col[:, s, :])
                act.wait_ge(v_ready, t + 1)
                wait(act, v_out, 16 * t)
                nc.scalar.activation(v_sb[:], p_v[:], ACT.Copy).then_inc(v_copied, 1)
                if latent:
                    act.wait_ge(g_ready, t - 1)
                    wait(act, sg_ready, t - 2)
                    nc.scalar.activation(g_tanh[:], p_g[:], ACT.Tanh, scale=0.5).then_inc(g_tanhed, 1)
                    act.wait_ge(qT_ready, t - 1)
                    wait(act, q_out[u], 32 * (i - 1))
                    nc.scalar.activation(qT[u][:, 0], p_qT[:], ACT.Identity, scale=gq[:, 1:2]).then_inc(q_rounded, 1)
                act.wait_ge(kT_ready, t + 1)
                wait(act, k_out[u], 64 * i)
                last = nc.scalar.activation(kT[u][:, 0], p_kT[:], ACT.Identity, scale=gk[:, 0:1])
                if latent:
                    wait(act, ks_out[u], 64 * (i - 1))
                    last = nc.scalar.activation(kside[u][:, 0], near(u), ACT.Identity, scale=gk[:, 0:1])
                last.then_inc(k_rounded, 1)

            pairs(act, tile)

        @block.tensor
        def _(pe):
            h.transpose(pe, 0, 0)

            def tile(i, u, more):
                t = 2 * i + u
                latent = not (isinstance(i, int) and i == 0)
                first = isinstance(t, int) and t in (0, 2)
                pe.wait_ge(h.split_ready, t + 1)
                if latent:
                    if first:
                        w.ready(pe, Q)
                    wait(pe, q_normed, t - 2)
                    h.products(u, p_q[:], w, Q).then_inc(q_ready, 1)
                wait(pe, k_normed, t)
                if first and not latent:
                    w.ready(pe, K)
                h.products(u, p_k[:], w, K).then_inc(k_ready, 1)
                if more:
                    h.transpose(pe, i + (u + 1) // 2, (u + 1) % 2)
                wait(pe, v_copied, t)
                if latent:
                    h.products(u, p_v[:], w, V).then_inc(v_ready, 1)
                    wait(pe, sg_ready, t - 2)
                    if first:
                        w.ready(pe, G)
                    h.products(u, p_g[:], w, G).then_inc(g_ready, 1)
                else:
                    if first:
                        w.ready(pe, V)
                    h.products(u, p_v[:], w, V).then_inc(v_ready, 1)
                if latent:
                    pe.wait_ge(q_normed, t - 1)
                    wait(pe, q_split, t - 2)
                    for a in range(PAIRS):
                        last = nc.tensor.transpose(p_qT[:, a * P:(a + 1) * P], qkn[:, 0, a * P:(a + 1) * P], ident[:])
                    last.then_inc(qT_ready, 1)
                pe.wait_ge(k_normed, t + 1)
                wait(pe, k_split, t)
                for a in range(PAIRS):
                    last = nc.tensor.transpose(p_kT[:, a * P:(a + 1) * P], qkn[:, 1, a * P:(a + 1) * P], ident[:])
                last.then_inc(kT_ready, 1)

            pairs(pe, tile)

        @block.vector
        def _(dve):
            h.mean(dve, 0, 0)
            h.normalise(dve, 0, 0)
            h.split(dve, 0, 0)
            dve.wait_ge(gains_in, 64)
            nc.vector.tensor_scalar(gq[:, 1:2], gq[:, 0:1], -DH ** -0.5, None, ALU.mult).then_inc(gq_ready, 1)
            w.take_lo(dve)

            def tile(i, u, more):
                t = 2 * i + u
                latent = not (isinstance(i, int) and i == 0)
                n, m = i + (u + 1) // 2, (u + 1) % 2
                if more:
                    h.mean(dve, n, m)
                    h.normalise(dve, n, m)
                wait(dve, means_ready, t)
                if latent:
                    dve.wait_ge(q_squared, t - 1)
                    nc.vector.tensor_reduce(sumsq[:, 0:H], squares[:, 0, :].rearrange("p (h d) -> p h d", h=H),
                                            AX.X, ALU.add)
                dve.wait_ge(k_squared, t + 1)
                nc.vector.tensor_reduce(sumsq[:, H:2 * H], squares[:, 1, :].rearrange("p (h d) -> p h d", h=H),
                                        AX.X, ALU.add).then_inc(sums_ready, 1)
                dve.wait_ge(sums_ready, t + 1)
                wait(dve, rstds_ready, t)
                used = slice(0, 2 * H) if latent else slice(H, 2 * H)
                nc.vector.tensor_scalar(meansq[:, used], sumsq[:, used], 1.0 / DH, EPS, ALU.mult,
                                        ALU.add).then_inc(means_ready, 1)
                if more:
                    h.split(dve, n, m)
                dve.wait_ge(rstds_ready, t + 1)
                if latent:
                    wait(dve, qT_ready, t - 2)
                    nc.vector.tensor_tensor(qkn[:, 0, :].rearrange("p (h d) -> p h d", h=H),
                                            p_q[:].rearrange("p (h d) -> p h d", h=H),
                                            rstd[:, 0:H].unsqueeze(2).to_broadcast([P, H, DH]),
                                            ALU.mult).then_inc(q_normed, 1)
                wait(dve, kT_ready, t)
                nc.vector.tensor_tensor(qkn[:, 1, :].rearrange("p (h d) -> p h d", h=H),
                                        p_k[:].rearrange("p (h d) -> p h d", h=H),
                                        rstd[:, H:2 * H].unsqueeze(2).to_broadcast([P, H, DH]),
                                        ALU.mult).then_inc(k_normed, 1)
                if latent:
                    dve.wait_ge(g_tanhed, t - 1)
                    wait(dve, sg_out, 16 * (t - 2))
                    nc.vector.scalar_tensor_tensor(out=sg[:], in0=g_tanh[:], scalar=1.0, in1=p_g[:],
                                                   op0=ALU.add, op1=ALU.mult).then_inc(sg_ready, 1)
                    dve.wait_ge(q_rounded, t - 1)
                    nc.vector.scalar_tensor_tensor(out=qT[u][:, 1], in0=p_qT[:], scalar=gq[:, 1:2],
                                                   in1=qT[u][:, 0].bitcast(F32), op0=ALU.mult,
                                                   op1=ALU.subtract).then_inc(q_split, 1)
                dve.wait_ge(k_rounded, t + 1)
                last = nc.vector.scalar_tensor_tensor(out=kT[u][:, 1], in0=p_kT[:], scalar=gk[:, 0:1],
                                                      in1=kT[u][:, 0].bitcast(F32), op0=ALU.mult, op1=ALU.subtract)
                if latent:
                    last = nc.vector.scalar_tensor_tensor(out=kside[u][:, 1], in0=near(u), scalar=gk[:, 0:1],
                                                          in1=kside[u][:, 0].bitcast(F32), op0=ALU.mult,
                                                          op1=ALU.subtract)
                last.then_inc(k_split, 1)

            pairs(dve, tile)


def attend(nc, ident, qT_d, kT_d, v_d, kside_d, sg_d, kctx_d, vctx_d, bias_d, mask_d, outb_d):
    STEPS, TURNS = TILES, TILES // RING
    T_LAG, PV_LAG, O_LAG = 2, 5, 7
    with nc.cleanup_on_exit(), ExitStack() as cx:
        sb = lambda n, s, d=F32: cx.enter_context(nc.sbuf_tensor("att_" + n, s, d))
        ps = lambda n, s: cx.enter_context(nc.psum_tensor("att_" + n, s, F32))
        sem = lambda n: nc.alloc_semaphore("att_" + n)
        q = [sb(f"q{k}", [P, 2, H, P], F32R) for k in range(2)]
        k_ring = sb("k_ring", [P, H, MIRROR * P], F32R)
        k_side = [sb(f"k_side{k}", [P, H, SIDECTX], F32R) for k in range(2)]
        v_ring = sb("v_ring", [P, RING, DA])
        v_side = [sb(f"v_side{k}", [P, DA]) for k in range(2)]
        v_ctx = sb("v_ctx", [P, 2, DA])
        sg = [sb(f"sgl{k}", [P, DA]) for k in range(2)]
        raw_bias = sb("raw_bias", [P, 2, H, 3 * GR, HC + SC])
        mask = sb("mask", [P, 2, 3, LAT])
        bias = sb("bias", [P, H, KEYS])
        scores = [sb(f"scores{k}", [P, KEYS]) for k in range(2)]
        probs = [sb(f"probs{k}", [P, KCH * P]) for k in range(2)]
        least = sb("least", [P, 2])
        den, rden = sb("den", [P, 2, H]), sb("rden", [P, H])
        pT = sb("pT", [P, 4, KCH * P])
        oT = [sb(f"oT{k}", [P, P]) for k in range(2)]
        o_div = sb("o_div", [P, DA])
        outb = [sb(f"outb{k}", [P, DA]) for k in range(2)]
        p_scores = [ps(f"p_scores{k}", [P, 1024])[:, 512 - MAIN:512 + SIDECTX] for k in range(2)]
        p_pT4, p_pT2 = ps("p_pT4", [P, 4 * P]), ps("p_pT2", [P, 4 * P])
        p_oT, p_o = ps("p_oT", [P, PAIRS * P]), ps("p_o", [P, DA])

        q_in, vs_in, sg_in = ([sem(f"{n}_in{k}") for k in range(2)] for n in ("q", "vs", "sgl"))
        side_in = [sem(f"side_in{k}") for k in range(2)]
        k_in = [sem(f"k_in{k}") for k in range(RING)]
        k_mirrored = sem("k_mirrored")
        v_in = [sem(f"v_in{k}") for k in range(RING)]
        kctx_in, vctx_in, tables_in = sem("kctx_in"), sem("vctx_in"), [sem(f"tables_in{k}") for k in range(2)]
        consts = sem("attend_consts")
        bias_ready = [sem(f"bias_ready{k}") for k in range(H)]
        bias_made = sem("bias_made")
        add_begun, mirror_begun, load_begun = sem("add_begun"), sem("mirror_begun"), sem("load_begun")
        scored, added, exped = sem("scored"), sem("added"), sem("exped")
        pT_ready, pT4_copied, pT2_copied = sem("pT_ready"), sem("pT4_copied"), sem("pT2_copied")
        oT_ready, oT_copied, o_ready = sem("oT_ready"), sem("oT_copied"), sem("o_ready")
        recip_ready, divided, outb_ready = sem("recip_ready"), sem("divided"), sem("outb_ready")
        outb_out = [sem(f"outb_out{k}") for k in range(2)]
        block = cx.enter_context(nc.Block())

        def back(i, u, n, lag):
            at = H * u + n - lag
            if at < 0:
                i, at = i - 1, at + H * RING
            return None if isinstance(i, int) and i < 0 else (i, at // H, at % H)

        def run(e, slot):
            for u in range(RING):
                for n in range(H):
                    slot(0, u, n, True)
            with e.Fori(1, TURNS) as i:
                for u in range(RING):
                    for n in range(H):
                        slot(i, u, n, True)
            for n in range(O_LAG + 1):
                slot(TURNS, 0, n, False)

        def masked_bias(e, s, n):
            half, edge = s // GN, {0: 0, 1: 1, GN - 1: 2}[s % GN]
            for at, width, first in ((0, HC, half * SC), (MAIN, SC, 0 if half else HC)):
                part = slice(at, at + 3 * GR * width)
                last = e.tensor_tensor(bias[:, n, part].rearrange("p (r c) -> p r c", c=width),
                                       raw_bias[:, half, n, :, first:first + width],
                                       mask[:, half, edge, part].rearrange("p (r c) -> p r c", c=width), ALU.add)
            return last

        @block.sync
        def _(sp):
            def store(s, b):
                sp.dma_start(outb_d[bass.ds(s, 1)][0], outb[b][:]).then_inc(outb_out[b], 16)

            def load_v(i, u, half):
                s, b = RING * i + u, u % 2
                wait(sp, oT_ready, PAIRS * (s - 1))
                sp.dma_start(v_ring[:, (u + 1) % RING, :],
                             v_d[bass.ds(s + 2, 1)][0]).then_inc(v_in[(u + 1) % RING], 16)
                n = s + GN if half == 0 else s - GN
                first = 0 if half == 0 else HC - SC
                rows = v_d.rearrange("n (r c) d -> (n r) c d", r=GR)[bass.ds(n * GR, 3 * GR), first:first + SC, :]
                sp.dma_start(v_side[b][0:SIDE, :], rows).then_inc(vs_in[b], 16)
                wait(sp, outb_ready, s - 1)
                if not (isinstance(s, int) and s < 2):
                    store(s - 2, b)
                sp.dma_start(sg[b][:], sg_d[bass.ds(s, 1)][0]).then_inc(sg_in[b], 16)

            def load_tables(half):
                sp.dma_start(mask[:, half], mask_d[:, half]).then_inc(tables_in[half], 16)
                sp.dma_start(raw_bias[:, half].rearrange("p n r c -> p n (r c)"),
                             bias_d[half, :, :, 0:3 * GR, :].rearrange("p n r c -> p n (r c)")
                             ).then_inc(tables_in[half], 16)

            load_tables(0)
            sp.wait_ge(k_mirrored, 1)
            for b in range(2):
                sp.dma_start(v_side[b][SIDE:P, :], vctx_d[0:P - SIDE, :]).then_inc(vctx_in, 16)
            sp.dma_start(v_ctx[:, 0, :], vctx_d[P - SIDE:2 * P - SIDE, :]).then_inc(vctx_in, 16)
            sp.wait_ge(consts, 6)
            sp.dma_start(v_ctx[0:SIDE, 1, :], vctx_d[2 * P - SIDE:CTX, :]).then_inc(vctx_in, 16)
            sp.dma_start(v_ring[:, 0, :], v_d[1]).then_inc(v_in[0], 16)
            HT = TURNS // 2
            for half in range(2):
                def turn(i, first, half=half):
                    for u in range(RING):
                        load_v(i, u, half)

                turn(half * HT, True)
                if half == 0:
                    load_tables(1)
                with sp.Fori(half * HT + 1, (half + 1) * HT) as i:
                    turn(i, False)
            for b in range(2):
                sp.wait_ge(outb_ready, STEPS - 1 + b)
                store(STEPS - 2 + b, b)
            for b in range(2):
                sp.wait_ge(outb_out[b], 16 * STEPS // 2)

        @block.gpsimd
        def _(pool):
            def load_k(seq, i, slot):
                wait(pool, scored, H * (seq - 2))
                if slot < MIRROR - RING:
                    wait(pool, k_mirrored, 2 * (i - 1) + slot + 1)
                pool.sem_inc(load_begun, 1)
                pool.dma_start(k_ring[:, :, slot * P:(slot + 1) * P],
                             kT_d[bass.ds(seq + 1, 1)][0].rearrange("s d h t -> (s d) h t")).then_inc(k_in[slot], 16)

            def load_q(i, u, half):
                s, b = RING * i + u, u % 2
                wait(pool, scored, H * (s - 1))
                pool.sem_inc(load_begun, 1)
                for n in range(2):
                    pool.dma_start(q[b][n * DH:(n + 1) * DH], qT_d[bass.ds(s, 1)][0]).then_inc(q_in[b], 16)
                n = s + GN if half == 0 else s - GN
                pool.dma_start(k_side[b][:, :, 0:SIDE],
                             kside_d[:, :, :, bass.ds(n, 3), :].rearrange("s d h g t -> (s d) h (g t)")
                             ).then_inc(side_in[b], 16)
                load_k(s + 1, i + (u + 1) // RING, (u + 1) % RING)

            def mirror(i, slot):
                pool.wait_ge(k_in[slot], 16 * (i + 1))
                pool.sem_inc(mirror_begun, 1)
                nc.gpsimd.tensor_copy(k_ring[:, :, (RING + slot) * P:(RING + slot + 1) * P],
                                      k_ring[:, :, slot * P:(slot + 1) * P]).then_inc(k_mirrored, 1)

            def gate(i, u):
                if isinstance(i, int) and i == 0 and u < 2:
                    return
                s, b, before = RING * i + u - 2, u % 2, 2 * i + u // 2 - 1
                pool.wait_ge(sg_in[b], 16 * (before + 1))
                wait(pool, outb_out[b], 16 * before)
                pool.wait_ge(divided, s + 1)
                nc.gpsimd.tensor_tensor(outb[b][:], sg[b][:], o_div[:], ALU.mult).then_inc(outb_ready, 1)

            made = [0]

            def make_bias(s, until):
                for n in range(H):
                    pool.wait_ge(added, H * (s - 1) + n + 1)
                    masked_bias(nc.gpsimd, s, n).then_inc(bias_made, 1)
                    made[0] += 1
                    pool.wait_ge(bias_made, made[0])
                    pool.sem_inc(bias_ready[n], until - s)

            load_k(0, 0, 0)
            load_q(0, 0, 0)
            nc.gpsimd.memset(k_ring[:, :, (RING - 1) * P:RING * P].bitcast(F32), 0.0).then_inc(consts, 1)
            nc.gpsimd.memset(v_ctx[:, 1, :], 0.0).then_inc(consts, 1)
            nc.gpsimd.memset(v_ring[:, RING - 1, :], 0.0).then_inc(consts, 1)
            nc.gpsimd.memset(bias[:, :, LAT:KEYS], 0.0).then_inc(consts, 1)
            for b in range(2):
                nc.gpsimd.memset(probs[b][:, KEYS:KCH * P], 0.0).then_inc(consts, 1)
            for b in range(2):
                pool.dma_start(k_side[b][:, :, SIDE:SIDECTX],
                               kctx_d.rearrange("s d h t -> (s d) h t")).then_inc(kctx_in, 16)
            HT = TURNS // 2
            for half in range(2):
                base, first = half * GN, half * HT
                for u in range(RING):
                    if half or u:
                        load_q(first, u, half)
                    if u == RING - 1:
                        mirror(first + 1, 0)
                    gate(first, u)
                    if half == 0 and u == 0:
                        mirror(0, 0)
                    if u == 0:
                        mirror(first, 1)
                        pool.wait_ge(tables_in[half], 32)
                        if half:
                            make_bias(base, base + 1)
                    if u == 1:
                        make_bias(base + 1, base + GN - 1)
                with pool.Fori(first + 1, first + HT - 1) as i:
                    for u in range(RING):
                        load_q(i, u, half)
                        if u == 0:
                            mirror(i, 1)
                        if u == RING - 1:
                            mirror(i + 1, 0)
                        gate(i, u)
                i = first + HT - 1
                for u in range(RING):
                    load_q(i, u, half)
                    if u == 0:
                        mirror(i, 1)
                    if u == RING - 1:
                        mirror(i + 1, 0)
                    gate(i, u)
                make_bias(base + GN - 1, base + GN)
            for u in range(2):
                gate(TURNS, u)

        @block.tensor
        def _(pe):
            pe.wait_ge(consts, 6)
            pe.wait_ge(kctx_in, 32)

            def score(i, u, n):
                s, b = RING * i + u, u % 2
                t = H * s + n
                if n == 0:
                    pe.wait_ge(q_in[b], 32 * (2 * i + u // 2 + 1))
                    pe.wait_ge(side_in[b], 16 * (2 * i + u // 2 + 1))
                    new = (u + 1) % RING
                    if new < MIRROR - RING:
                        pe.wait_ge(k_mirrored, 2 * (i + (u + 1) // RING) + new + 1)
                    else:
                        pe.wait_ge(k_in[new], 16 * (i + 1))
                wait(pe, added, t - 1)
                first = ((u + RING - 1) % RING) * P
                main = k_ring[:, n, first:first + MAIN]
                side = k_side[b][:, n, :]
                m = n % 2
                nc.tensor.matmul(p_scores[m][:, 0:MAIN], q[b][:, 0, n, :], main, start=True, stop=False)
                nc.tensor.matmul(p_scores[m][:, 0:MAIN], q[b][:, 1, n, :], main, start=False, stop=True)
                nc.tensor.matmul(p_scores[m][:, MAIN:KEYS], q[b][:, 0, n, :], side, start=True, stop=False)
                nc.tensor.matmul(p_scores[m][:, MAIN:KEYS], q[b][:, 1, n, :], side, start=False,
                                 stop=True).then_inc(scored, 1)

            def transpose(i, u, n):
                t = H * (RING * i + u) + n
                pe.wait_ge(exped, t + 1)
                wait(pe, pT4_copied, t)
                wait(pe, pT2_copied, t)
                for j in range(KCH):
                    bank, at = (p_pT4, j) if j < 4 else (p_pT2, j - 4)
                    last = nc.tensor.transpose(bank[:, at * P:(at + 1) * P], probs[n % 2][:, j * P:(j + 1) * P],
                                               ident[:])
                last.then_inc(pT_ready, 1)

            def values(i, u, a, second):
                s, b = RING * i + u, u % 2
                t = H * s + 2 * a
                if a == 0 and not second:
                    pe.wait_ge(v_in[(u + 1) % RING], 16 * (i + (u + 1) // RING + 1))
                    pe.wait_ge(vs_in[b], 16 * (2 * i + u // 2 + 1))
                    if isinstance(i, int) and i == 0 and u == 0:
                        pe.wait_ge(v_in[0], 16)
                        pe.wait_ge(vctx_in, 64)
                if not second:
                    pe.wait_ge(pT4_copied, t + 2)
                    pe.wait_ge(pT2_copied, t + 2)
                    wait(pe, oT_copied, PAIRS * s + a)
                for j in range(KCH // 2, KCH) if second else range(KCH // 2):
                    v = (v_ring[:, (u + RING - 1 + j) % RING, :] if j < 3 else
                         v_side[b][:] if j == 3 else v_ctx[:, j - 4, :])
                    for k in range(2):
                        n = 2 * a + k
                        last = nc.tensor.matmul(p_oT[k * DH:(k + 1) * DH, a * P:(a + 1) * P],
                                                v[:, n * DH:(n + 1) * DH], pT[:, n % 4, j * P:(j + 1) * P],
                                                start=(j == 0), stop=(j == KCH - 1))
                if second:
                    last.then_inc(oT_ready, 1)

            def untranspose(i, u, a):
                s = RING * i + u
                pe.wait_ge(oT_copied, PAIRS * s + a + 1)
                if a == 0:
                    wait(pe, divided, s)
                nc.tensor.transpose(p_o[:, a * P:(a + 1) * P], oT[a % 2][:], ident[:]).then_inc(o_ready, 1)

            def slot(i, u, n, live):
                if live:
                    score(i, u, n)
                t2 = back(i, u, n, T_LAG)
                if t2 and (live or n < T_LAG):
                    transpose(*t2)
                lag = PV_LAG - 1 + n % 2
                pv = back(i, u, n, lag)
                if pv and (live or n < lag):
                    values(pv[0], pv[1], pv[2] // 2, n % 2)
                o = back(i, u, n, O_LAG)
                if n % 2 and o and (live or n < O_LAG):
                    untranspose(o[0], o[1], o[2] // 2)

            run(pe, slot)

        @block.scalar
        def _(act):
            def copy_pT(i, u, n):
                t = H * (RING * i + u) + n
                act.wait_ge(pT_ready, t + 1)
                wait(act, oT_ready, PAIRS * (RING * i + u) + n // 2 - 1)
                nc.scalar.activation(pT[:, n % 4, 0:4 * P], p_pT4[:], ACT.Copy).then_inc(pT4_copied, 1)

            def softmax(i, u, n):
                s, b = RING * i + u, n % 2
                t = H * s + n
                act.wait_ge(added, t + 1)
                wait(act, pT_ready, t - 1)
                if n == 0:
                    wait(act, divided, s - 1)
                if isinstance(i, int) and i == 0 and u == 0 and n == 0:
                    act.wait_ge(consts, 6)
                nc.scalar.activation(probs[b][:, 0:KEYS], scores[b][:], ACT.Exp, scale=-1.0, bias=least[:, b:b + 1],
                                     accum_out=den[:, u % 2, n:n + 1]).then_inc(exped, 1)

            def copy_oT(i, u, a):
                m = PAIRS * (RING * i + u) + a
                act.wait_ge(oT_ready, m + 1)
                wait(act, o_ready, m - 1)
                nc.scalar.activation(oT[a % 2][:], p_oT[:, a * P:(a + 1) * P], ACT.Copy,
                                     scale=0.5).then_inc(oT_copied, 1)

            def slot(i, u, n, live):
                t2 = back(i, u, n, T_LAG)
                if t2 and (live or n < T_LAG):
                    copy_pT(*t2)
                if live:
                    softmax(i, u, n)
                pv, o = back(i, u, n, PV_LAG), back(i, u, n, O_LAG)
                if n % 2 and pv and (live or n < PV_LAG):
                    copy_oT(pv[0], pv[1], pv[2] // 2)

            run(act, slot)

        @block.vector
        def _(dve):
            def add_bias(i, u, n):
                s, b = RING * i + u, n % 2
                t = H * s + n
                if isinstance(i, int) and t == 0:
                    dve.wait_ge(consts, 6)
                dve.wait_ge(scored, t + 1)
                dve.wait_ge(bias_ready[n], s + 1)
                wait(dve, exped, t - 1)
                dve.sem_inc(add_begun, 1)
                nc.vector.tensor_tensor_reduce(
                    out=scores[b][:], in0=p_scores[b], in1=bias[:, n, :], scale=1.0, scalar=HIGHEST,
                    op0=ALU.add, op1=ALU.min, accum_out=least[:, b:b + 1]).then_inc(added, 1)

            def copy_pT(i, u, n):
                t = H * (RING * i + u) + n
                dve.wait_ge(pT_ready, t + 1)
                wait(dve, oT_ready, PAIRS * (RING * i + u) + n // 2 - 1)
                nc.vector.tensor_copy(pT[:, n % 4, 4 * P:KCH * P], p_pT2[:, 0:2 * P]).then_inc(pT2_copied, 1)

            def divide(i, u):
                s, b = RING * i + u, u % 2
                dve.wait_ge(exped, H * (s + 1))
                wait(dve, divided, s)
                nc.vector.reciprocal(rden[:], den[:, b, :]).then_inc(recip_ready, 1)
                dve.wait_ge(recip_ready, s + 1)
                dve.wait_ge(o_ready, PAIRS * (s + 1))
                wait(dve, outb_ready, s)
                nc.vector.tensor_tensor(o_div[:].rearrange("p (h d) -> p h d", h=H),
                                        p_o[:].rearrange("p (h d) -> p h d", h=H),
                                        rden[:].unsqueeze(2).to_broadcast([P, H, DH]), ALU.mult).then_inc(divided, 1)

            def slot(i, u, n, live):
                if live:
                    add_bias(i, u, n)
                t2 = back(i, u, n, T_LAG)
                if t2 and (live or n < T_LAG):
                    copy_pT(*t2)
                if n == O_LAG - 1 and back(i, u, n, H):
                    divide(*back(i, u, n, H)[0:2])

            dve.wait_ge(tables_in[0], 32)
            for n in range(H):
                masked_bias(nc.vector, 0, n).then_inc(bias_ready[n], 1)
            run(dve, slot)


def combine(nc, ident, gate_bc, x2, w_out, outa_d, outb_d, out2):
    with nc.cleanup_on_exit(), ExitStack() as cx:
        sb = lambda n, s, d=F32: cx.enter_context(nc.sbuf_tensor("com_" + n, s, d))
        ps = lambda n, s: cx.enter_context(nc.psum_tensor("com_" + n, s, F32))
        sem = lambda n: nc.alloc_semaphore("com_" + n)
        w = SplitWeights(nc, cx, "wo", w_out[0], [0, 512])
        mix = [sb(f"mix{k}", [P, D]) for k in range(2)]
        xt = [sb(f"xr{k}", [P, D]) for k in range(2)]
        hi = [sb(f"mixT_hi{k}", [P, KT, P], F32R) for k in range(2)]
        lo = [sb(f"mixT_lo{k}", [P, KT, P], F32R) for k in range(2)]
        gated = sb("out_gated", [P, D])
        result = [sb(f"result{k}", [P, D]) for k in range(2)]
        p_t = [ps(f"p_mixT{k}", [P, KT, P]) for k in range(2)]
        p_o = [ps(f"p_out{k}", [P, 512]) for k in range(4)]
        mix_in = [sem(f"mix_in{k}") for k in range(2)]
        x_in = [sem(f"xr_in{k}") for k in range(2)]
        transposed, hi_ready, split_ready = sem("mix_transposed"), sem("mix_hi"), sem("mix_split")
        product = sem("product")
        gated_ready, result_ready = sem("out_gated_ready"), sem("result_ready")
        out_out = [sem(f"out_out{k}") for k in range(2)]
        block = cx.enter_context(nc.Block())
        PT = TILES // 2

        @block.sync
        def _(sp):
            def load_mix(i, u):
                sp.dma_start(mix[u][:, 0:DA], outa_d[bass.ds((2 * i + u) * P, P), :]).then_inc(mix_in[u], 16)
                for half in range(2):
                    for r in range(2):
                        src = outb_d[bass.ds(i + half * GN, 1)][0]
                        row = (2 * u + r) * HC
                        sp.dma_start(mix[u][r * GW + half * HC:r * GW + (half + 1) * HC, DA:D],
                                     src[row:row + HC, :]).then_inc(mix_in[u], 16)

            def load_x(i, u):
                sp.dma_start(xt[u][:], x2[bass.ds((2 * i + u) * P, P), :]).then_inc(x_in[u], 16)

            for u in range(2):
                load_mix(0, u)
            w.load(sp)
            for u in range(2):
                load_x(0, u)

            def tile(i, u, more):
                t = 2 * i + u
                if more:
                    sp.wait_ge(transposed, t + 1)
                    load_mix(i + 1, u)
                sp.wait_ge(result_ready, t + 1)
                sp.dma_start(out2[bass.ds(t * P, P), :], result[u][:]).then_inc(out_out[u], 16)
                if more:
                    load_x(i + 1, u)

            with sp.Fori(0, PT - 1) as i:
                for u in range(2):
                    tile(i, u, True)
            for u in range(2):
                tile(PT - 1, u, False)
            for u in range(2):
                sp.wait_ge(out_out[u], 16 * PT)

        def tiles(e, tile):
            for u in range(2):
                tile(0, u, True)
            with e.Fori(1, PT - 1) as i:
                for u in range(2):
                    tile(i, u, True)
            for u in range(2):
                tile(PT - 1, u, u == 0)

        @block.scalar
        def _(act):
            def round_hi(i, u):
                t = 2 * i + u
                act.wait_ge(transposed, t + 1)
                wait(act, product, 2 * (t - 1))
                nc.scalar.activation(hi[u][:], p_t[u][:], ACT.Copy).then_inc(hi_ready, 1)

            round_hi(0, 0)
            w.round_hi(act)

            def tile(i, u, more):
                if more:
                    round_hi(i + (u + 1) // 2, (u + 1) % 2)

            tiles(act, tile)

        @block.tensor
        def _(pe):
            def transpose(i, u):
                t = 2 * i + u
                pe.wait_ge(mix_in[u], 80 * (i + 1))
                wait(pe, split_ready, t - 1)
                for k in range(KT):
                    last = nc.tensor.transpose(p_t[u][:, k, :], mix[u][:, k * P:(k + 1) * P], ident[:])
                last.then_inc(transposed, 1)

            transpose(0, 0)

            def tile(i, u, more):
                t = 2 * i + u
                pe.wait_ge(split_ready, t + 1)
                for n in range(2):
                    bank, c = p_o[2 * u + n], slice(n * 512, (n + 1) * 512)
                    wait(pe, gated_ready, 2 * (t - 2) + n + 1)
                    if isinstance(t, int) and t == 0:
                        w.ready(pe, n * 512)
                    for k in range(KT):
                        nc.tensor.matmul(bank[:], hi[u][:, k, :], w.hi[:, k, c], start=(k == 0), stop=False)
                        nc.tensor.matmul(bank[:], hi[u][:, k, :], w.lo[:, k, c], start=False, stop=False)
                        last = nc.tensor.matmul(bank[:], lo[u][:, k, :], w.hi[:, k, c], start=False,
                                                stop=(k == KT - 1))
                    last.then_inc(product, 1)
                    if n == 0 and more:
                        transpose(i + (u + 1) // 2, (u + 1) % 2)

            tiles(pe, tile)

        @block.vector
        def _(dve):
            def take_lo(i, u):
                t = 2 * i + u
                dve.wait_ge(hi_ready, t + 1)
                nc.vector.tensor_tensor(lo[u][:], p_t[u][:], hi[u][:].bitcast(F32),
                                        ALU.subtract).then_inc(split_ready, 1)

            take_lo(0, 0)
            w.take_lo(dve)

            def tile(i, u, more):
                t = 2 * i + u
                if more:
                    take_lo(i + (u + 1) // 2, (u + 1) % 2)
                wait(dve, result_ready, t)
                for n in range(2):
                    c = slice(n * 512, (n + 1) * 512)
                    dve.wait_ge(product, 2 * t + n + 1)
                    nc.vector.tensor_tensor(gated[:, c], p_o[2 * u + n][:], gate_bc[:, c],
                                            ALU.mult).then_inc(gated_ready, 1)
                dve.wait_ge(gated_ready, 2 * t + 2)
                dve.wait_ge(x_in[u], 16 * (i + 1))
                wait(dve, out_out[u], 16 * i)
                nc.vector.tensor_tensor(result[u][:], gated[:], xt[u][:], ALU.add).then_inc(result_ready, 1)

            tiles(dve, tile)


_INS = ["x", "c", "ctx", "c_ctx", "w_ada", "b_ada", "norm_g", "w_in", "sgu_norm_g", "w_spatial", "b_spatial",
        "q_norm_g", "k_norm_g", "rpb", "w_out"]


def kernel(**inputs):
    import numpy as np
    from concourse import bacc
    from concourse.bass_utils import run_bass_kernel_spmd

    nc = bacc.Bacc("TRN2", target_bir_lowering=False, num_devices=1)
    arrays, args = {}, []
    for name in _INS:
        a = np.ascontiguousarray(inputs[name])
        arrays[f"in_{name}"] = a
        args.append(nc.dram_tensor(f"in_{name}", a.shape, mybir.dt.from_np(a.dtype), kind="ExternalInput").ap())
    args.append(nc.dram_tensor("out_x", inputs["x"].shape, F32, kind="ExternalOutput").ap())
    build(nc, *args)
    r = run_bass_kernel_spmd(nc, [arrays], core_ids=[0])
    return r.results[0]["out_x"]
```

```python
import concourse.bass as bass
from concourse import mybir
from contextlib import ExitStack

F32 = mybir.dt.float32
F32R = mybir.dt.float32r
ACT = mybir.ActivationFunctionType
ALU = mybir.AluOpType
AX = mybir.AxisListType

P = 128
D = 1024
KT = D // P
L = 4096
CTX = 256
DA = 512
GROUPS = 4
H = 8
DH = 64
PAIRS = H // 2
GW = 64
GR = 4
HC = 32
GN = L // (GR * GW)
TILES = L // P
WR, WC = 8, 16
RPR, RPC = 2 * WR - 1, 2 * WC - 1
SC = 8
MAIN = 3 * P
SIDE = 3 * GR * SC
LAT = MAIN + SIDE
KEYS = LAT + CTX
SIDECTX = SIDE + CTX
KCH = 6
RING = 4
MIRROR = RING + 2
EPS = 1e-6
MASKED = 1e30
HIGHEST = 3.0e38
PAD, PAD_END = 64, 192
MODS = 3 * D
U_A, V_A, G_A, Q_B, K_B, V_B, G_B = range(0, 7 * DA, DA)


def place(head):
    return head % 2 * PAIRS + head // 2


def wait(e, sem, count):
    if not (isinstance(count, int) and count <= 0):
        e.wait_ge(sem, count)


def build(nc, x, c, ctx_in, c_ctx, w_ada, b_ada, norm_g, w_in, sgu_norm_g, w_spatial, b_spatial,
          q_norm_g, k_norm_g, rpb, w_out, out):
    x2, ctx2, out2 = x[0], ctx_in[0], out[0]
    with ExitStack() as top:
        def dram(name, shape, dt=F32):
            return nc.dram_tensor(name, shape, dt, kind="Internal").ap()

        outa_d = dram("outa_d", [L, DA])
        outb_d = dram("outb_d", [TILES, P, DA])
        kT_d = dram("kT_d", [TILES + 2, 2, DH, H, P], F32R)
        v_d = dram("v_d", [TILES + 2, P, DA])
        kside_d = dram("kside_d", [2, DH, H, TILES + 2, GR * SC], F32R)
        qT_d = dram("qT_d", [TILES, DH, 2, H, P], F32R)
        sg_d = dram("sg_d", [TILES, P, DA])
        kctx_d = dram("kctx_d", [2, DH, H, CTX], F32R)
        vctx_d = dram("vctx_d", [CTX, DA])
        rpbpad_d = dram("rpbpad_d", [1, PAD + H * RPR * RPC + PAD_END])
        bias_d = dram("bias_d", [2, P, H, RPR, HC + SC])
        mask_d = dram("mask_d", [P, 2, 3, LAT])

        def sbt(name, shape, dt=F32):
            return top.enter_context(nc.sbuf_tensor(name, shape, dt))

        ident = sbt("ident", [P, P])
        a_col = sbt("a_col", [P, 2, KT])
        b_col = sbt("b_col", [P, 2, KT])
        gate_bc = sbt("gate_bc", [P, D])

        with nc.cleanup_on_exit(), ExitStack() as cx:
            h = NormedInput(nc, cx, "x", ident)
            w = SplitWeights(nc, cx, "w", w_in[0], 3)
            shared = [w.buffers(cx, f"shared{k}") for k in range(2)]
            w.block(V_A, shared[0])
            modulate(nc, ident, a_col, b_col, gate_bc, x2, c, c_ctx, w_ada, b_ada, norm_g, rpb,
                     rpbpad_d, mask_d, kT_d, v_d, kside_d, h, w)
            gating(nc, ident, a_col, b_col, x2, ctx2, h, w, shared[1], sgu_norm_g, w_spatial, b_spatial, outa_d,
                   rpbpad_d, bias_d)
            project(nc, ident, a_col, b_col, x2, h, w, shared[0], q_norm_g, k_norm_g,
                    qT_d, kT_d, v_d, kside_d, sg_d, kctx_d, vctx_d)
        attend(nc, ident, qT_d, kT_d, v_d, kside_d, sg_d, kctx_d, vctx_d, bias_d, mask_d, outb_d)
        combine(nc, ident, gate_bc, x2, w_out, outa_d, outb_d, out2)


def modulate(nc, ident, a_col, b_col, gate_bc, x2, c, c_ctx, w_ada, b_ada, norm_g, rpb,
             rpbpad_d, mask_d, kT_d, v_d, kside_d, h, w):
    NB = MODS // 512
    ROWS = 6 * KT
    with nc.cleanup_on_exit(), ExitStack() as cx:
        sb = lambda n, s, d=F32: cx.enter_context(nc.sbuf_tensor("mod_" + n, s, d))
        ps = lambda n, s: cx.enter_context(nc.psum_tensor("mod_" + n, s, F32))
        sem = lambda n: nc.alloc_semaphore("mod_" + n)
        rows = sb("rows", [ROWS, P])
        cols = sb("cols", [P, ROWS])
        cth = sb("cth", [P, 2 * KT])
        csum = sb("csum", [P, 2 * KT])
        cond = sb("cond", [P, 2 * KT])
        wada = [sb(f"wada{k}", [P, MODS]) for k in range(4)]
        mod = sb("mod", [2, MODS])
        gate_col = sb("gate_col", [P, KT])
        gate_wide = sb("gate_wide", [P, KT, P])
        scale1 = sb("scale1", [P, 2, KT])
        scale2 = sb("scale2", [P, 2, KT])
        rpb_raw = sb("rpb_raw", [H, RPR * RPC])
        rpb_minus = sb("rpb_minus", [H, RPR * RPC])
        masks = sb("masks", [P, 2, 3, LAT])
        zeros = sb("zeros", [P, D])
        p_rows = [ps(f"p_rows{n}", [P, 512]) for n in range(NB)]
        p_cols = p_rows[NB - 1][:, 0:ROWS]
        p_mod_cols = p_rows[0][:, 0:2 * MODS // P]
        p_mod = p_mod_cols.rearrange("p (j k s) -> p j s k", j=3, s=2)
        p_gate = p_rows[1:3]

        rows_in = sem("rows_in")
        wada_in = [sem(f"wada_in{k}") for k in range(4)]
        wada_used = sem("wada_used")
        ident_ready = sem("ident_ready")
        cols_t = sem("cols_t")
        cols_ready = sem("cols_ready")
        cth_ready = sem("cth_ready")
        csum_ready = sem("csum_ready")
        cond_ready = sem("cond_ready")
        mod_copied = [sem(f"mod_copied{k}") for k in range(2)]
        modcols_t = sem("modcols_t")
        cols_made = sem("cols_made")
        scale_step = sem("scale_step")
        gate_added, gate_widened, gate_p = sem("gate_added"), sem("gate_widened"), sem("gate_p")
        rpb_in = sem("rpb_in")
        rpb_turned = sem("rpb_turned")
        mask_step = sem("mask_step")
        masks_ready = sem("masks_ready")
        zeros_ready = sem("zeros_ready")
        side_out = sem("side_out")
        block = cx.enter_context(nc.Block())

        @block.sync
        def _(sp):
            sp.dma_start(rows[0:KT, :], c.rearrange("b (k p) -> (b k) p", p=P)).then_inc(rows_in, 16)
            sp.dma_start(rows[KT:2 * KT, :], c_ctx.rearrange("(k p) -> k p", p=P)).then_inc(rows_in, 16)
            sp.dma_start(rows[2 * KT:3 * KT, :], norm_g.rearrange("b (k p) -> (b k) p", p=P)).then_inc(rows_in, 16)
            sp.dma_start(rows[3 * KT:6 * KT, :], b_ada.rearrange("b (k p) -> (b k) p", p=P)).then_inc(rows_in, 16)
            for k in range(KT):
                if k >= 4:
                    sp.wait_ge(wada_used, k - 3)
                sp.dma_start(wada[k % 4][:], w_ada[0, k * P:(k + 1) * P, :]).then_inc(wada_in[k % 4], 16)
            for u in range(2):
                sp.dma_start(h.xt[u][:], x2[u * P:(u + 1) * P, :]).then_inc(h.x_in[u], 16)
            w.load(sp, V_A)

        @block.scalar
        def _(act):
            act.wait_ge(zeros_ready, 1)
            for n in (0, TILES + 1):
                act.dma_start(kT_d[n].rearrange("s d h t -> (s d) (h t)").bitcast(F32),
                              zeros[:]).then_inc(side_out, 16)
                act.dma_start(v_d[n], zeros[:, 0:DA]).then_inc(side_out, 16)
                act.dma_start(kside_d[:, :, :, n, :].rearrange("s d h t -> (s d) h t").bitcast(F32),
                              zeros[:, 0:H * GR * SC].rearrange("p (h t) -> p h t", h=H)).then_inc(side_out, 16)
            act.dma_start(rpb_raw[:], rpb[0].rearrange("h r c -> h (r c)")).then_inc(rpb_in, 16)
            act.wait_ge(cols_ready, 1)
            nc.scalar.activation(cth[:], cols[:, 0:2 * KT], ACT.Tanh, scale=0.5).then_inc(cth_ready, 1)
            act.wait_ge(rpb_in, 16)
            nc.scalar.activation(rpb_minus[:], rpb_raw[:], ACT.Copy, scale=-1.0).then_inc(rpb_turned, 1)
            act.wait_ge(rpb_turned, 1)
            end = PAD + H * RPR * RPC
            act.dma_start(rpbpad_d[0, PAD:end].rearrange("(h x) -> h x", h=H), rpb_minus[:]).then_inc(side_out, 16)
            act.dma_start(rpbpad_d[:, 0:PAD], zeros[0:1, 0:PAD]).then_inc(side_out, 16)
            act.dma_start(rpbpad_d[:, end:end + PAD_END], zeros[0:1, 0:PAD_END]).then_inc(side_out, 16)
            act.wait_ge(masks_ready, 1)
            act.dma_start(mask_d, masks[:]).then_inc(side_out, 16)
            h.square(act, 0, 0)
            w.round_hi(act, V_A, slice(0, 2))
            act.wait_ge(wada_used, KT)
            for n in range(NB // 2, NB):
                last = nc.scalar.activation(mod[:, n * 512:(n + 1) * 512], p_rows[n][0:2], ACT.Copy)
            last.then_inc(mod_copied[1], 1)
            act.wait_ge(cols_made, 1)
            h.modulate(act, 0, 0, a_col[:, 0, :], b_col[:, 0, :])
            w.round_hi(act, V_A, slice(2, 4))
            act.wait_ge(side_out, 10 * 16)

        @block.gpsimd
        def _(pool):
            nc.gpsimd.memset(ident[:], 0.0).then_inc(ident_ready, 1)
            nc.gpsimd.memset(h.minus_half[:], -0.5).then_inc(h.half_ready, 1)
            pool.wait_ge(ident_ready, 1)
            nc.gpsimd.affine_select(out=ident[:], in_=ident[:], compare_op=ALU.not_equal, fill=1.0, base=0,
                                    pattern=[[-1, P]], channel_multiplier=1).then_inc(ident_ready, 1)
            nc.gpsimd.memset(zeros[:], 0.0).then_inc(zeros_ready, 1)
            step = 1
            nc.gpsimd.memset(masks[:], 0.0).then_inc(mask_step, 1)
            for half in range(2):
                for qr in range(GR):
                    q = slice(qr * HC, (qr + 1) * HC)
                    at_main, at_side = (0, HC), (MAIN, SC)

                    def keep(part, lo, hi, compare, base, mult, patt):
                        first, width = part
                        for edge in range(3):
                            view = masks[q, half, edge, first:first + 3 * GR * width].rearrange(
                                "p (r c) -> p r c", c=width)[:, :, lo:hi]
                            nc.gpsimd.affine_select(out=view, in_=view, compare_op=compare, fill=MASKED, base=base,
                                                    pattern=[[0, 3 * GR], [patt, hi - lo]],
                                                    channel_multiplier=mult).then_inc(mask_step, 1)

                    pool.wait_ge(mask_step, step)
                    if half == 0:
                        keep(at_main, 0, HC, ALU.is_ge, WC // 2, -1, 1)
                        pool.wait_ge(mask_step, step + 3)
                        keep(at_main, WC, HC, ALU.is_ge, WC // 2 - 1 - WC, 1, -1)
                        keep(at_side, 0, SC, ALU.is_ge, WC // 2 - 1 - HC, 1, -1)
                    else:
                        keep(at_main, 0, WC, ALU.is_ge, WC // 2, -1, 1)
                        pool.wait_ge(mask_step, step + 3)
                        keep(at_main, 0, HC, ALU.is_ge, WC // 2 - 1, 1, -1)
                        keep(at_side, 0, SC, ALU.is_ge, 0, -1, 1)
                    step += 9
                    pool.wait_ge(mask_step, step)
                    for edge, first in enumerate((GR, qr, 0)):
                        for lo, hi in ((0, first), (first + WR, 3 * GR)):
                            if lo < hi:
                                nc.gpsimd.memset(masks[q, half, edge, lo * HC:hi * HC], MASKED).then_inc(mask_step, 1)
                                nc.gpsimd.memset(masks[q, half, edge, MAIN + lo * SC:MAIN + hi * SC],
                                                 MASKED).then_inc(mask_step, 1)
                                step += 2
            pool.wait_ge(mask_step, step)
            pool.sem_inc(masks_ready, 1)
            pool.wait_ge(h.half_ready, 1)
            h.root(pool, 0, 0)

        @block.tensor
        def _(pe):
            pe.wait_ge(ident_ready, 2)
            pe.wait_ge(rows_in, 64)
            nc.tensor.transpose(p_cols, rows[:], ident[0:ROWS, 0:ROWS]).then_inc(cols_t, 1)
            pe.wait_ge(cond_ready, 1)
            cond3 = cond[:].rearrange("p (s k) -> p s k", s=2)
            for k in range(KT):
                pe.wait_ge(wada_in[k % 4], 16 * (k // 4 + 1))
                for n in range(NB):
                    last = nc.tensor.matmul(p_rows[n][0:2], cond3[:, :, k], wada[k % 4][:, n * 512:(n + 1) * 512],
                                            start=(k == 0), stop=(k == KT - 1))
                last.then_inc(wada_used, 1)
            for j in range(MODS // P):
                if j % (MODS // P // 2) == 0:
                    pe.wait_ge(mod_copied[2 * j // (MODS // P)], 1)
                last = nc.tensor.transpose(p_mod_cols[:, 2 * j:2 * j + 2], mod[:, j * P:(j + 1) * P], ident[0:2, 0:2])
            last.then_inc(modcols_t, 1)
            h.transpose(pe, 0, 0)
            pe.wait_ge(gate_widened, 1)
            for k in range(KT):
                last = nc.tensor.matmul(p_gate[k // 4][:, k % 4 * P:(k % 4 + 1) * P], gate_wide[:, k, :], ident[:],
                                        start=True, stop=True)
            last.then_inc(gate_p, 1)

        @block.vector
        def _(dve):
            dve.wait_ge(cols_t, 1)
            nc.vector.tensor_copy(cols[:], p_cols).then_inc(cols_ready, 1)
            dve.wait_ge(cth_ready, 1)
            nc.vector.tensor_scalar(csum[:], cth[:], 1.0, 0.5, ALU.add, ALU.mult).then_inc(csum_ready, 1)
            dve.wait_ge(csum_ready, 1)
            nc.vector.tensor_tensor(cond[:], csum[:], cols[:, 0:2 * KT], ALU.mult).then_inc(cond_ready, 1)
            h.mean(dve, 0, 0)
            h.normalise(dve, 0, 0)
            w.take_lo(dve, V_A, slice(0, 2))
            dve.wait_ge(wada_used, KT)
            for n in range(NB // 2):
                last = nc.vector.tensor_copy(mod[:, n * 512:(n + 1) * 512], p_rows[n][0:2])
            last.then_inc(mod_copied[0], 1)
            dve.wait_ge(modcols_t, 1)
            for s in range(2):
                nc.vector.tensor_tensor(b_col[:, s, :], p_mod[:, 0, s, :], cols[:, 3 * KT:4 * KT], ALU.add)
                nc.vector.tensor_tensor(scale1[:, s, :], p_mod[:, 1, s, :], cols[:, 4 * KT:5 * KT],
                                        ALU.add).then_inc(scale_step, 1)
            nc.vector.tensor_tensor(gate_col[:], p_mod[:, 2, 0, :], cols[:, 5 * KT:6 * KT],
                                    ALU.add).then_inc(gate_added, 1)
            dve.wait_ge(scale_step, 2)
            nc.vector.tensor_scalar(scale2[:], scale1[:], 1.0, None, ALU.add).then_inc(scale_step, 1)
            dve.wait_ge(scale_step, 3)
            for s in range(2):
                last = nc.vector.tensor_tensor(a_col[:, s, :], scale2[:, s, :], cols[:, 2 * KT:3 * KT], ALU.mult)
            last.then_inc(cols_made, 1)
            dve.wait_ge(gate_added, 1)
            nc.vector.tensor_copy(gate_wide[:], gate_col[:].unsqueeze(2).to_broadcast([P, KT, P])
                                  ).then_inc(gate_widened, 1)
            w.take_lo(dve, V_A, slice(2, 4))
            h.split(dve, 0, 0)
            dve.wait_ge(gate_p, 1)
            for n in range(2):
                nc.vector.tensor_copy(gate_bc[:, n * 512:(n + 1) * 512], p_gate[n][:])


class SplitWeights:
    PER_BLOCK = KT // 2

    def __init__(self, nc, cx, name, source, staged):
        self.nc, self.name, self.staged = nc, name, staged
        self.source = source.rearrange("(k p) n -> p k n", p=P)
        self.raw = [cx.enter_context(nc.sbuf_tensor(f"{name}_raw{k}", [P, 2, 512], F32)) for k in range(staged)]
        self.loaded = [nc.alloc_semaphore(f"{name}_loaded{k}") for k in range(staged)]
        self.hi_done = nc.alloc_semaphore(f"{name}_hi_done")
        self.lo_done = nc.alloc_semaphore(f"{name}_lo_done")
        self.number, self.hi, self.lo = {}, {}, {}

    def buffers(self, cx, name):
        return [cx.enter_context(self.nc.sbuf_tensor(f"{self.name}_{name}_{part}", [P, KT, 512], F32R))
                for part in ("hi", "lo")]

    def block(self, col, buffers):
        self.number[col] = len(self.number)
        self.hi[col], self.lo[col] = buffers

    def chunks(self, col, which=slice(None)):
        first = self.number[col] * self.PER_BLOCK
        return [(first + j, slice(2 * j, 2 * j + 2)) for j in range(self.PER_BLOCK)][which]

    def ready(self, pe, col):
        pe.wait_ge(self.lo_done, self.PER_BLOCK * (self.number[col] + 1))

    def load(self, dma, col):
        for n, k in self.chunks(col):
            if n >= self.staged:
                dma.wait_ge(self.lo_done, n - self.staged + 1)
            b = n % self.staged
            dma.dma_start(self.raw[b][:], self.source[:, k, col:col + 512]).then_inc(self.loaded[b], 16)

    def round_hi(self, act, col, which=slice(None)):
        for n, k in self.chunks(col, which):
            b = n % self.staged
            act.wait_ge(self.loaded[b], 16 * (n // self.staged + 1))
            self.nc.scalar.activation(self.hi[col][:, k], self.raw[b][:], ACT.Copy).then_inc(self.hi_done, 1)

    def take_lo(self, dve, col, which=slice(None)):
        for n, k in self.chunks(col, which):
            dve.wait_ge(self.hi_done, n + 1)
            self.nc.vector.tensor_tensor(self.lo[col][:, k], self.raw[n % self.staged][:],
                                         self.hi[col][:, k].bitcast(F32), ALU.subtract).then_inc(self.lo_done, 1)


def split_products(nc, bank, hi, lo, weights, col):
    w_hi, w_lo = weights.hi[col], weights.lo[col]
    for k in range(KT):
        nc.tensor.matmul(bank, hi[:, k, :], w_hi[:, k, :], start=(k == 0), stop=False)
        nc.tensor.matmul(bank, hi[:, k, :], w_lo[:, k, :], start=False, stop=False)
        last = nc.tensor.matmul(bank, lo[:, k, :], w_hi[:, k, :], start=False, stop=(k == KT - 1))
    return last


class NormedInput:

    def __init__(self, nc, cx, stage, ident):
        self.nc, self.ident = nc, ident
        sb = lambda n, s, d=F32: cx.enter_context(nc.sbuf_tensor(f"{stage}_{n}", s, d))
        sem = lambda n: nc.alloc_semaphore(f"{stage}_{n}")
        self.xt = [sb(f"xt{k}", [P, D]) for k in range(2)]
        self.sumsq = sb("x_sumsq", [P, 2])
        self.meansq = sb("x_meansq", [P, 2])
        self.rstd = sb("x_rstd", [P, 2])
        self.minus_half = sb("minus_half", [P, 2 * H])
        self.normed = sb("x_normed", [P, D])
        self.hT = sb("hT", [P, KT, P])
        self.hi = [sb(f"hT_hi{k}", [P, KT, P], F32R) for k in range(2)]
        self.lo = [sb(f"hT_lo{k}", [P, KT, P], F32R) for k in range(2)]
        self.p_t = cx.enter_context(nc.psum_tensor(f"{stage}_p_hT", [P, KT, P], F32))
        self.x_in = [sem(f"x_in{k}") for k in range(2)]
        self.half_ready = sem("half_ready")
        self.sumsq_ready = sem("sumsq_ready")
        self.meansq_ready = sem("meansq_ready")
        self.rstd_ready = sem("rstd_ready")
        self.normed_ready = sem("normed_ready")
        self.transposed = sem("transposed")
        self.modulated = sem("modulated")
        self.hi_ready = sem("hi_ready")
        self.split_ready = sem("split_ready")
        self.tile_done = sem("tile_done")

    def square(self, act, i, u):
        t = 2 * i + u
        act.wait_ge(self.x_in[u], 16 * (i + 1))
        wait(act, self.meansq_ready, t - 1)
        wait(act, self.split_ready, t)
        self.nc.scalar.activation(self.hT[:].rearrange("p k c -> p (k c)"), self.xt[u][:], ACT.Square,
                                  accum_out=self.sumsq[:, u:u + 1]).then_inc(self.sumsq_ready, 1)

    def mean(self, dve, i, u):
        t = 2 * i + u
        dve.wait_ge(self.sumsq_ready, t + 1)
        wait(dve, self.rstd_ready, t - 1)
        self.nc.vector.tensor_scalar(self.meansq[:, u:u + 1], self.sumsq[:, u:u + 1], 1.0 / D, EPS,
                                     ALU.mult, ALU.add).then_inc(self.meansq_ready, 1)

    def root(self, pool, i, u):
        t = 2 * i + u
        pool.wait_ge(self.meansq_ready, t + 1)
        wait(pool, self.normed_ready, t - 1)
        self.nc.gpsimd.tensor_tensor(self.rstd[:, u:u + 1], self.meansq[:, u:u + 1], self.minus_half[:, 0:1],
                                     ALU.pow).then_inc(self.rstd_ready, 1)

    def normalise(self, dve, i, u):
        t = 2 * i + u
        dve.wait_ge(self.rstd_ready, t + 1)
        wait(dve, self.transposed, t)
        self.nc.vector.tensor_scalar(self.normed[:], self.xt[u][:], self.rstd[:, u:u + 1], None,
                                     ALU.mult).then_inc(self.normed_ready, 1)

    def transpose(self, pe, i, u):
        t = 2 * i + u
        pe.wait_ge(self.normed_ready, t + 1)
        wait(pe, self.modulated, t)
        for k in range(KT):
            last = self.nc.tensor.transpose(self.p_t[:, k, :], self.normed[:, k * P:(k + 1) * P], self.ident[:])
        last.then_inc(self.transposed, 1)

    def modulate(self, act, i, u, a_col, b_col):
        t = 2 * i + u
        act.wait_ge(self.transposed, t + 1)
        act.wait_ge(self.sumsq_ready, t + 1)
        for k in range(KT):
            last = self.nc.scalar.activation(self.hT[:, k, :], self.p_t[:, k, :], ACT.Identity,
                                             scale=a_col[:, k:k + 1], bias=b_col[:, k:k + 1])
        last.then_inc(self.modulated, 1)

    def split(self, dve, i, u):
        t = 2 * i + u
        dve.wait_ge(self.modulated, t + 1)
        wait(dve, self.tile_done, t - 1)
        self.nc.vector.tensor_copy(self.hi[u][:], self.hT[:]).then_inc(self.hi_ready, 1)
        dve.wait_ge(self.hi_ready, t + 1)
        self.nc.vector.tensor_tensor(self.lo[u][:], self.hT[:], self.hi[u][:].bitcast(F32),
                                     ALU.subtract).then_inc(self.split_ready, 1)

    def products(self, u, bank, weights, col):
        return split_products(self.nc, bank, self.hi[u], self.lo[u], weights, col)


def gating(nc, ident, a_col, b_col, x2, ctx2, h, w, k_buffers, sgu_norm_g, w_spatial, b_spatial, outa_d,
           rpbpad_d, bias_d):
    CH = DA // GROUPS
    with nc.cleanup_on_exit(), ExitStack() as cx:
        sb = lambda n, s, d=F32: cx.enter_context(nc.sbuf_tensor("sgu_" + n, s, d))
        ps = lambda n, s: cx.enter_context(nc.psum_tensor("sgu_" + n, s, F32))
        sem = lambda n: nc.alloc_semaphore("sgu_" + n)
        w.block(U_A, w.buffers(cx, "u"))
        w.block(G_A, w.buffers(cx, "g"))
        w.block(K_B, k_buffers)
        ws_raw = sb("ws_raw", [P, GROUPS, P])
        wsT = sb("wsT", [P, GROUPS, P])
        bs_raw = sb("bs_raw", [GROUPS, P])
        bs = sb("bs", [P, GROUPS])
        sgu_bc = sb("sgu_bc", [P, DA])
        v_act = sb("v_act", [P, DA])
        v_squares = sb("v_squares", [P, DA])
        v_sumsq = sb("v_sumsq", [P, GROUPS])
        v_meansq = sb("v_meansq", [P, GROUPS])
        v_rstd = sb("v_rstd", [P, GROUPS])
        v_normed = sb("v_normed", [P, DA])
        u_act = sb("u_act", [P, DA])
        g_tanh = sb("g_tanh", [P, DA])
        g_silu2 = sb("g_silu2", [P, DA])
        gated = sb("gated", [P, DA])
        outa = [sb(f"outa{k}", [P, DA]) for k in range(2)]
        p_v, p_u, p_g, p_mix = ps("p_v", [P, DA]), ps("p_u", [P, DA]), ps("p_g", [P, DA]), ps("p_mix", [P, DA])

        small_in = sem("small_in")
        ws_t = sem("ws_t")
        ws_ready = sem("ws_ready")
        bias_out = sem("bias_out")
        v_ready, u_ready = sem("v_ready"), sem("u_ready")
        g_ready = h.tile_done
        v_gelu, u_gelu, g_tanh_ready = sem("v_gelu"), sem("u_gelu"), sem("g_tanh_ready")
        v_sumsq_ready, v_meansq_ready, v_rstd_ready = sem("v_ssq"), sem("v_msq"), sem("v_rstd_ready")
        v_normed_ready = sem("v_normed_ready")
        mix_ready = sem("mix_ready")
        silu_ready = sem("silu_ready")
        gated_ready = sem("gated_ready")
        outa_ready = sem("outa_ready")
        outa_out = [sem(f"outa_out{k}") for k in range(2)]
        block = cx.enter_context(nc.Block())
        PT = TILES // 2

        def load_x(dma, i, u):
            last = isinstance(i, int) and i == PT
            src = ctx2[u * P:(u + 1) * P, :] if last else x2[bass.ds((2 * i + u) * P, P), :]
            dma.dma_start(h.xt[u][:], src).then_inc(h.x_in[u], 16)

        def tiles(e, tile):
            for u in range(2):
                tile(0, u)
            with e.Fori(1, PT - 1) as i:
                for u in range(2):
                    tile(i, u)
            for u in range(2):
                tile(PT - 1, u)

        def columns(i):
            return 1 if isinstance(i, int) and i == PT else 0

        @block.sync
        def _(sp):
            w.load(sp, U_A)
            w.load(sp, G_A)

            def tile(i, u):
                t = 2 * i + u
                sp.wait_ge(h.normed_ready, t + 1)
                load_x(sp, i + 1, u)
                if isinstance(i, int) and (i, u) == (PT - 1, 0):
                    w.load(sp, K_B)
                sp.wait_ge(outa_ready, t + 1)
                sp.dma_start(outa_d[bass.ds(t * P, P), :], outa[u][:]).then_inc(outa_out[u], 16)

            tiles(sp, tile)
            for u in range(2):
                sp.wait_ge(outa_out[u], 16 * PT)

        @block.gpsimd
        def _(pool):
            def tile(i, u):
                t = 2 * i + u
                h.root(pool, i + (u + 1) // 2, (u + 1) % 2)
                pool.wait_ge(v_meansq_ready, t + 1)
                wait(pool, v_normed_ready, t)
                nc.gpsimd.tensor_tensor(v_rstd[:], v_meansq[:], h.minus_half[:, 0:GROUPS],
                                        ALU.pow).then_inc(v_rstd_ready, 1)

            tiles(pool, tile)

        @block.scalar
        def _(act):
            act.dma_start(ws_raw[:], w_spatial[0].rearrange("g p q -> p g q")).then_inc(small_in, 16)
            act.dma_start(bs_raw[:], b_spatial[0]).then_inc(small_in, 16)
            act.dma_start(sgu_bc[:], sgu_norm_g.to_broadcast([P, DA])).then_inc(small_in, 16)
            w.round_hi(act, U_A)

            def make_tables():
                for half in range(2):
                    for qr in range(GR):
                        at = PAD + (GR - 1 - qr) * RPC + WC - 1 - half * SC
                        act.dma_start(
                            bias_d[half, qr * HC:(qr + 1) * HC].rearrange("p n r c -> (n r) p c"),
                            bass.AP(rpbpad_d.tensor, at,
                                    [[RPC, H * RPR], [-1, HC], [1, HC + SC]])).then_inc(bias_out, 16)

            def tile(i, u):
                t = 2 * i + u
                n, m = i + (u + 1) // 2, (u + 1) % 2
                h.square(act, n, m)
                act.wait_ge(v_ready, t + 1)
                wait(act, v_normed_ready, t)
                nc.scalar.activation(v_act[:], p_v[:], ACT.Gelu).then_inc(v_gelu, 1)
                act.wait_ge(v_gelu, t + 1)
                wait(act, v_meansq_ready, t)
                for k in range(GROUPS):
                    c = slice(k * CH, (k + 1) * CH)
                    last = nc.scalar.activation(v_squares[:, c], v_act[:, c], ACT.Square,
                                                accum_out=v_sumsq[:, k:k + 1])
                last.then_inc(v_sumsq_ready, 1)
                if isinstance(t, int) and t == 0:
                    w.round_hi(act, G_A)
                act.wait_ge(u_ready, t + 1)
                wait(act, gated_ready, t)
                nc.scalar.activation(u_act[:], p_u[:], ACT.Gelu).then_inc(u_gelu, 1)
                h.modulate(act, n, m, a_col[:, columns(n), :], b_col[:, columns(n), :])
                act.wait_ge(g_ready, t + 1)
                wait(act, silu_ready, t)
                nc.scalar.activation(g_tanh[:], p_g[:], ACT.Tanh, scale=0.5).then_inc(g_tanh_ready, 1)
                if isinstance(t, int) and t == 1:
                    make_tables()
                if isinstance(t, int) and t == TILES - 2:
                    w.round_hi(act, K_B)

            tiles(act, tile)
            act.wait_ge(bias_out, 16 * 2 * GR)

        @block.tensor
        def _(pe):
            def tile(i, u):
                t = 2 * i + u
                pe.wait_ge(h.split_ready, t + 1)
                wait(pe, v_gelu, t)
                if isinstance(t, int) and t == 0:
                    w.ready(pe, V_A)
                h.products(u, p_v[:], w, V_A).then_inc(v_ready, 1)
                wait(pe, u_gelu, t)
                if isinstance(t, int) and t == 0:
                    w.ready(pe, U_A)
                h.products(u, p_u[:], w, U_A).then_inc(u_ready, 1)
                h.transpose(pe, i + (u + 1) // 2, (u + 1) % 2)
                wait(pe, silu_ready, t)
                if isinstance(t, int) and t == 0:
                    pe.wait_ge(small_in, 48)
                    for k in range(GROUPS):
                        nc.tensor.transpose(p_mix[:, k * P:(k + 1) * P], ws_raw[:, k, :], ident[:])
                    nc.tensor.transpose(p_g[:, 0:GROUPS], bs_raw[:], ident[0:GROUPS, 0:GROUPS]).then_inc(ws_t, 1)
                    pe.wait_ge(ws_ready, 1)
                    w.ready(pe, G_A)
                h.products(u, p_g[:], w, G_A).then_inc(h.tile_done, 1)
                pe.wait_ge(v_normed_ready, t + 1)
                wait(pe, gated_ready, t)
                for k in range(GROUPS):
                    last = nc.tensor.matmul(p_mix[:, k * CH:(k + 1) * CH], wsT[:, k, :],
                                            v_normed[:, k * CH:(k + 1) * CH], start=True, stop=True)
                last.then_inc(mix_ready, 1)

            tiles(pe, tile)

        @block.vector
        def _(dve):
            w.take_lo(dve, U_A)

            def tile(i, u):
                t = 2 * i + u
                n, m = i + (u + 1) // 2, (u + 1) % 2
                h.mean(dve, n, m)
                h.normalise(dve, n, m)
                dve.wait_ge(v_sumsq_ready, t + 1)
                wait(dve, v_rstd_ready, t)
                nc.vector.tensor_scalar(v_meansq[:], v_sumsq[:], 1.0 / CH, EPS, ALU.mult,
                                        ALU.add).then_inc(v_meansq_ready, 1)
                dve.wait_ge(v_rstd_ready, t + 1)
                wait(dve, mix_ready, t)
                if isinstance(t, int) and t == 0:
                    dve.wait_ge(small_in, 48)
                for k in range(GROUPS):
                    s = slice(k * CH, (k + 1) * CH)
                    last = nc.vector.scalar_tensor_tensor(out=v_normed[:, s], in0=v_act[:, s],
                                                          scalar=v_rstd[:, k:k + 1], in1=sgu_bc[:, s],
                                                          op0=ALU.mult, op1=ALU.mult)
                last.then_inc(v_normed_ready, 1)
                if isinstance(t, int) and t == 0:
                    w.take_lo(dve, G_A)
                    dve.wait_ge(ws_t, 1)
                    nc.vector.tensor_copy(wsT[:].rearrange("p a b -> p (a b)"), p_mix[:])
                    nc.vector.tensor_copy(bs[:], p_g[:, 0:GROUPS]).then_inc(ws_ready, 1)
                h.split(dve, n, m)
                dve.wait_ge(g_tanh_ready, t + 1)
                wait(dve, outa_ready, t)
                nc.vector.scalar_tensor_tensor(out=g_silu2[:], in0=g_tanh[:], scalar=1.0, in1=p_g[:],
                                               op0=ALU.add, op1=ALU.mult).then_inc(silu_ready, 1)
                dve.wait_ge(mix_ready, t + 1)
                dve.wait_ge(u_gelu, t + 1)
                for k in range(GROUPS):
                    s = slice(k * CH, (k + 1) * CH)
                    last = nc.vector.scalar_tensor_tensor(out=gated[:, s], in0=p_mix[:, s], scalar=bs[:, k:k + 1],
                                                          in1=u_act[:, s], op0=ALU.add, op1=ALU.mult)
                last.then_inc(gated_ready, 1)
                dve.wait_ge(gated_ready, t + 1)
                dve.wait_ge(silu_ready, t + 1)
                wait(dve, outa_out[u], 16 * i)
                nc.vector.scalar_tensor_tensor(out=outa[u][:], in0=g_silu2[:], scalar=0.5, in1=gated[:],
                                               op0=ALU.mult, op1=ALU.mult).then_inc(outa_ready, 1)
                if isinstance(t, int) and t == TILES - 2:
                    w.take_lo(dve, K_B)

            tiles(dve, tile)


def project(nc, ident, a_col, b_col, x2, h, w, v_buffers, q_norm_g, k_norm_g,
            qT_d, kT_d, v_d, kside_d, sg_d, kctx_d, vctx_d):
    with nc.cleanup_on_exit(), ExitStack() as cx:
        sb = lambda n, s, d=F32: cx.enter_context(nc.sbuf_tensor("pro_" + n, s, d))
        ps = lambda n, s: cx.enter_context(nc.psum_tensor("pro_" + n, s, F32))
        sem = lambda n: nc.alloc_semaphore("pro_" + n)
        w.block(V_B, v_buffers)
        w.block(Q_B, w.buffers(cx, "q"))
        w.block(G_B, w.buffers(cx, "g_b"))
        gq = sb("gq", [P, 2])
        gk = sb("gk", [P, 1])
        squares = sb("qk_squares", [P, 2, DA])
        sumsq = sb("qk_sumsq", [P, 2 * H])
        meansq = sb("qk_meansq", [P, 2 * H])
        rstd = sb("qk_rstd", [P, 2 * H])
        qkn = sb("qkn", [P, 2, DA])
        qT = [sb(f"qT{k}", [P, 2, PAIRS * P], F32R) for k in range(2)]
        kT = [sb(f"kT{k}", [P, 2, PAIRS * P], F32R) for k in range(2)]
        kside = [sb(f"kside{k}", [P, 2, PAIRS * GR, SC], F32R) for k in range(2)]
        v_sb, sg = sb("v_sb", [P, DA]), sb("sg", [P, DA])
        p_q, p_k, p_v, p_g = ps("pb_q", [P, DA]), ps("pb_k", [P, DA]), ps("pb_v", [P, DA]), ps("pb_g", [P, DA])
        p_qT, p_kT = ps("p_qT", [P, PAIRS * P]), ps("p_kT", [P, PAIRS * P])

        gains_in = sem("gains_in")
        gq_ready = sem("gq_ready")
        q_ready, k_ready, v_ready = sem("q_ready"), sem("k_ready"), sem("vb_ready")
        q_squared, k_squared = sem("q_squared"), sem("k_squared")
        sums_ready, means_ready, rstds_ready = sem("qk_sums"), sem("qk_means"), sem("qk_rstds")
        q_normed, k_normed = sem("q_normed"), sem("k_normed")
        qT_ready = sem("qT_ready")
        q_rounded, k_rounded, q_split, k_split = (sem("q_rounded"), sem("k_rounded"), sem("qT_split"),
                                                  sem("kT_split"))
        v_copied, g_tanhed, sg_ready = sem("v_copied"), sem("bg_tanhed"), sem("sg_ready")
        q_out, k_out, ks_out = ([sem(f"{n}_out{k}") for k in range(2)] for n in ("q", "k", "ks"))
        v_out, sg_out, ctxk_out = sem("vb_out"), sem("sg_out"), sem("ctxk_out")
        g_ready = sem("bg_ready")
        kT_ready = h.tile_done
        block = cx.enter_context(nc.Block())
        PT = TILES // 2 + 1
        HT = TILES // 2


        def load_x(dma, i, u):
            rows = x2[bass.ds((i - 1) * (GR * GW), GR * GW), :].rearrange("(r h c) d -> h r c d", r=GR, h=2)
            dma.dma_start(h.xt[u][:], rows[u]).then_inc(h.x_in[u], 16)

        def near(u):
            first = HC - SC if u == 0 else 0
            return p_kT[:].rearrange("p (x c) -> p x c", c=HC)[:, :, first:first + SC]

        def pairs(e, tile):
            for i in (0, 1):
                for u in range(2):
                    tile(i, u, True)
            with e.Fori(2, PT - 1) as i:
                for u in range(2):
                    tile(i, u, True)
            for u in range(2):
                tile(PT - 1, u, u == 0)

        def store_heads(dma, dst, src, done):
            for part in range(2):
                heads = dst[part].rearrange("d (n a) t -> n d (a t)", n=2)
                dma.dma_start(heads.bitcast(F32), src[:, part].bitcast(F32)).then_inc(done, 16)

        @block.sync
        def _(sp):
            w.load(sp, V_B)
            w.load(sp, Q_B)

            def tile(i, u, more):
                t = 2 * i + u
                latent = not (isinstance(i, int) and i == 0)
                if not (isinstance(i, int) and i == PT - 1):
                    sp.wait_ge(h.normed_ready, TILES + t + 1)
                    load_x(sp, i + 1, u)
                if isinstance(i, int) and (i, u) == (0, 1):
                    w.load(sp, G_B)
                n = (i - 1) + u * GN
                sp.wait_ge(v_copied, t + 1)
                if latent:
                    sp.dma_start(v_d[bass.ds(n + 1, 1)][0], v_sb[:]).then_inc(v_out, 16)
                    sp.wait_ge(sg_ready, t - 1)
                    sp.dma_start(sg_d[bass.ds(n, 1)][0], sg[:]).then_inc(sg_out, 16)
                    sp.wait_ge(q_split, t - 1)
                    store_heads(sp, qT_d[bass.ds(n, 1)][0].rearrange("d s h t -> s d h t"), qT[u], q_out[u])
                    sp.wait_ge(k_split, t + 1)
                    store_heads(sp, kT_d[bass.ds(n + 1, 1)][0], kT[u], k_out[u])
                    near_d = kside_d[:, :, :, bass.ds(n + 1, 1), :].rearrange("s d h o t -> s d h (o t)")
                    for part in range(2):
                        for odd in range(2):
                            sp.dma_start(
                                near_d[part, :, odd * PAIRS:(odd + 1) * PAIRS].bitcast(F32),
                                kside[u][odd * DH:(odd + 1) * DH, part].bitcast(F32).rearrange(
                                    "p (a r) c -> p a (r c)", a=PAIRS)).then_inc(ks_out[u], 16)
                else:
                    sp.dma_start(vctx_d[u * P:(u + 1) * P, :], v_sb[:]).then_inc(v_out, 16)
                    sp.wait_ge(k_split, t + 1)
                    for part in range(2):
                        for odd in range(2):
                            sp.dma_start(
                                kctx_d[part, :, odd * PAIRS:(odd + 1) * PAIRS, u * P:(u + 1) * P].bitcast(F32),
                                kT[u][odd * DH:(odd + 1) * DH, part].bitcast(F32).rearrange(
                                    "p (a t) -> p a t", t=P)).then_inc(ctxk_out, 16)

            pairs(sp, tile)
            sp.wait_ge(v_out, 16 * (TILES + 2))
            sp.wait_ge(sg_out, 16 * TILES)
            for u in range(2):
                sp.wait_ge(k_out[u], 32 * (PT - 1))
                sp.wait_ge(q_out[u], 32 * (PT - 1))
                sp.wait_ge(ks_out[u], 64 * (PT - 1))

        @block.gpsimd
        def _(pool):
            def tile(i, u, more):
                t = 2 * i + u
                if more:
                    h.root(pool, HT + i + (u + 1) // 2, (u + 1) % 2)
                pool.wait_ge(means_ready, t + 1)
                wait(pool, k_normed, t)
                used = slice(H, 2 * H) if isinstance(i, int) and i == 0 else slice(0, 2 * H)
                nc.gpsimd.tensor_tensor(rstd[:, used], meansq[:, used], h.minus_half[:, used],
                                        ALU.pow).then_inc(rstds_ready, 1)

            pairs(pool, tile)

        @block.scalar
        def _(act):
            for n in range(2):
                half = slice(n * DH, (n + 1) * DH)
                act.dma_start(gq[half, 0:1], q_norm_g.rearrange("b d -> d b")).then_inc(gains_in, 16)
                act.dma_start(gk[half, :], k_norm_g.rearrange("b d -> d b")).then_inc(gains_in, 16)
            act.wait_ge(gq_ready, 1)

            def tile(i, u, more):
                t = 2 * i + u
                latent = not (isinstance(i, int) and i == 0)
                n, m = i + (u + 1) // 2, (u + 1) % 2
                if more:
                    h.square(act, HT + n, m)
                if isinstance(t, int) and t == 0:
                    w.round_hi(act, V_B)
                if latent:
                    act.wait_ge(q_ready, t - 1)
                    wait(act, sums_ready, t)
                    nc.scalar.activation(squares[:, 0, :], p_q[:], ACT.Square).then_inc(q_squared, 1)
                act.wait_ge(k_ready, t + 1)
                wait(act, sums_ready, t)
                nc.scalar.activation(squares[:, 1, :], p_k[:], ACT.Square).then_inc(k_squared, 1)
                if more:
                    s = 1 if isinstance(n, int) and n == 0 else 0
                    h.modulate(act, HT + n, m, a_col[:, s, :], b_col[:, s, :])
                act.wait_ge(v_ready, t + 1)
                wait(act, v_out, 16 * t)
                nc.scalar.activation(v_sb[:], p_v[:], ACT.Copy).then_inc(v_copied, 1)
                if latent:
                    act.wait_ge(g_ready, t - 1)
                    wait(act, sg_out, 16 * (t - 2))
                    nc.scalar.activation(sg[:], p_g[:], ACT.Tanh, scale=0.5).then_inc(g_tanhed, 1)
                    act.wait_ge(qT_ready, t - 1)
                    wait(act, q_out[u], 32 * (i - 1))
                    nc.scalar.activation(qT[u][:, 0], p_qT[:], ACT.Identity, scale=gq[:, 1:2]).then_inc(q_rounded, 1)
                act.wait_ge(kT_ready, TILES + t + 1)
                if latent:
                    wait(act, k_out[u], 32 * (i - 1))
                    if isinstance(i, int) and i == 1:
                        act.wait_ge(ctxk_out, 64 * 2)
                last = nc.scalar.activation(kT[u][:, 0], p_kT[:], ACT.Identity, scale=gk[:, 0:1])
                if latent:
                    wait(act, ks_out[u], 64 * (i - 1))
                    last = nc.scalar.activation(kside[u][:, 0], near(u), ACT.Identity, scale=gk[:, 0:1])
                last.then_inc(k_rounded, 1)
                if not latent:
                    w.round_hi(act, (Q_B, G_B)[u])

            pairs(act, tile)

        @block.tensor
        def _(pe):

            def tile(i, u, more):
                t = 2 * i + u
                latent = not (isinstance(i, int) and i == 0)
                first = isinstance(t, int) and t in (0, 2)
                pe.wait_ge(h.split_ready, TILES + t + 1)
                if latent:
                    if first:
                        w.ready(pe, Q_B)
                    wait(pe, q_normed, t - 2)
                    h.products(u, p_q[:], w, Q_B).then_inc(q_ready, 1)
                wait(pe, k_normed, t)
                if first and not latent:
                    w.ready(pe, K_B)
                h.products(u, p_k[:], w, K_B).then_inc(k_ready, 1)
                if more:
                    h.transpose(pe, HT + i + (u + 1) // 2, (u + 1) % 2)
                wait(pe, v_copied, t)
                if latent:
                    h.products(u, p_v[:], w, V_B).then_inc(v_ready, 1)
                    wait(pe, sg_ready, t - 2)
                    if first:
                        w.ready(pe, G_B)
                    h.products(u, p_g[:], w, G_B).then_inc(g_ready, 1)
                else:
                    if first:
                        w.ready(pe, V_B)
                    h.products(u, p_v[:], w, V_B).then_inc(v_ready, 1)
                if latent:
                    pe.wait_ge(q_normed, t - 1)
                    wait(pe, q_split, t - 2)
                    for a in range(PAIRS):
                        last = nc.tensor.transpose(p_qT[:, a * P:(a + 1) * P], qkn[:, 0, a * P:(a + 1) * P], ident[:])
                    last.then_inc(qT_ready, 1)
                pe.wait_ge(k_normed, t + 1)
                wait(pe, k_split, t)
                for a in range(PAIRS):
                    last = nc.tensor.transpose(p_kT[:, a * P:(a + 1) * P], qkn[:, 1, a * P:(a + 1) * P], ident[:])
                last.then_inc(kT_ready, 1)

            pairs(pe, tile)

        @block.vector
        def _(dve):
            dve.wait_ge(gains_in, 64)
            nc.vector.tensor_scalar(gq[:, 1:2], gq[:, 0:1], -DH ** -0.5, None, ALU.mult).then_inc(gq_ready, 1)

            def tile(i, u, more):
                t = 2 * i + u
                latent = not (isinstance(i, int) and i == 0)
                n, m = i + (u + 1) // 2, (u + 1) % 2
                if more:
                    h.mean(dve, HT + n, m)
                    h.normalise(dve, HT + n, m)
                if isinstance(t, int) and t == 0:
                    w.take_lo(dve, V_B)
                wait(dve, means_ready, t)
                if latent:
                    dve.wait_ge(q_squared, t - 1)
                    nc.vector.tensor_reduce(sumsq[:, 0:H], squares[:, 0, :].rearrange("p (h d) -> p h d", h=H),
                                            AX.X, ALU.add)
                dve.wait_ge(k_squared, t + 1)
                nc.vector.tensor_reduce(sumsq[:, H:2 * H], squares[:, 1, :].rearrange("p (h d) -> p h d", h=H),
                                        AX.X, ALU.add).then_inc(sums_ready, 1)
                dve.wait_ge(sums_ready, t + 1)
                wait(dve, rstds_ready, t)
                used = slice(0, 2 * H) if latent else slice(H, 2 * H)
                nc.vector.tensor_scalar(meansq[:, used], sumsq[:, used], 1.0 / DH, EPS, ALU.mult,
                                        ALU.add).then_inc(means_ready, 1)
                if more:
                    h.split(dve, HT + n, m)
                dve.wait_ge(rstds_ready, t + 1)
                if latent:
                    wait(dve, qT_ready, t - 2)
                    nc.vector.tensor_tensor(qkn[:, 0, :].rearrange("p (h d) -> p h d", h=H),
                                            p_q[:].rearrange("p (h d) -> p h d", h=H),
                                            rstd[:, 0:H].unsqueeze(2).to_broadcast([P, H, DH]),
                                            ALU.mult).then_inc(q_normed, 1)
                dve.wait_ge(kT_ready, TILES + t)
                nc.vector.tensor_tensor(qkn[:, 1, :].rearrange("p (h d) -> p h d", h=H),
                                        p_k[:].rearrange("p (h d) -> p h d", h=H),
                                        rstd[:, H:2 * H].unsqueeze(2).to_broadcast([P, H, DH]),
                                        ALU.mult).then_inc(k_normed, 1)
                if latent:
                    dve.wait_ge(g_tanhed, t - 1)
                    nc.vector.scalar_tensor_tensor(out=sg[:], in0=sg[:], scalar=1.0, in1=p_g[:],
                                                   op0=ALU.add, op1=ALU.mult).then_inc(sg_ready, 1)
                    dve.wait_ge(q_rounded, t - 1)
                    nc.vector.scalar_tensor_tensor(out=qT[u][:, 1], in0=p_qT[:], scalar=gq[:, 1:2],
                                                   in1=qT[u][:, 0].bitcast(F32), op0=ALU.mult,
                                                   op1=ALU.subtract).then_inc(q_split, 1)
                dve.wait_ge(k_rounded, t + 1)
                last = nc.vector.scalar_tensor_tensor(out=kT[u][:, 1], in0=p_kT[:], scalar=gk[:, 0:1],
                                                      in1=kT[u][:, 0].bitcast(F32), op0=ALU.mult, op1=ALU.subtract)
                if latent:
                    last = nc.vector.scalar_tensor_tensor(out=kside[u][:, 1], in0=near(u), scalar=gk[:, 0:1],
                                                          in1=kside[u][:, 0].bitcast(F32), op0=ALU.mult,
                                                          op1=ALU.subtract)
                last.then_inc(k_split, 1)
                if not latent:
                    w.take_lo(dve, (Q_B, G_B)[u])

            pairs(dve, tile)


def attend(nc, ident, qT_d, kT_d, v_d, kside_d, sg_d, kctx_d, vctx_d, bias_d, mask_d, outb_d):
    STEPS, TURNS = TILES, TILES // RING
    T_LAG, PV_LAG, O_LAG = 2, 5, 7
    with nc.cleanup_on_exit(), ExitStack() as cx:
        sb = lambda n, s, d=F32: cx.enter_context(nc.sbuf_tensor("att_" + n, s, d))
        ps = lambda n, s: cx.enter_context(nc.psum_tensor("att_" + n, s, F32))
        sem = lambda n: nc.alloc_semaphore("att_" + n)
        q = [sb(f"q{k}", [P, 2, H, P], F32R) for k in range(2)]
        k_ring = sb("k_ring", [P, H, MIRROR * P], F32R)
        k_side = [sb(f"k_side{k}", [P, H, SIDECTX], F32R) for k in range(2)]
        v_ring = sb("v_ring", [P, RING, DA])
        v_side = [sb(f"v_side{k}", [P, DA]) for k in range(2)]
        v_ctx = sb("v_ctx", [P, 2, DA])
        sg = [sb(f"sgl{k}", [P, DA]) for k in range(2)]
        raw_bias = sb("raw_bias", [P, 2, H, 3 * GR, HC + SC])
        mask = sb("mask", [P, 2, 3, LAT])
        bias = sb("bias", [P, H, KEYS])
        scores = [sb(f"scores{k}", [P, KEYS]) for k in range(2)]
        probs = [sb(f"probs{k}", [P, KCH * P]) for k in range(2)]
        least = sb("least", [P, 2])
        den, rden = sb("den", [P, 2, H]), sb("rden", [P, H])
        pT = sb("pT", [P, 4, KCH * P])
        oT = [sb(f"oT{k}", [P, P]) for k in range(2)]
        o_div = sb("o_div", [P, DA])
        outb = [sb(f"outb{k}", [P, DA]) for k in range(2)]
        p_scores = [ps(f"p_scores{k}", [P, 1024])[:, 512 - MAIN:512 + SIDECTX] for k in range(2)]
        p_pT4, p_pT2 = ps("p_pT4", [P, 4 * P]), ps("p_pT2", [P, 4 * P])
        p_oT, p_o = ps("p_oT", [P, PAIRS * P]), ps("p_o", [P, DA])

        q_in, vs_in, sg_in = ([sem(f"{n}_in{k}") for k in range(2)] for n in ("q", "vs", "sgl"))
        side_in = [sem(f"side_in{k}") for k in range(2)]
        k_in = [sem(f"k_in{k}") for k in range(RING)]
        k_mirrored = sem("k_mirrored")
        v_in = [sem(f"v_in{k}") for k in range(RING)]
        kctx_in, vctx_in, tables_in = [sem(f"kctx_in{k}") for k in range(2)], sem("vctx_in"), [
            [sem(f"tables_in{half}{k}") for k in range(4)] for half in range(2)]
        consts = sem("attend_consts")
        bias_ready = [sem(f"bias_ready{k}") for k in range(H)]
        bias_made = sem("bias_made")
        add_begun, mirror_begun, load_begun = sem("add_begun"), sem("mirror_begun"), sem("load_begun")
        scored, added, exped = sem("scored"), sem("added"), sem("exped")
        pT_ready, pT4_copied, pT2_copied = sem("pT_ready"), sem("pT4_copied"), sem("pT2_copied")
        oT_ready, oT_copied, o_ready = sem("oT_ready"), sem("oT_copied"), sem("o_ready")
        recip_ready, divided, outb_ready = sem("recip_ready"), sem("divided"), sem("outb_ready")
        outb_out = [sem(f"outb_out{k}") for k in range(2)]
        block = cx.enter_context(nc.Block())

        def back(i, u, n, lag):
            at = H * u + n - lag
            if at < 0:
                i, at = i - 1, at + H * RING
            return None if isinstance(i, int) and i < 0 else (i, at // H, at % H)

        def run(e, slot, apart=(0,)):
            def turn(i):
                for u in range(RING):
                    for n in range(H):
                        slot(i, u, n, True)

            for k, first in enumerate(apart):
                turn(first)
                end = apart[k + 1] if k + 1 < len(apart) else TURNS
                if end > first + 1:
                    with e.Fori(first + 1, end) as i:
                        turn(i)
            for n in range(O_LAG + 1):
                slot(TURNS, 0, n, False)

        def masked_bias(e, s, n):
            half, edge = s // GN, {0: 0, 1: 1, GN - 1: 2}[s % GN]
            for at, width, first in ((0, HC, half * SC), (MAIN, SC, 0 if half else HC)):
                part = slice(at, at + 3 * GR * width)
                last = e.tensor_tensor(bias[:, n, part].rearrange("p (r c) -> p r c", c=width),
                                       raw_bias[:, half, n, :, first:first + width],
                                       mask[:, half, edge, part].rearrange("p (r c) -> p r c", c=width), ALU.add)
            return last

        @block.sync
        def _(sp):
            def store(s, b):
                sp.dma_start(outb_d[bass.ds(s, 1)][0], outb[b][:]).then_inc(outb_out[b], 16)

            def load_v(i, u, half):
                s, b = RING * i + u, u % 2
                wait(sp, oT_ready, PAIRS * (s - 1))
                sp.dma_start(v_ring[:, (u + 1) % RING, :],
                             v_d[bass.ds(s + 2, 1)][0]).then_inc(v_in[(u + 1) % RING], 16)
                n = s + GN if half == 0 else s - GN
                first = 0 if half == 0 else HC - SC
                rows = v_d.rearrange("n (r c) d -> (n r) c d", r=GR)[bass.ds(n * GR, 3 * GR), first:first + SC, :]
                sp.dma_start(v_side[b][0:SIDE, :], rows).then_inc(vs_in[b], 16)
                wait(sp, outb_ready, s - 1)
                if not (isinstance(s, int) and s < 2):
                    store(s - 2, b)
                sp.dma_start(sg[b][:], sg_d[bass.ds(s, 1)][0]).then_inc(sg_in[b], 16)

            def load_tables(half, quarter):
                if quarter == 0:
                    sp.dma_start(mask[:, half], mask_d[:, half]).then_inc(tables_in[half][0], 16)
                heads = slice(2 * quarter, 2 * quarter + 2)
                sp.dma_start(raw_bias[:, half, heads].rearrange("p n r c -> p n (r c)"),
                             bias_d[half, :, heads, 0:3 * GR, :].rearrange("p n r c -> p n (r c)")
                             ).then_inc(tables_in[half][quarter], 16)

            load_tables(0, 0)
            sp.wait_ge(q_in[0], 16)
            for quarter in range(1, 4):
                load_tables(0, quarter)
            sp.wait_ge(k_mirrored, 1)
            for b in range(2):
                sp.dma_start(v_side[b][SIDE:P, :], vctx_d[0:P - SIDE, :]).then_inc(vctx_in, 16)
            sp.dma_start(v_ctx[:, 0, :], vctx_d[P - SIDE:2 * P - SIDE, :]).then_inc(vctx_in, 16)
            sp.wait_ge(consts, 6)
            sp.dma_start(v_ctx[0:SIDE, 1, :], vctx_d[2 * P - SIDE:CTX, :]).then_inc(vctx_in, 16)
            sp.dma_start(v_ring[:, 0, :], v_d[1]).then_inc(v_in[0], 16)
            HT = TURNS // 2
            for half in range(2):
                def turn(i, first, half=half):
                    for u in range(RING):
                        load_v(i, u, half)
                        if first and half == 0 and u >= 2:
                            load_tables(1, 2 * u - 4)
                            load_tables(1, 2 * u - 3)

                turn(half * HT, True)
                with sp.Fori(half * HT + 1, (half + 1) * HT) as i:
                    turn(i, False)
            for b in range(2):
                sp.wait_ge(outb_ready, STEPS - 1 + b)
                store(STEPS - 2 + b, b)
            for b in range(2):
                sp.wait_ge(outb_out[b], 16 * STEPS // 2)

        @block.gpsimd
        def _(pool):
            def load_k(seq, i, slot):
                wait(pool, scored, H * (seq - 2))
                if slot < MIRROR - RING:
                    wait(pool, k_mirrored, 2 * (i - 1) + slot + 1)
                pool.sem_inc(load_begun, 1)
                pool.dma_start(k_ring[:, :, slot * P:(slot + 1) * P],
                             kT_d[bass.ds(seq + 1, 1)][0].rearrange("s d h t -> (s d) h t")).then_inc(k_in[slot], 16)

            def load_context(b):
                pool.dma_start(k_side[b][:, :, SIDE:SIDECTX],
                               kctx_d.rearrange("s d h t -> (s d) h t")).then_inc(kctx_in[b], 16)

            def load_q(i, u, half):
                s, b = RING * i + u, u % 2
                wait(pool, scored, H * (s - 1))
                pool.sem_inc(load_begun, 1)
                once = qT_d[bass.ds(s, 1)].rearrange("o d s h t -> o d (s h t)")
                pool.dma_start(q[b][:].rearrange("p s h t -> p (s h t)"),
                               once.to_broadcast([2, DH, 2 * H * P])).then_inc(q_in[b], 16)
                load_k(s + 1, i + (u + 1) // RING, (u + 1) % RING)
                n = s + GN if half == 0 else s - GN
                pool.dma_start(k_side[b][:, :, 0:SIDE],
                             kside_d[:, :, :, bass.ds(n, 3), :].rearrange("s d h g t -> (s d) h (g t)")
                             ).then_inc(side_in[b], 16)

            def mirror(i, slot):
                pool.wait_ge(k_in[slot], 16 * (i + 1))
                pool.sem_inc(mirror_begun, 1)
                nc.gpsimd.tensor_copy(k_ring[:, :, (RING + slot) * P:(RING + slot + 1) * P],
                                      k_ring[:, :, slot * P:(slot + 1) * P]).then_inc(k_mirrored, 1)

            def gate(i, u):
                if isinstance(i, int) and i == 0 and u < 2:
                    return
                s, b, before = RING * i + u - 2, u % 2, 2 * i + u // 2 - 1
                pool.wait_ge(sg_in[b], 16 * (before + 1))
                wait(pool, outb_out[b], 16 * before)
                pool.wait_ge(divided, s + 1)
                nc.gpsimd.tensor_tensor(outb[b][:], sg[b][:], o_div[:], ALU.mult).then_inc(outb_ready, 1)

            made = [0]

            def make_bias(s, until):
                for n in range(H):
                    pool.wait_ge(added, H * (s - 1) + n + 1)
                    masked_bias(nc.gpsimd, s, n).then_inc(bias_made, 1)
                    made[0] += 1
                    pool.wait_ge(bias_made, made[0])
                    pool.sem_inc(bias_ready[n], until - s)

            load_k(0, 0, 0)
            load_q(0, 0, 0)
            load_context(0)
            nc.gpsimd.memset(k_ring[:, :, (RING - 1) * P:RING * P].bitcast(F32), 0.0).then_inc(consts, 1)
            nc.gpsimd.memset(v_ctx[:, 1, :], 0.0).then_inc(consts, 1)
            nc.gpsimd.memset(v_ring[:, RING - 1, :], 0.0).then_inc(consts, 1)
            nc.gpsimd.memset(bias[:, :, LAT:KEYS], 0.0).then_inc(consts, 1)
            for b in range(2):
                nc.gpsimd.memset(probs[b][:, KEYS:KCH * P], 0.0).then_inc(consts, 1)
            HT = TURNS // 2
            for half in range(2):
                base, first = half * GN, half * HT
                for u in range(RING):
                    if half or u:
                        load_q(first, u, half)
                    if u == RING - 1:
                        mirror(first + 1, 0)
                    if half == 0 and u == 0:
                        mirror(0, 0)
                    if u == 0:
                        mirror(first, 1)
                    if half == 0 and u == 1:
                        load_context(1)
                    if u == 1:
                        make_bias(base + 1, base + GN - 1)
                    gate(first, u)
                with pool.Fori(first + 1, first + HT - 1) as i:
                    for u in range(RING):
                        load_q(i, u, half)
                        if u == 0:
                            mirror(i, 1)
                        if u == RING - 1:
                            mirror(i + 1, 0)
                        gate(i, u)
                i = first + HT - 1
                for u in range(RING):
                    load_q(i, u, half)
                    if u == 0:
                        mirror(i, 1)
                    if u == RING - 1:
                        mirror(i + 1, 0)
                    gate(i, u)
            for u in range(2):
                gate(TURNS, u)

        @block.tensor
        def _(pe):
            pe.wait_ge(consts, 6)

            def score(i, u, n):
                s, b = RING * i + u, u % 2
                t = H * s + n
                if n == 0:
                    pe.wait_ge(q_in[b], 16 * (2 * i + u // 2 + 1))
                    pe.wait_ge(side_in[b], 16 * (2 * i + u // 2 + 1))
                    if isinstance(i, int) and i == 0 and u < 2:
                        pe.wait_ge(kctx_in[b], 16)
                    new = (u + 1) % RING
                    if new < MIRROR - RING:
                        pe.wait_ge(k_mirrored, 2 * (i + (u + 1) // RING) + new + 1)
                    else:
                        pe.wait_ge(k_in[new], 16 * (i + 1))
                wait(pe, added, t - 1)
                first = ((u + RING - 1) % RING) * P
                main = k_ring[:, place(n), first:first + MAIN]
                side = k_side[b][:, place(n), :]
                m = n % 2
                nc.tensor.matmul(p_scores[m][:, 0:MAIN], q[b][:, 0, place(n), :], main, start=True, stop=False)
                nc.tensor.matmul(p_scores[m][:, 0:MAIN], q[b][:, 1, place(n), :], main, start=False, stop=True)
                nc.tensor.matmul(p_scores[m][:, MAIN:KEYS], q[b][:, 0, place(n), :], side, start=True, stop=False)
                nc.tensor.matmul(p_scores[m][:, MAIN:KEYS], q[b][:, 1, place(n), :], side, start=False,
                                 stop=True).then_inc(scored, 1)

            def transpose(i, u, n):
                t = H * (RING * i + u) + n
                pe.wait_ge(exped, t + 1)
                wait(pe, pT4_copied, t)
                wait(pe, pT2_copied, t)
                for j in range(KCH):
                    bank, at = (p_pT4, j) if j < 4 else (p_pT2, j - 4)
                    last = nc.tensor.transpose(bank[:, at * P:(at + 1) * P], probs[n % 2][:, j * P:(j + 1) * P],
                                               ident[:])
                last.then_inc(pT_ready, 1)

            def values(i, u, a, second):
                s, b = RING * i + u, u % 2
                t = H * s + 2 * a
                if a == 0 and not second:
                    pe.wait_ge(v_in[(u + 1) % RING], 16 * (i + (u + 1) // RING + 1))
                    pe.wait_ge(vs_in[b], 16 * (2 * i + u // 2 + 1))
                    if isinstance(i, int) and i == 0 and u == 0:
                        pe.wait_ge(v_in[0], 16)
                        pe.wait_ge(vctx_in, 64)
                if not second:
                    pe.wait_ge(pT4_copied, t + 2)
                    pe.wait_ge(pT2_copied, t + 2)
                    wait(pe, oT_copied, PAIRS * s + a)
                for j in range(KCH // 2, KCH) if second else range(KCH // 2):
                    v = (v_ring[:, (u + RING - 1 + j) % RING, :] if j < 3 else
                         v_side[b][:] if j == 3 else v_ctx[:, j - 4, :])
                    for k in range(2):
                        n = 2 * a + k
                        last = nc.tensor.matmul(p_oT[k * DH:(k + 1) * DH, a * P:(a + 1) * P],
                                                v[:, n * DH:(n + 1) * DH], pT[:, n % 4, j * P:(j + 1) * P],
                                                start=(j == 0), stop=(j == KCH - 1))
                if second:
                    last.then_inc(oT_ready, 1)

            def untranspose(i, u, a):
                s = RING * i + u
                pe.wait_ge(oT_copied, PAIRS * s + a + 1)
                if a == 0:
                    wait(pe, divided, s)
                nc.tensor.transpose(p_o[:, a * P:(a + 1) * P], oT[a % 2][:], ident[:]).then_inc(o_ready, 1)

            def slot(i, u, n, live):
                if live:
                    score(i, u, n)
                t2 = back(i, u, n, T_LAG)
                if t2 and (live or n < T_LAG):
                    transpose(*t2)
                lag = PV_LAG - 1 + n % 2
                pv = back(i, u, n, lag)
                if pv and (live or n < lag):
                    values(pv[0], pv[1], pv[2] // 2, n % 2)
                o = back(i, u, n, O_LAG)
                if n % 2 and o and (live or n < O_LAG):
                    untranspose(o[0], o[1], o[2] // 2)

            run(pe, slot)

        @block.scalar
        def _(act):
            def copy_pT(i, u, n):
                t = H * (RING * i + u) + n
                act.wait_ge(pT_ready, t + 1)
                wait(act, oT_ready, PAIRS * (RING * i + u) + n // 2 - 1)
                nc.scalar.activation(pT[:, n % 4, 0:4 * P], p_pT4[:], ACT.Copy).then_inc(pT4_copied, 1)

            def softmax(i, u, n):
                s, b = RING * i + u, n % 2
                t = H * s + n
                act.wait_ge(added, t + 1)
                wait(act, pT_ready, t - 1)
                if n == 0:
                    wait(act, divided, s - 1)
                if isinstance(i, int) and i == 0 and u == 0 and n == 0:
                    act.wait_ge(consts, 6)
                nc.scalar.activation(probs[b][:, 0:KEYS], scores[b][:], ACT.Exp, scale=-1.0, bias=least[:, b:b + 1],
                                     accum_out=den[:, u % 2, n:n + 1]).then_inc(exped, 1)

            def copy_oT(i, u, a):
                m = PAIRS * (RING * i + u) + a
                act.wait_ge(oT_ready, m + 1)
                wait(act, o_ready, m - 1)
                nc.scalar.activation(oT[a % 2][:], p_oT[:, a * P:(a + 1) * P], ACT.Copy,
                                     scale=0.5).then_inc(oT_copied, 1)

            def slot(i, u, n, live):
                t2 = back(i, u, n, T_LAG)
                if t2 and (live or n < T_LAG):
                    copy_pT(*t2)
                if live:
                    softmax(i, u, n)
                pv, o = back(i, u, n, PV_LAG), back(i, u, n, O_LAG)
                if n % 2 and pv and (live or n < PV_LAG):
                    copy_oT(pv[0], pv[1], pv[2] // 2)

            run(act, slot)

        @block.vector
        def _(dve):
            def add_bias(i, u, n):
                s, b = RING * i + u, n % 2
                t = H * s + n
                if isinstance(i, int) and t == 0:
                    dve.wait_ge(consts, 6)
                dve.wait_ge(scored, t + 1)
                dve.wait_ge(bias_ready[n], s + 1)
                wait(dve, exped, t - 1)
                dve.sem_inc(add_begun, 1)
                nc.vector.tensor_tensor_reduce(
                    out=scores[b][:], in0=p_scores[b], in1=bias[:, n, :], scale=1.0, scalar=HIGHEST,
                    op0=ALU.add, op1=ALU.min, accum_out=least[:, b:b + 1]).then_inc(added, 1)

            def copy_pT(i, u, n):
                t = H * (RING * i + u) + n
                dve.wait_ge(pT_ready, t + 1)
                wait(dve, oT_ready, PAIRS * (RING * i + u) + n // 2 - 1)
                nc.vector.tensor_copy(pT[:, n % 4, 4 * P:KCH * P], p_pT2[:, 0:2 * P]).then_inc(pT2_copied, 1)

            def divide(i, u):
                s, b = RING * i + u, u % 2
                dve.wait_ge(exped, H * (s + 1))
                wait(dve, divided, s)
                nc.vector.reciprocal(rden[:], den[:, b, :]).then_inc(recip_ready, 1)
                dve.wait_ge(recip_ready, s + 1)
                dve.wait_ge(o_ready, PAIRS * (s + 1))
                wait(dve, outb_ready, s)
                nc.vector.tensor_tensor(o_div[:].rearrange("p (h d) -> p h d", h=H),
                                        p_o[:].rearrange("p (h d) -> p h d", h=H),
                                        rden[:].unsqueeze(2).to_broadcast([P, H, DH]), ALU.mult).then_inc(divided, 1)

            def slot(i, u, n, live):
                s = RING * i + u
                if live and isinstance(s, int) and s in (0, GN - 1, GN, 2 * GN - 1):
                    if n % 2 == 0 and s % GN == 0:
                        dve.wait_ge(tables_in[s // GN][n // 2], 16 if n else 32)
                    wait(dve, added, H * (s - 1) + n + 1 if s else 0)
                    masked_bias(nc.vector, s, n).then_inc(bias_ready[n], 1)
                if live:
                    add_bias(i, u, n)
                t2 = back(i, u, n, T_LAG)
                if t2 and (live or n < T_LAG):
                    copy_pT(*t2)
                if n == O_LAG - 1 and back(i, u, n, H):
                    divide(*back(i, u, n, H)[0:2])

            run(dve, slot, (0, TURNS // 2 - 1, TURNS // 2, TURNS - 1))


def combine(nc, ident, gate_bc, x2, w_out, outa_d, outb_d, out2):
    with nc.cleanup_on_exit(), ExitStack() as cx:
        sb = lambda n, s, d=F32: cx.enter_context(nc.sbuf_tensor("com_" + n, s, d))
        ps = lambda n, s: cx.enter_context(nc.psum_tensor("com_" + n, s, F32))
        sem = lambda n: nc.alloc_semaphore("com_" + n)
        w = SplitWeights(nc, cx, "wo", w_out[0], 6)
        for col in (0, 512):
            w.block(col, w.buffers(cx, f"from{col}"))
        mix = [sb(f"mix{k}", [P, D]) for k in range(2)]
        xt = [sb(f"xr{k}", [P, D]) for k in range(2)]
        hi = [sb(f"mixT_hi{k}", [P, KT, P], F32R) for k in range(2)]
        lo = [sb(f"mixT_lo{k}", [P, KT, P], F32R) for k in range(2)]
        gated = sb("out_gated", [P, D])
        result = [sb(f"result{k}", [P, D]) for k in range(2)]
        p_t = [ps(f"p_mixT{k}", [P, KT, P]) for k in range(2)]
        p_o = [ps(f"p_out{k}", [P, 512]) for k in range(4)]
        mix_in = [sem(f"mix_in{k}") for k in range(2)]
        x_in = [sem(f"xr_in{k}") for k in range(2)]
        transposed, hi_ready, split_ready = sem("mix_transposed"), sem("mix_hi"), sem("mix_split")
        product = sem("product")
        gated_ready, result_ready = sem("out_gated_ready"), sem("result_ready")
        out_out = [sem(f"out_out{k}") for k in range(2)]
        block = cx.enter_context(nc.Block())
        PT = TILES // 2

        @block.sync
        def _(sp):
            def load_mix(i, u):
                sp.dma_start(mix[u][:, 0:DA], outa_d[bass.ds((2 * i + u) * P, P), :]).then_inc(mix_in[u], 16)
                halves = outb_d.rearrange("(h g) p d -> g h p d", h=2)[bass.ds(i, 1)][0]
                for r in range(2):
                    row = (2 * u + r) * HC
                    sp.dma_start(mix[u][r * GW:(r + 1) * GW, DA:D], halves[:, row:row + HC, :]).then_inc(mix_in[u], 16)

            def load_x(i, u):
                sp.dma_start(xt[u][:], x2[bass.ds((2 * i + u) * P, P), :]).then_inc(x_in[u], 16)

            load_mix(0, 0)
            w.load(sp, 0)
            load_mix(0, 1)
            w.load(sp, 512)
            for u in range(2):
                load_x(0, u)

            def tile(i, u, more):
                t = 2 * i + u
                if more:
                    sp.wait_ge(transposed, t + 1)
                    load_mix(i + 1, u)
                sp.wait_ge(result_ready, t + 1)
                sp.dma_start(out2[bass.ds(t * P, P), :], result[u][:]).then_inc(out_out[u], 16)
                if more:
                    load_x(i + 1, u)

            with sp.Fori(0, PT - 1) as i:
                for u in range(2):
                    tile(i, u, True)
            for u in range(2):
                tile(PT - 1, u, False)
            for u in range(2):
                sp.wait_ge(out_out[u], 16 * PT)

        def tiles(e, tile):
            for u in range(2):
                tile(0, u, True)
            with e.Fori(1, PT - 1) as i:
                for u in range(2):
                    tile(i, u, True)
            for u in range(2):
                tile(PT - 1, u, u == 0)

        @block.scalar
        def _(act):
            def round_hi(i, u):
                t = 2 * i + u
                act.wait_ge(transposed, t + 1)
                wait(act, product, 2 * (t - 1))
                nc.scalar.activation(hi[u][:], p_t[u][:], ACT.Copy).then_inc(hi_ready, 1)

            w.round_hi(act, 0)
            round_hi(0, 0)
            w.round_hi(act, 512)

            def tile(i, u, more):
                if more:
                    round_hi(i + (u + 1) // 2, (u + 1) % 2)

            tiles(act, tile)

        @block.tensor
        def _(pe):
            def transpose(i, u):
                t = 2 * i + u
                pe.wait_ge(mix_in[u], 48 * (i + 1))
                wait(pe, split_ready, t - 1)
                for k in range(KT):
                    last = nc.tensor.transpose(p_t[u][:, k, :], mix[u][:, k * P:(k + 1) * P], ident[:])
                last.then_inc(transposed, 1)

            transpose(0, 0)

            def tile(i, u, more):
                t = 2 * i + u
                pe.wait_ge(split_ready, t + 1)
                for n in range(2):
                    bank = p_o[2 * u + n]
                    wait(pe, gated_ready, 2 * (t - 2) + n + 1)
                    if isinstance(t, int) and t == 0:
                        w.ready(pe, n * 512)
                    split_products(nc, bank[:], hi[u], lo[u], w, n * 512).then_inc(product, 1)
                    if n == 0 and more:
                        transpose(i + (u + 1) // 2, (u + 1) % 2)

            tiles(pe, tile)

        @block.vector
        def _(dve):
            def take_lo(i, u):
                t = 2 * i + u
                dve.wait_ge(hi_ready, t + 1)
                nc.vector.tensor_tensor(lo[u][:], p_t[u][:], hi[u][:].bitcast(F32),
                                        ALU.subtract).then_inc(split_ready, 1)

            w.take_lo(dve, 0)
            take_lo(0, 0)
            w.take_lo(dve, 512)

            def tile(i, u, more):
                t = 2 * i + u
                if more:
                    take_lo(i + (u + 1) // 2, (u + 1) % 2)
                wait(dve, result_ready, t)
                for n in range(2):
                    c = slice(n * 512, (n + 1) * 512)
                    dve.wait_ge(product, 2 * t + n + 1)
                    nc.vector.tensor_tensor(gated[:, c], p_o[2 * u + n][:], gate_bc[:, c],
                                            ALU.mult).then_inc(gated_ready, 1)
                dve.wait_ge(gated_ready, 2 * t + 2)
                dve.wait_ge(x_in[u], 16 * (i + 1))
                wait(dve, out_out[u], 16 * i)
                nc.vector.tensor_tensor(result[u][:], gated[:], xt[u][:], ALU.add).then_inc(result_ready, 1)

            tiles(dve, tile)


_INS = ["x", "c", "ctx", "c_ctx", "w_ada", "b_ada", "norm_g", "w_in", "sgu_norm_g", "w_spatial", "b_spatial",
        "q_norm_g", "k_norm_g", "rpb", "w_out"]


def kernel(**inputs):
    import numpy as np
    from concourse import bacc
    from concourse.bass_utils import run_bass_kernel_spmd

    nc = bacc.Bacc("TRN2", target_bir_lowering=False, num_devices=1)
    arrays, args = {}, []
    for name in _INS:
        a = np.ascontiguousarray(inputs[name])
        arrays[f"in_{name}"] = a
        args.append(nc.dram_tensor(f"in_{name}", a.shape, mybir.dt.from_np(a.dtype), kind="ExternalInput").ap())
    args.append(nc.dram_tensor("out_x", inputs["x"].shape, F32, kind="ExternalOutput").ap())
    build(nc, *args)
    r = run_bass_kernel_spmd(nc, [arrays], core_ids=[0])
    return r.results[0]["out_x"]
```
